# Optimizing a Trainium2 kernel written in Bass

```python
import jax, jax.numpy as jnp
from jax import lax
import numpy as np

D_MODEL = 1024
BATCH = 1
SEQ = 512
DEPTH = 2

GRID_W = 64
CTX_LEN = 256
HEAD_DIM = 64
ATT_HEADS = (D_MODEL // 2) // HEAD_DIM
ATT_KV_HEADS = ATT_HEADS // 4
ATT_GROUP = ATT_HEADS // ATT_KV_HEADS
ATT_WIDTH = ATT_HEADS * HEAD_DIM
KV_WIDTH = ATT_KV_HEADS * HEAD_DIM
WINDOW = 128
BLOCK = 128
ROPE_BASE = 10000.0
RWKV_HEADS = (D_MODEL // 2) // HEAD_DIM
RWKV_WIDTH = RWKV_HEADS * HEAD_DIM
DECAY_LORA = 64
ICLR_LORA = 64
GATE_LORA = 128
MLP_HIDDEN = 4 * D_MODEL
N_EVEN = (DEPTH + 1) // 2
N_ODD = DEPTH // 2
NORM_EPS = 1e-6
GN_EPS = 64e-5
ATT_SPLITS = (ATT_WIDTH, KV_WIDTH, KV_WIDTH)
RWKV_SPLITS = (RWKV_WIDTH, RWKV_WIDTH, RWKV_WIDTH, DECAY_LORA, DECAY_LORA, ICLR_LORA, ICLR_LORA, GATE_LORA)
ATT_IN_WIDTH = ATT_WIDTH + 2 * KV_WIDTH
RWKV_IN_WIDTH = 3 * RWKV_WIDTH + 2 * DECAY_LORA + 2 * ICLR_LORA + GATE_LORA
AB_IN_WIDTH = ATT_IN_WIDTH + RWKV_IN_WIDTH
MIX_WIDTH = ATT_WIDTH + RWKV_WIDTH
F32 = jnp.float32

kernel_name = 'hybrid_swa_rwkv7_shortconv_dit'

def _split(u, sizes):
    out, start = [], 0
    for s in sizes:
        out.append(u[..., start:start + s])
        start += s
    return out

def rms_norm(u, g):
    uf = u.astype(F32)
    y = uf * lax.rsqrt(jnp.mean(uf * uf, axis=-1, keepdims=True) + NORM_EPS)
    return (y * g.astype(F32)).astype(u.dtype)

def shift_centred(u):
    prev = jnp.pad(u[:, :-1], ((0, 0), (1, 0), (0, 0)))
    nxt = jnp.pad(u[:, 1:], ((0, 0), (0, 1), (0, 0)))
    return 0.5 * (prev + nxt)

def conv3_centred(u, w):
    prev = jnp.pad(u[:, :-1], ((0, 0), (1, 0), (0, 0)))
    nxt = jnp.pad(u[:, 1:], ((0, 0), (0, 1), (0, 0)))
    return prev * w[0] + u * w[1] + nxt * w[2]

def rope_1d(u, pos):
    m = u.shape[-1] // 2
    inv = ROPE_BASE ** (-jnp.arange(m, dtype=F32) / m)
    ang = pos.astype(F32)[:, None] * inv[None, :]
    cos = jnp.cos(ang)[None, :, None, :]
    sin = jnp.sin(ang)[None, :, None, :]
    uf = u.astype(F32)
    u1, u2 = uf[..., :m], uf[..., m:]
    return jnp.concatenate([u1 * cos - u2 * sin, u2 * cos + u1 * sin], axis=-1).astype(u.dtype)

def rope_2d(u, row, col):
    h = u.shape[-1] // 2
    return jnp.concatenate([rope_1d(u[..., :h], row), rope_1d(u[..., h:], col)], axis=-1)

def window_attention(q, k, v, kc, vc, sink):
    B, S = q.shape[0], q.shape[1]
    L = kc.shape[1]
    nb = S // BLOCK
    n_loc = 3 * BLOCK
    scale = HEAD_DIM ** -0.5
    qb = q.reshape(B, nb, BLOCK, ATT_KV_HEADS, ATT_GROUP, HEAD_DIM).transpose(1, 0, 2, 3, 4, 5)
    pad = ((0, 0), (BLOCK, BLOCK), (0, 0), (0, 0))
    kp, vp = jnp.pad(k, pad), jnp.pad(v, pad)
    sink_l = sink.astype(F32).reshape(1, ATT_KV_HEADS, ATT_GROUP, 1, 1)
    rel = jnp.arange(BLOCK)[:, None] + BLOCK - jnp.arange(n_loc)[None, :]
    band = jnp.abs(rel) <= WINDOW

    def one_block(args):
        bi, qblk = args
        start = bi * BLOCK
        kb = lax.dynamic_slice_in_dim(kp, start, n_loc, axis=1)
        vb = lax.dynamic_slice_in_dim(vp, start, n_loc, axis=1)
        kpos = start - BLOCK + jnp.arange(n_loc)
        valid = band & ((kpos >= 0) & (kpos < S))[None, :]
        s_loc = jnp.einsum('bqhgd,bkhd->bhgqk', qblk, kb).astype(F32) * scale
        s_loc = jnp.where(valid, s_loc, -jnp.inf)
        s_ctx = jnp.einsum('bqhgd,bkhd->bhgqk', qblk, kc).astype(F32) * scale
        s_sink = jnp.broadcast_to(sink_l, s_loc.shape[:-1] + (1,))
        p = jax.nn.softmax(jnp.concatenate([s_loc, s_ctx, s_sink], axis=-1), axis=-1).astype(v.dtype)
        return (jnp.einsum('bhgqk,bkhd->bqhgd', p[..., :n_loc], vb)
                + jnp.einsum('bhgqk,bkhd->bqhgd', p[..., n_loc:n_loc + L], vc))

    out = lax.map(one_block, (jnp.arange(nb), qb))
    return out.transpose(1, 0, 2, 3, 4, 5).reshape(B, S, ATT_WIDTH)

def context_attention(qc, kc, vc, sink):
    B, L = qc.shape[0], qc.shape[1]
    qg = qc.reshape(B, L, ATT_KV_HEADS, ATT_GROUP, HEAD_DIM)
    s = jnp.einsum('bqhgd,bkhd->bhgqk', qg, kc).astype(F32) * HEAD_DIM ** -0.5
    s_sink = jnp.broadcast_to(sink.astype(F32).reshape(1, ATT_KV_HEADS, ATT_GROUP, 1, 1), s.shape[:-1] + (1,))
    p = jax.nn.softmax(jnp.concatenate([s, s_sink], axis=-1), axis=-1).astype(vc.dtype)
    return jnp.einsum('bhgqk,bkhd->bqhgd', p[..., :L], vc).reshape(B, L, ATT_WIDTH)

def _heads(u):
    return u.reshape(u.shape[:-1] + (RWKV_HEADS, HEAD_DIM))

def rwkv_features(pr, lp):
    pr = pr.astype(F32)
    pr = pr + lp['mu'] * (shift_centred(pr) - pr)
    r, k, v, wf, wb, af, ab, g = _split(pr, RWKV_SPLITS)
    kk = _heads(k * lp['kk'])
    kk = kk / jnp.maximum(jnp.sqrt(jnp.sum(kk * kk, axis=-1, keepdims=True)), 1e-12)
    decays, ks, iclrs = [], [], []
    for d, (wd, ad) in enumerate(((wf, af), (wb, ab))):
        w_log = -jax.nn.softplus(-(lp['w0'][d] + jnp.tanh(wd) @ lp['w2'][d])) - 0.5
        a = jax.nn.sigmoid(lp['a0'][d] + ad @ lp['a2'][d])
        decays.append(_heads(jnp.exp(-jnp.exp(w_log))))
        ks.append(_heads(k * (1.0 + (a - 1.0) * lp['ka'])))
        iclrs.append(_heads(a))
    gate = jax.nn.sigmoid(g) @ lp['g2']
    return dict(r=_heads(r), v=_heads(v), kk=kk, gate=gate, decay=decays, k=ks, a=iclrs)

def rwkv_scan(state0, f, d, emit, reverse):
    xs = tuple(jnp.moveaxis(t, 1, 0) for t in (f['decay'][d], f['k'][d], f['v'], -f['kk'], f['kk'] * f['a'][d]))

    def update(S, w_t, k_t, v_t, a_t, b_t):
        sa = jnp.einsum('bhvk,bhk->bhv', S, a_t)
        return S * w_t[:, :, None, :] + sa[..., None] * b_t[:, :, None, :] + v_t[..., None] * k_t[:, :, None, :]

    if not emit:
        s_fin, _ = lax.scan(lambda S, inp: (update(S, *inp), None), state0, xs, reverse=reverse)
        return s_fin, None

    def step(S, inp):
        S = update(S, *inp[1:])
        return S, jnp.einsum('bhvk,bhk->bhv', S, inp[0])

    s_fin, ys = lax.scan(step, state0, (jnp.moveaxis(f['r'], 1, 0),) + xs, reverse=reverse)
    return s_fin, jnp.moveaxis(ys, 0, 1)

def rwkv_output(y, f, lp):
    mean = jnp.mean(y, axis=-1, keepdims=True)
    var = jnp.mean(jnp.square(y - mean), axis=-1, keepdims=True)
    yn = ((y - mean) * lax.rsqrt(var + GN_EPS)).reshape(y.shape[:2] + (RWKV_WIDTH,))
    yn = yn * lp['ln_w'] + lp['ln_b']
    bonus = sum(jnp.sum(f['r'] * kd * lp['rk'], axis=-1, keepdims=True) * f['v'] for kd in f['k'])
    return (yn + bonus.reshape(yn.shape)) * f['gate']

def ab_mixer(hl, hc, row, col, lp, need_ctx_out):
    B, S = hl.shape[0], hl.shape[1]
    L = hc.shape[1]
    pl = hl @ lp['w_in']
    pc = hc @ lp['w_in']
    ql, kl, vl = _split(pl[..., :ATT_IN_WIDTH], ATT_SPLITS)
    qc, kc, vc = _split(pc[..., :ATT_IN_WIDTH], ATT_SPLITS)
    ql = rope_2d(ql.reshape(B, S, ATT_HEADS, HEAD_DIM), row, col)
    kl = rope_2d(kl.reshape(B, S, ATT_KV_HEADS, HEAD_DIM), row, col)
    vl = vl.reshape(B, S, ATT_KV_HEADS, HEAD_DIM)
    kc = kc.reshape(B, L, ATT_KV_HEADS, HEAD_DIM)
    vc = vc.reshape(B, L, ATT_KV_HEADS, HEAD_DIM)
    att_l = window_attention(ql, kl, vl, kc, vc, lp['sink'])

    fl = rwkv_features(pl[..., ATT_IN_WIDTH:], lp)
    fc = rwkv_features(pc[..., ATT_IN_WIDTH:], lp)
    state0 = jnp.zeros((B, RWKV_HEADS, HEAD_DIM, HEAD_DIM), F32)
    ys_l, ys_c = [], []
    for d in range(2):
        rev = d == 1
        s_ctx, yc_d = rwkv_scan(state0, fc, d, need_ctx_out, rev)
        _, yl_d = rwkv_scan(s_ctx, fl, d, True, rev)
        ys_l.append(yl_d)
        ys_c.append(yc_d)
    rw_l = rwkv_output(ys_l[0] + ys_l[1], fl, lp)
    out_l = jnp.concatenate([att_l, rw_l.astype(att_l.dtype)], axis=-1) @ lp['w_out']
    if not need_ctx_out:
        return out_l, None
    att_c = context_attention(qc.reshape(B, L, ATT_HEADS, HEAD_DIM), kc, vc, lp['sink'])
    rw_c = rwkv_output(ys_c[0] + ys_c[1], fc, lp)
    out_c = jnp.concatenate([att_c, rw_c.astype(att_c.dtype)], axis=-1) @ lp['w_out']
    return out_l, out_c

def conv_mixer(h, w_in, conv_w, w_out):
    gate_b, gate_c, u = jnp.split(h @ w_in, 3, axis=-1)
    return (gate_b * conv3_centred(gate_c * u, conv_w)) @ w_out

def sq_relu_mlp(h, w1, w2):
    return jnp.square(jax.nn.relu(h @ w1)) @ w2

def setup_inputs(seed: int = 0) -> dict:
    key = jax.random.key(seed)
    ks = jax.random.split(key, 26)
    D = D_MODEL

    def nrm(k, shape, s):
        return jax.random.normal(k, shape, F32) * s

    return {
        'x': nrm(ks[0], (BATCH, SEQ, D), 1.0),
        'c': nrm(ks[1], (BATCH, D), 1.0),
        'ctx': nrm(ks[2], (BATCH, CTX_LEN, D), 1.0),
        'c_ctx': nrm(ks[3], (D,), 1.0),
        'mod_w': nrm(ks[4], (DEPTH, D, 6 * D), 0.5 * D ** -0.5),
        'mod_b': nrm(ks[5], (DEPTH, 6 * D), 0.02),
        'norm_g': 1.0 + nrm(ks[6], (DEPTH, 4, D), 0.02),
        'mlp_w1': nrm(ks[7], (DEPTH, D, MLP_HIDDEN), D ** -0.5),
        'mlp_w2': nrm(ks[8], (DEPTH, MLP_HIDDEN, D), MLP_HIDDEN ** -0.5),
        'ab_w_in': nrm(ks[9], (N_EVEN, D, AB_IN_WIDTH), D ** -0.5),
        'ab_w_out': nrm(ks[10], (N_EVEN, MIX_WIDTH, D), MIX_WIDTH ** -0.5),
        'att_sink': nrm(ks[11], (N_EVEN, ATT_HEADS), 0.5),
        'rwkv_mu': jax.random.uniform(ks[12], (N_EVEN, RWKV_IN_WIDTH), F32, 0.0, 1.0),
        'rwkv_w0': nrm(ks[13], (N_EVEN, 2, RWKV_WIDTH), 0.5),
        'rwkv_w2': nrm(ks[14], (N_EVEN, 2, DECAY_LORA, RWKV_WIDTH), 0.5 * DECAY_LORA ** -0.5),
        'rwkv_a0': nrm(ks[15], (N_EVEN, 2, RWKV_WIDTH), 0.5),
        'rwkv_a2': nrm(ks[16], (N_EVEN, 2, ICLR_LORA, RWKV_WIDTH), 0.5 * ICLR_LORA ** -0.5),
        'rwkv_g2': nrm(ks[17], (N_EVEN, GATE_LORA, RWKV_WIDTH), GATE_LORA ** -0.5),
        'rwkv_kk': 0.85 + nrm(ks[18], (N_EVEN, RWKV_WIDTH), 0.05),
        'rwkv_ka': 1.0 + nrm(ks[19], (N_EVEN, RWKV_WIDTH), 0.05),
        'rwkv_rk': nrm(ks[20], (N_EVEN, RWKV_HEADS, HEAD_DIM), 0.1),
        'rwkv_ln_w': 1.0 + nrm(ks[21], (N_EVEN, RWKV_WIDTH), 0.02),
        'rwkv_ln_b': nrm(ks[22], (N_EVEN, RWKV_WIDTH), 0.02),
        'conv_w_in': nrm(ks[23], (N_ODD, D, 3 * D), D ** -0.5),
        'conv_w': nrm(ks[24], (N_ODD, 3, D), 3.0 ** -0.5),
        'conv_w_out': nrm(ks[25], (N_ODD, D, D), D ** -0.5),
    }

def reference(x, c, ctx, c_ctx, mod_w, mod_b, norm_g, mlp_w1, mlp_w2, ab_w_in, ab_w_out, att_sink,
              rwkv_mu, rwkv_w0, rwkv_w2, rwkv_a0, rwkv_a2, rwkv_g2, rwkv_kk, rwkv_ka, rwkv_rk,
              rwkv_ln_w, rwkv_ln_b, conv_w_in, conv_w, conv_w_out):
    S = x.shape[1]
    rows = S // GRID_W
    t = jnp.arange(rows * GRID_W)
    row, col = t // GRID_W, t % GRID_W
    last_even = DEPTH - 1 if (DEPTH - 1) % 2 == 0 else DEPTH - 2
    xl, xc = x, ctx
    for i in range(DEPTH):
        need_ctx = i < last_even
        ctx_live = (i % 2 == 0) or need_ctx
        mod_l = (jax.nn.silu(c) @ mod_w[i] + mod_b[i])[:, None, :]
        sh_a, sc_a, gt_a, sh_m, sc_m, gt_m = jnp.split(mod_l, 6, axis=-1)
        hl = rms_norm(xl, norm_g[i, 0]) * (1 + sc_a) + sh_a
        hc = None
        if ctx_live:
            mod_c = (jax.nn.silu(c_ctx) @ mod_w[i] + mod_b[i])[None, None, :]
            csh_a, csc_a, cgt_a, csh_m, csc_m, cgt_m = jnp.split(mod_c, 6, axis=-1)
            hc = rms_norm(xc, norm_g[i, 0]) * (1 + csc_a) + csh_a
        if i % 2 == 0:
            e = i // 2
            lp = dict(w_in=ab_w_in[e], w_out=ab_w_out[e], sink=att_sink[e], mu=rwkv_mu[e],
                      w0=rwkv_w0[e], w2=rwkv_w2[e], a0=rwkv_a0[e], a2=rwkv_a2[e], g2=rwkv_g2[e],
                      kk=rwkv_kk[e], ka=rwkv_ka[e], rk=rwkv_rk[e], ln_w=rwkv_ln_w[e], ln_b=rwkv_ln_b[e])
            yl, yc = ab_mixer(hl, hc, row, col, lp, need_ctx)
        else:
            o = i // 2
            yl = conv_mixer(hl, conv_w_in[o], conv_w[o], conv_w_out[o])
            yc = conv_mixer(hc, conv_w_in[o], conv_w[o], conv_w_out[o]) if need_ctx else None
        xl = xl + gt_a * rms_norm(yl, norm_g[i, 1])
        hm = rms_norm(xl, norm_g[i, 2]) * (1 + sc_m) + sh_m
        xl = xl + gt_m * rms_norm(sq_relu_mlp(hm, mlp_w1[i], mlp_w2[i]), norm_g[i, 3])
        if need_ctx:
            xc = xc + cgt_a * rms_norm(yc, norm_g[i, 1])
            hmc = rms_norm(xc, norm_g[i, 2]) * (1 + csc_m) + csh_m
            xc = xc + cgt_m * rms_norm(sq_relu_mlp(hmc, mlp_w1[i], mlp_w2[i]), norm_g[i, 3])
    return xl


_drawn_inputs = setup_inputs


def setup_inputs(seed=0):
    import zlib

    import numpy as np

    out = dict(_drawn_inputs(seed))
    spreads = {}
    factors = {'norm_g': 2.715,
     'att_sink': 64.0,
     'rwkv_w2': 2.894,
     'rwkv_kk': 61.21,
     'rwkv_ka': 2.758,
     'rwkv_ln_w': 38.814,
     'rwkv_ln_b': 34.924}
    for name, (base, spread) in spreads.items():
        noise = np.random.default_rng([zlib.crc32(name.encode()), seed]).standard_normal(out[name].shape)
        drawn = base * np.exp(spread * noise) if base else spread * noise
        out[name] = __import__('jax').numpy.asarray(drawn.astype(out[name].dtype))
    for name, factor in factors.items():
        out[name] = (out[name] * factor).astype(out[name].dtype)
    return out
```

```python
_PRM = [("modb0", 48), ("modb1", 48), ("g00", 8), ("g01", 8), ("g02", 8), ("g03", 8), ("g10", 8), ("g11", 8),
        ("g12", 8), ("g13", 8), ("mu", 15), ("w0", 8), ("a0", 8), ("kk", 4), ("ka", 4), ("rk", 4), ("lnw", 4),
        ("lnb", 4), ("cw", 24), ("sink", 8), ("c", 16)]
_CST = [("ident", 128), ("ones", 128), ("onesh", 128), ("scan", 768), ("upper", 64), ("upper_eq", 64), ("lower", 64),
        ("lvl1", 64), ("lvl1t", 64), ("eye64", 64), ("lvl", 5 * 64)]
_CSA = [("rot", 128), ("sel", 512), ("cos", 512), ("sin", 512), ("band_lo", 128), ("band_hi", 128)]


def _columns(table):
    at, out = 0, {}
    for name, n in table:
        out[name] = (at, n)
        at += n
    return out, at

def _constants(np, T, C, table):
    f = np.float32
    r, c = np.arange(128)[:, None], np.arange(128)[None, :]
    out = {"ident": r == c, "ones": np.ones((128, 128)), "onesh": r // 64 == c // 64}
    rot = np.where((c % 32 < 16) & (r == c + 16), -1.0, 0.0) + np.where((c % 32 >= 16) & (r == c - 16), 1.0, 0.0)
    out["rot"] = rot
    sel = []
    for kv in range(2):
        s = (r == kv * 64 + c % 64).astype(f)
        sel += [s, rot @ s]
    out["sel"] = np.concatenate(sel, 1)
    m = 16
    inv = (10000.0 ** (-np.arange(m, dtype=f) / m)).astype(f)
    t = np.arange(T)
    ch = np.arange(128)
    pos = np.where((ch % 64 < 32)[:, None], (t // 64)[None, :], (t % 64)[None, :]).astype(f)
    ang = (pos * inv[ch % 16][:, None]).astype(f)
    out["cos"], out["sin"] = np.cos(ang), np.sin(ang)
    out["band_lo"] = np.where(c >= r, 0.0, -1e30)
    out["band_hi"] = np.where(c <= r, 0.0, -1e30)
    out["scan"] = np.broadcast_to((np.arange(T + C) % 64 != 0)[None, :], (128, T + C))
    i, j = np.arange(128)[:, None] % 64, np.arange(64)[None, :]
    out["upper"], out["upper_eq"], out["lower"] = i < j, i <= j, i > j
    l1 = (i // 2 == j // 2) & (i > j)
    out["lvl1"], out["lvl1t"], out["eye64"] = l1, (i // 2 == j // 2) & (i < j), i == j
    out["lvl"] = np.concatenate([(i // (2 * n) == j // (2 * n)) & (i // n > j // n) for n in (2, 4, 8, 16, 32)], 1)
    return np.concatenate([np.asarray(out[name]).astype(f) for name, _ in table], axis=1)


def build(nc, A):
    from contextlib import ExitStack
    import concourse.bass as bass
    from concourse import mybir

    F32, F32R = mybir.dt.float32, mybir.dt.float32r
    ALU, ACT, AX = mybir.AluOpType, mybir.ActivationFunctionType, mybir.AxisListType
    MUL, ADD, SUB, MAX, MIN = ALU.mult, ALU.add, ALU.subtract, ALU.max, ALU.min

    P = 128
    T = A["x"].shape[2]
    C = A["ctx"].shape[2]
    KT = A["x"].shape[1]
    N = C + T
    D = KT * P
    EPS, GN_EPS = 1e-6, 64e-5
    DECAY = 0.6065306597126334
    HD = 64
    PAIRS = 4
    Q = 64
    G = 2 * N // P
    GD = N // P
    GC = C // P
    NBLK = A["w"].shape[0]
    S_MOD0A, S_IN, S_MOD, S_OUT, S_MLP0, S_CIN, S_COUT, S_MLP1 = 0, 8, 19, 59, 63, 95, 107, 111
    assert NBLK == S_MLP1 + 32

    prm_at, NPRM = _columns(_PRM)
    cst_at, NCST = _columns(_CST)
    csa_at, NCSA = _columns(_CSA)
    top = ExitStack()

    taken = {}

    def own(name):
        taken[name] = taken.get(name, 0) + 1
        return name if taken[name] == 1 else f"{name}_{taken[name]}"

    def sb(stack, name, shape, dt=F32):
        return stack.enter_context(nc.sbuf_tensor(own(name), shape, dt))

    def sems(stack, *names):
        return [stack.enter_context(nc.semaphore(own(n))) for n in names]

    class Chain:

        def __init__(self, eng, sem):
            self.eng, self.sem, self.n = eng, sem, 0

        def __call__(self, ins):
            self.n += 1
            ins.then_inc(self.sem, 1)
            self.eng.wait_ge(self.sem, self.n)

    cst = sb(top, "cst", [P, NCST])
    prm = sb(top, "prm", [P, NPRM])
    x = sb(top, "xres", [P, KT, T])
    yb = sb(top, "yb", [P, KT, T])
    raw = [sb(top, f"raw{s}", [P, KT, 256]) for s in range(2)]
    mod = sb(top, "mod", [P, 2, 48, 2])
    cs = sb(top, "cs", [P, KT, 2])
    nsc = sb(top, "nsc", [P, 4, KT])
    small = sb(top, "small", [P, 64])
    psum = [top.enter_context(nc.psum_tensor(f"bank{i}", [P, 1024], F32)) for i in range(4)]

    def bank(i, lo=0, hi=512):
        return psum[i // 2][:, (i % 2) * 512 + lo:(i % 2) * 512 + hi]

    def K(name, lo=0, hi=None):
        a, n = cst_at[name]
        return cst[:, a + lo:a + (n if hi is None else hi)]

    def KA(name):
        a, n = csa_at[name]
        return csa[:, a:a + n]

    def R(name, lo=0, hi=None):
        a, n = prm_at[name]
        return prm[:, a + lo:a + (n if hi is None else hi)]

    raw_loaded = sems(top, "raw_loaded0", "raw_loaded1")
    hi_ready = sems(top, "hi_ready0", "hi_ready1")
    split_ready = sems(top, "split_ready0", "split_ready1")
    mod_used = sems(top, "mod_used0", "mod_used1")
    tile_done = [sems(top, f"tile_done{s}0", f"tile_done{s}1") for s in range(2)]
    tile_free = [sems(top, f"tile_free{s}0", f"tile_free{s}1") for s in range(2)]

    def is_mod(n):
        return n < S_IN or S_MOD <= n < S_OUT

    def nth(n):
        return sum(is_mod(m) == is_mod(n) for m in range(n % 2, n + 1, 2))

    def clear(stack_sems):
        with nc.Block() as block:
            @block.gpsimd
            def _(pool):
                for s in stack_sems:
                    pool.sem_clear(s)

    def sp_load(sp, n, up=0):
        sp.dma_start(raw[n % 2][:].rearrange("p k m -> p (k m)"), A["w"][n + up]).then_inc(raw_loaded[n % 2], 16)

    def sp_next(sp, n, up=0):
        if is_mod(n):
            sp.wait_ge(mod_used[n % 2], nth(n) + up // 2)
        else:
            sp.wait_ge(split_ready[n % 2], nth(n) + up // 2)
        sp_load(sp, n + 2, up)

    def act_hi(act, n, W, up=0):
        act.wait_ge(raw_loaded[n % 2], 16 * (n // 2 + 1) + 8 * up)
        if nth(n) > 1:
            act.wait_ge(tile_done[n % 2][1], nth(n) - 1 + up // 2)
        nc.scalar.activation(W[0][n % 2][:], raw[n % 2][:], ACT.Copy).then_inc(hi_ready[n % 2], 1)

    def pool_lo(pool, n, W, up=0):
        pool.wait_ge(hi_ready[n % 2], nth(n) + up // 2)
        nc.gpsimd.tensor_tensor(W[1][n % 2][:], raw[n % 2][:], W[0][n % 2][:].bitcast(F32), SUB)\
            .then_inc(split_ready[n % 2], 1)

    def pe_block(pe, n, W, H, up=0, tiles=2, parts=((0, None),), ready=None, start_k=0):
        s = n % 2
        pe.wait_ge(split_ready[s], nth(n) + up // 2)
        for m in range(tiles):
            if nth(n) > 1:
                pe.wait_ge(tile_free[s][m], nth(n) - 1 + up // 2)
            for k in range(KT):
                if ready is not None and m == 0:
                    pe.wait_ge(ready[0], ready[1](k))
                for w, h in ((0, 0), (0, 1), (1, 0)):
                    for b, (lo, hi) in parts:
                        last = nc.tensor.matmul(bank(b(s, m), 0, hi - lo), W[w][s][:, k, m * P:(m + 1) * P],
                                                H[h][:, k, lo:hi], start=(k == 0 and w == h == 0),
                                                stop=(k == KT - 1 and w == 1))
            last.then_inc(tile_done[s][m], 1)

    def clear_then_block(stack_sems):
        clear(stack_sems)
        return nc.Block()

    mix = ExitStack()
    qT, rT = yb[:, 0:PAIRS, :], yb[:, PAIRS:KT, :]
    attT = qT
    kT = sb(mix, "kT", [P, PAIRS, N])
    vT = sb(mix, "vT", [P, PAIRS, N])
    lora = sb(mix, "lora", [P, 2, N])
    gT = sb(mix, "gT", [P, T])
    kkT = sb(mix, "kkT", [P, PAIRS, N])
    att_in = ExitStack()
    csa = sb(att_in, "csa", [P, NCSA])
    kvT = sb(att_in, "kvT", [P, 2, N])
    proj = ExitStack()
    hT = [sb(proj, f"h{i}", [P, KT, N], F32R) for i in range(2)]
    W = [[sb(proj, f"w{i}{s}", [P, KT, 256], F32R) for s in range(2)] for i in range(2)]
    with ExitStack() as st:
        ctxT = kkT[:].rearrange("p a n -> p (a n)")[:, 0:KT * C].rearrange("p (k c) -> p k c", c=C)
        sq, rst = [kT[:, i, :] for i in range(2)], kT[:, 2, :]
        hf = [vT[:, i, :] for i in range(2)]
        S = sems(st, "const_in", "x_in", "csig", "cs_ready", "mod_done", "mod_ready", "sq_ready", "sq_used",
                 "ssum_done", "root_ready", "rst_ready", "hf_ready", "hs_ready", "hhi_ready", "hf_used", "dve_chain",
                 "csa_in")
        (const_in, x_in, csig, cs_ready, mod_done, mod_ready, sq_ready, sq_used, ssum_done, root_ready,
         rst_ready, hf_ready, hs_ready, hhi_ready, hf_used, dve_chain, csa_in) = S
        with nc.Block() as block:
            @block.sync
            def _(sp):
                sp.dma_start(prm[:], A["prm"]).then_inc(const_in, 16)
                sp_load(sp, 0)
                sp_load(sp, 1)
                with sp.Fori(0, S_IN // 2) as turn:
                    n = 2 * turn
                    for s in range(2):
                        sp_next(sp, s, n)
                sp.wait_ge(csa_in, 16)

            @block.scalar
            def _(act):
                act.dma_start(x[:], A["x"]).then_inc(x_in, 16)
                act.dma_start(ctxT, A["ctx"]).then_inc(x_in, 16)
                act.dma_start(cst[:], A["cst"]).then_inc(x_in, 16)
                act.dma_start(csa[:], A["csa"]).then_inc(csa_in, 16)
                act.wait_ge(const_in, 16)
                nc.scalar.activation(cs[:].rearrange("p k c -> p (k c)"), R("c"), ACT.Sigmoid).then_inc(csig, 1)
                act.wait_ge(x_in, 48)
                for k in range(KT):
                    if k >= 2:
                        act.wait_ge(sq_used, k - 1)
                    nc.scalar.activation(sq[k % 2][:, 0:C], ctxT[:, k], ACT.Square)
                    nc.scalar.activation(sq[k % 2][:, C:N], x[:, k], ACT.Square).then_inc(sq_ready, 1)
                act.wait_ge(ssum_done, 1)
                act.wait_ge(mod_ready, 1)
                nc.scalar.activation(rst[:, 0:C], bank(3, 0, C), ACT.Sqrt, bias=small[:, 0:1], scale=1.0 / D)
                nc.scalar.activation(rst[:, C:N], bank(2), ACT.Sqrt, bias=small[:, 0:1], scale=1.0 / D)\
                    .then_inc(root_ready, 1)
                act.wait_ge(mod_ready, 2)
                for k in range(KT):
                    act.wait_ge(hf_ready, k + 1)
                    f = hf[k % 2]
                    nc.scalar.activation(f[:, 0:C], f[:, 0:C], ACT.Identity, scale=nsc[:, 1, k:k + 1],
                                         bias=mod[:, 0, k, 1:2])
                    nc.scalar.activation(f[:, C:N], f[:, C:N], ACT.Identity, scale=nsc[:, 0, k:k + 1],
                                         bias=mod[:, 0, k, 0:1]).then_inc(hs_ready, 1)
                    act.wait_ge(hs_ready, k + 1)
                    nc.scalar.activation(hT[0][:, k], f, ACT.Copy).then_inc(hhi_ready, 1)

            @block.tensor
            def _(pe):
                pe.wait_ge(x_in, 48)
                for k in range(KT):
                    pe.wait_ge(sq_ready, k + 1)
                    nc.tensor.matmul(bank(2), K("ones"), sq[k % 2][:, C:N], start=k == 0, stop=k == KT - 1)
                    nc.tensor.matmul(bank(3, 0, C), K("ones"), sq[k % 2][:, 0:C], start=k == 0, stop=k == KT - 1)\
                        .then_inc(sq_used if k < KT - 1 else ssum_done, 1)
                pe.wait_ge(cs_ready, 1)
                for n in range(S_IN):
                    pe.wait_ge(raw_loaded[n % 2], 16 * (n // 2 + 1))
                    for m in range(2):
                        for k in range(KT):
                            last = nc.tensor.matmul(bank(0, 4 * n + 2 * m, 4 * n + 2 * m + 2),
                                                    raw[n % 2][:, k, m * P:(m + 1) * P], cs[:, k, :],
                                                    start=k == 0, stop=k == KT - 1)
                    last.then_inc(mod_used[n % 2], 1)

            @block.vector
            def _(dve):
                link = Chain(dve, dve_chain)
                nc.vector.memset(small[:, 0:1], EPS)
                nc.vector.memset(small[:, 1:2], GN_EPS).then_inc(mod_ready, 1)
                dve.wait_ge(csig, 1)
                link(nc.vector.tensor_tensor(cs[:].rearrange("p k c -> p (k c)"), cs[:].rearrange("p k c -> p (k c)"),
                                             R("c"), MUL))
                dve.sem_inc(cs_ready, 1)
                for s in range(2):
                    dve.wait_ge(mod_used[s], S_IN // 2)
                link(nc.vector.tensor_tensor(mod[:, 0, 0:16, :], bank(0, 0, 32).rearrange("p (m c) -> p m c", c=2),
                                             R("modb0", 0, 16).unsqueeze(2).to_broadcast([P, 16, 2]), ADD))
                for c in range(2):
                    i = nc.vector.scalar_tensor_tensor(nsc[:, c, :], mod[:, 0, 8:16, c], 1.0, R("g00"), ADD, MUL)
                i.then_inc(mod_ready, 1)
                dve.wait_ge(root_ready, 1)
                link(nc.vector.reciprocal(rst, rst))
                for k in range(KT):
                    if k >= 2:
                        dve.wait_ge(hf_used, k - 1)
                    nc.vector.tensor_tensor(hf[k % 2][:, 0:C], ctxT[:, k], rst[:, 0:C], MUL)
                    nc.vector.tensor_tensor(hf[k % 2][:, C:N], x[:, k], rst[:, C:N], MUL).then_inc(hf_ready, 1)

            @block.gpsimd
            def _(pool):
                for k in range(KT):
                    pool.wait_ge(hhi_ready, k + 1)
                    nc.gpsimd.tensor_tensor(hT[1][:, k], hf[k % 2], hT[0][:, k].bitcast(F32), SUB)\
                        .then_inc(hf_used, 1)

    with ExitStack() as st:
        pad = [sb(st, f"pad{i}", [P, N + 4]) for i in range(2)]
        nb = [sb(st, f"nb{i}", [P, N + 2]) for i in range(2)]
        mus = sb(st, "mus", [P, 2, 15])
        S = sems(st, "mus_ready", "pad_ready", "pad_used", "base_ready", "mixed", "dve_chain")
        mus_ready, pad_ready, pad_used, base_ready, mixed, dve_chain = S
        dest = [(qT[:, i, :], C) for i in range(4)] + [(kvT[:, i, :], 0) for i in range(2)] \
            + [(rT[:, i, :], C) for i in range(4)] + [(kT[:, i, :], 0) for i in range(4)] \
            + [(vT[:, i, :], 0) for i in range(4)] + [(lora[:, i, :], 0) for i in range(2)] + [(gT[:], C)]
        NB = S_MOD - S_IN

        def acc(n, m, lo, hi):
            t = psum[2 * (n % 2) + m]
            return t[:, 512 + lo:512 + hi] if lo < C else t[:, lo - C:hi - C]

        with clear_then_block(S) as block:
            @block.sync
            def _(sp):
                sp_next(sp, S_IN)
                with sp.Fori(0, (NB - 1) // 2) as turn:
                    up = 2 * turn
                    for j in range(2):
                        sp_next(sp, S_IN + 1 + j, up)

            @block.tensor
            def _(pe):
                b = lambda s, m: 2 * (2 * s + m)
                bc = lambda s, m: 2 * (2 * s + m) + 1
                both = ((b, (C, N)), (bc, (0, C)))
                for n in range(S_IN, S_IN + 2):
                    pe_block(pe, n, W, hT, parts=both[:1])
                with pe.Fori(0, (NB - 3) // 2) as turn:
                    up = 2 * turn
                    for j in range(2):
                        pe_block(pe, S_IN + 2 + j, W, hT, up=up, parts=both)
                pe_block(pe, S_MOD - 1, W, hT, tiles=1, parts=both[:1])
                pe.sem_inc(tile_done[(S_MOD - 1) % 2][1], 1)

            @block.gpsimd
            def _(pool):
                pool_lo(pool, S_IN, W)
                with pool.Fori(0, (NB - 1) // 2) as turn:
                    up = 2 * turn
                    for j in range(2):
                        pool_lo(pool, S_IN + 1 + j, W, up)

            @block.scalar
            def _(act):
                act_hi(act, S_IN, W)
                act_hi(act, S_IN + 1, W)
                for n in range(S_IN, S_MOD):
                    for m in range(2):
                        t = 2 * (n - S_IN) + m
                        if t > 20:
                            act.sem_inc(tile_free[n % 2][1], 1)
                            continue
                        act.wait_ge(tile_done[n % 2][m], nth(n))
                        d, first = dest[t]
                        segs = ((0, C), (C, N))[first > 0:]
                        if t < 6:
                            for lo, hi in segs:
                                i = nc.scalar.activation(d[:, lo - first:hi - first], acc(n, m, lo, hi), ACT.Copy)
                        else:
                            j = t - 6
                            if j == 0:
                                act.wait_ge(mus_ready, 1)
                            if j >= 2:
                                act.wait_ge(pad_used, j - 1)
                            for lo, hi in segs:
                                o = 1 + 2 * (lo > 0)
                                i = nc.scalar.activation(pad[j % 2][:, o + lo:o + hi], acc(n, m, lo, hi), ACT.Copy)
                            i.then_inc(pad_ready, 1)
                            for lo, hi in segs:
                                i = nc.scalar.activation(d[:, lo - first:hi - first], acc(n, m, lo, hi), ACT.Copy,
                                                         scale=mus[:, 0, j:j + 1])
                        i.then_inc(tile_free[n % 2][m], 1)
                    if n + 2 < S_MOD:
                        act_hi(act, n + 2, W)
                act.wait_ge(mixed, 15)
                nc.scalar.activation(lora[:, 0, :], lora[:, 0, :], ACT.Tanh)
                nc.scalar.activation(gT[:], gT[:], ACT.Sigmoid)

            @block.vector
            def _(dve):
                link = Chain(dve, dve_chain)
                for i in range(2):
                    nc.vector.memset(pad[i][:], 0.0)
                nc.vector.tensor_scalar(mus[:, 1, :], R("mu"), 0.5, None, MUL)
                link(nc.vector.tensor_scalar(mus[:, 0, :], R("mu"), -1.0, 1.0, MUL, ADD))
                dve.sem_inc(mus_ready, 1)
                for j in range(15):
                    n, m = S_IN + (j + 6) // 2, j % 2
                    d, first = dest[j + 6]
                    segs = ((0, C), (C, N))[first > 0:]
                    dve.wait_ge(pad_ready, j + 1)
                    a = segs[0][0] + (2 if first else 0)
                    link(nc.vector.tensor_tensor(nb[j % 2][:, a:N + 2], pad[j % 2][:, a:N + 2],
                                                 pad[j % 2][:, a + 2:N + 4], ADD))
                    dve.sem_inc(pad_used, 1)
                    dve.wait_ge(tile_free[n % 2][m], nth(n))
                    for lo, hi in segs:
                        o = 2 * (lo > 0)
                        i = nc.vector.scalar_tensor_tensor(d[:, lo - first:hi - first], nb[j % 2][:, o + lo:o + hi],
                                                           mus[:, 1, j:j + 1], d[:, lo - first:hi - first], MUL, ADD)
                    i.then_inc(mixed, 1)
    proj.close()

    vtok = sb(att_in, "vtok", [P, GD, P])
    NM = S_OUT - S_MOD
    with ExitStack() as st:
        sq = [sb(st, f"ksq{i}", [P, N]) for i in range(2)]
        nrm = sb(st, "knorm", [P, PAIRS, N])
        S = sems(st, "mod_done", "ksq_ready", "knorm_sum", "knorm_used", "knorm_ready", "vt_done", "dve_chain")
        mod_done, ksq_ready, knorm_sum, knorm_used, knorm_ready, vt_done, dve_chain = S
        with clear_then_block(S) as block:
            @block.sync
            def _(sp):
                with sp.Fori(0, NM // 2) as turn:
                    up = 2 * turn
                    for s in range(2):
                        sp_next(sp, S_MOD + s, up)

            @block.tensor
            def _(pe):
                for g in range(GD):
                    last = nc.tensor.transpose(psum[3][:, g * P:(g + 1) * P], kvT[:, 1, g * P:(g + 1) * P], K("ident"))
                last.then_inc(vt_done, 1)
                for p in range(PAIRS):
                    pe.wait_ge(ksq_ready, p + 1)
                    if p >= 2:
                        pe.wait_ge(knorm_used, p - 1)
                    for lo, hi in ((0, 512), (512, N)):
                        last = nc.tensor.matmul(psum[1 + p % 2][:, lo:hi], K("onesh"), sq[p % 2][:, lo:hi],
                                                start=True, stop=True)
                    last.then_inc(knorm_sum, 1)
                with pe.Fori(0, NM // 2) as turn:
                    up = 2 * turn
                    for s in range(2):
                        n = S_MOD + s
                        pe.wait_ge(raw_loaded[n % 2], 16 * (n // 2 + 1) + 8 * up)
                        for m in range(2):
                            for k in range(KT):
                                last = nc.tensor.matmul(psum[0][:, bass.ds(4 * up + 4 * s + 2 * m, 2)],
                                                        raw[n % 2][:, k, m * P:(m + 1) * P], cs[:, k, :],
                                                        start=k == 0, stop=k == KT - 1)
                        last.then_inc(mod_used[n % 2], 1)

            @block.scalar
            def _(act):
                for p in range(PAIRS):
                    act.wait_ge(knorm_sum, p + 1)
                    nc.scalar.activation(nrm[:, p, :], psum[1 + p % 2][:, 0:N], ACT.Sqrt).then_inc(knorm_used, 1)
                act.wait_ge(vt_done, 1)
                nc.scalar.activation(vtok[:].rearrange("p g c -> p (g c)"), psum[3][:, 0:N], ACT.Copy)

            @block.vector
            def _(dve):
                link = Chain(dve, dve_chain)
                for p in range(PAIRS):
                    if p >= 2:
                        dve.wait_ge(knorm_sum, p - 1)
                    nc.vector.tensor_scalar(kkT[:, p, :], kT[:, p, :], R("kk", p, p + 1), None, MUL)
                    link(nc.vector.tensor_scalar(sq[p % 2][:], kT[:, p, :], R("kk", p, p + 1), None, MUL))
                    nc.vector.tensor_tensor(sq[p % 2][:], sq[p % 2][:], sq[p % 2][:], MUL).then_inc(ksq_ready, 1)
                for p in range(PAIRS):
                    dve.wait_ge(knorm_used, p + 1)
                    link(nc.vector.tensor_scalar(nrm[:, p, :], nrm[:, p, :], 1e-12, None, MAX))
                    link(nc.vector.reciprocal(nrm[:, p, :], nrm[:, p, :]))
                    link(nc.vector.tensor_tensor(kkT[:, p, :], kkT[:, p, :], nrm[:, p, :], MUL))
                for s in range(2):
                    dve.wait_ge(mod_used[s], S_IN // 2 + NM // 2)
                nl0 = 32 * 2
                nc.vector.tensor_tensor(mod[:, 0, 16:48, :], psum[0][:, 0:nl0].rearrange("p (m c) -> p m c", c=2),
                                        R("modb0", 16, 48).unsqueeze(2).to_broadcast([P, 32, 2]), ADD)
                nc.vector.tensor_tensor(mod[:, 1, :, :], psum[0][:, nl0:nl0 + 96].rearrange("p (m c) -> p m c", c=2),
                                        R("modb1").unsqueeze(2).to_broadcast([P, 48, 2]), ADD)

    NQ = T // P
    with ExitStack() as st:
        selS = sb(st, "selS", [P, 2, P])
        kd = sb(st, "kd", [P, N])
        vS = sb(st, "vS", [P, GD, HD])
        qs = [sb(st, f"qs{i}", [P, T]) for i in range(2)]
        tmp = [sb(st, f"rot{i}", [P, T]) for i in range(3)]
        pr = [sb(st, f"prob{i}", [P, 5 * P]) for i in range(2)]
        pt = [sb(st, f"probT{i}", [P, 5 * P]) for i in range(2)]
        stat = [sb(st, f"stat{i}", [P, 8]) for i in range(2)]
        S = sems(st, "sel_ready", "kd_done", "q_done", "rot_used", "kd_ready", "q_ready", "vs_ready", "s_done",
                 "max_ready", "exp_ready", "p_ready", "pt_done", "pt_ready", "o_done", "att_ready", "dve_chain",
                 "sink_ready")
        (sel_ready, kd_done, q_done, rot_used, kd_ready, q_ready, vs_ready, s_done, max_ready, exp_ready, p_ready,
         pt_done, pt_ready, o_done, att_ready, dve_chain, sink_ready) = S
        units = [(i, b, h) for i in range(2) for b in range(NQ) for h in range(2)]

        def keys(b):
            return [j for j in (b - 1, b, b + 1) if 0 <= j < NQ]

        with nc.Fori(0, 2) as kv:
            with clear_then_block(S) as block:
                @block.scalar
                def _(act):
                    nc.scalar.activation(selS[:].rearrange("p a c -> p (a c)"),
                                         csa[:, bass.ds(csa_at["sel"][0] + kv * 256, 256)], ACT.Copy)\
                        .then_inc(sel_ready, 1)
                    nc.scalar.activation(vS[:], vtok[:, :, bass.ds(kv * HD, HD)], ACT.Copy).then_inc(vs_ready, 1)
                    act.wait_ge(kd_done, 1)
                    nc.scalar.activation(kd[:, 0:C], psum[0][:, 0:C], ACT.Copy).then_inc(sel_ready, 1)

                    def transposed(u):
                        i, b, h = units[u]
                        w = (2 + len(keys(b))) * P
                        act.wait_ge(pt_done, u + 1)
                        if u >= 2:
                            act.wait_ge(o_done, u - 1)
                        nc.scalar.activation(pt[u % 2][:, 0:w], psum[2][:, 0:w], ACT.Copy).then_inc(pt_ready, 1)

                    for u, (i, b, h) in enumerate(units):
                        w = (2 + len(keys(b))) * P
                        act.wait_ge(max_ready, u + 1)
                        if u >= 2:
                            act.wait_ge(pt_done, u - 1)
                        nc.scalar.activation(pr[u % 2][:, 0:w], psum[u % 2][:, 0:w], ACT.Exp,
                                             bias=stat[u % 2][:, 1:2], scale=HD ** -0.5,
                                             accum_out=stat[u % 2][:, 2:3])
                        nc.scalar.activation(stat[u % 2][:, 3:4], stat[u % 2][:, 4:5], ACT.Exp,
                                             bias=stat[u % 2][:, 1:2], scale=1.0).then_inc(exp_ready, 1)
                        if u >= 1:
                            transposed(u - 1)
                    transposed(len(units) - 1)

                @block.tensor
                def _(pe):
                    pe.wait_ge(sel_ready, 1)
                    for lo, hi in ((0, C), (C, 512), (512, N)):
                        nc.tensor.matmul(psum[0][:, lo:hi], selS[:, 0, :], kvT[:, 0, lo:hi], start=True, stop=True)
                    for a, lo, hi in ((0, C, 512), (256, 512, N)):
                        last = nc.tensor.matmul(psum[1][:, a:a + hi - lo], selS[:, 1, :], kvT[:, 0, lo:hi],
                                                start=True, stop=True)
                    last.then_inc(kd_done, 1)
                    for i in range(2):
                        last = nc.tensor.matmul(bank(4 + i), KA("rot"), qT[:, 2 * kv + i, :], start=True,
                                                stop=True)
                        last.then_inc(q_done, 1)

                    def scores(u):
                        i, b, h = units[u]
                        r = slice(h * HD, (h + 1) * HD)
                        lhs = qs[i][r, b * P:(b + 1) * P]
                        js = keys(b)
                        pe.wait_ge(q_ready, i + 1)
                        if u >= 2:
                            pe.wait_ge(exp_ready, u - 1)
                        t = psum[u % 2]
                        nc.tensor.matmul(t[:, 0:C], lhs, kd[r, 0:C], start=True, stop=True)
                        at = C + js[0] * P
                        n0 = min(len(js) * P, 512 - C)
                        last = nc.tensor.matmul(t[:, C:C + n0], lhs, kd[r, at:at + n0], start=True, stop=True)
                        if len(js) == 3:
                            last = nc.tensor.matmul(t[:, 512:512 + P], lhs, kd[r, at + n0:at + n0 + P], start=True,
                                                    stop=True)
                        last.then_inc(s_done, 1)

                    def products(u):
                        i, b, h = units[u]
                        n = 2 + len(keys(b))
                        pe.wait_ge(pt_ready, u + 1)
                        if u == 0:
                            pe.wait_ge(vs_ready, 1)
                        for c in range(n):
                            g = c if c < 2 else GC + keys(b)[c - 2]
                            last = nc.tensor.matmul(bank(6 + i, b * P, (b + 1) * P)[h * HD:(h + 1) * HD], vS[:, g, :],
                                                    pt[u % 2][:, c * P:(c + 1) * P], start=c == 0, stop=c == n - 1)
                        last.then_inc(o_done, 1)

                    pe.wait_ge(kd_ready, 1)
                    scores(0)
                    for u, (i, b, h) in enumerate(units):
                        if u + 1 < len(units):
                            scores(u + 1)
                        pe.wait_ge(p_ready, u + 1)
                        if u >= 1:
                            pe.wait_ge(pt_ready, u)
                        else:
                            pe.wait_ge(q_ready, 2)
                        for c in range(2 + len(keys(b))):
                            last = nc.tensor.transpose(psum[2][:, c * P:(c + 1) * P],
                                                       pr[u % 2][:, c * P:(c + 1) * P], K("ident"))
                        last.then_inc(pt_done, 1)
                        products(u)

                @block.vector
                def _(dve):
                    link = Chain(dve, dve_chain)
                    dve.wait_ge(kd_done, 1)
                    dve.wait_ge(sel_ready, 2)
                    nc.vector.tensor_tensor(tmp[0][:], psum[0][:, C:N], KA("cos"), MUL)
                    link(nc.vector.tensor_tensor(tmp[1][:], psum[1][:, 0:T], KA("sin"), MUL))
                    link(nc.vector.tensor_tensor(kd[:, C:N], tmp[0][:], tmp[1][:], ADD))
                    dve.sem_inc(kd_ready, 1)
                    for i in range(2):
                        dve.wait_ge(q_done, i + 1)
                        nc.vector.tensor_tensor(tmp[0][:], qT[:, 2 * kv + i, :], KA("cos"), MUL)
                        link(nc.vector.tensor_tensor(tmp[1][:], bank(4 + i), KA("sin"), MUL))
                        link(nc.vector.tensor_tensor(qs[i][:], tmp[0][:], tmp[1][:], ADD))
                        dve.sem_inc(q_ready, 1)

                    def maximum(u):
                        i, b, h = units[u]
                        js = keys(b)
                        w = (2 + len(js)) * P
                        t, sc = psum[u % 2], stat[u % 2]
                        dve.wait_ge(s_done, u + 1)
                        for c, j in enumerate(js):
                            if j != b:
                                a = C + c * P
                                nc.vector.tensor_tensor(t[:, a:a + P], t[:, a:a + P],
                                                        KA("band_lo" if j < b else "band_hi"), ADD)\
                                    .then_inc(sink_ready, 1)
                                sink_n[0] += 1
                        nc.vector.tensor_copy(sc[:, 4:5], prm[:, bass.ds(prm_at["sink"][0] + kv * 4 + 2 * i + h, 1)])\
                            .then_inc(sink_ready, 1)
                        sink_n[0] += 1
                        dve.wait_ge(sink_ready, sink_n[0])
                        link(nc.vector.reduce_max(sc[:, 0:1], t[:, 0:w], AX.X))
                        link(nc.vector.tensor_scalar(sc[:, 0:1], sc[:, 0:1], HD ** -0.5, sc[:, 4:5], MUL, MAX))
                        nc.vector.tensor_scalar(sc[:, 1:2], sc[:, 0:1], -1.0, None, MUL).then_inc(max_ready, 1)

                    def normalise(u):
                        i, b, h = units[u]
                        w = (2 + len(keys(b))) * P
                        sc = stat[u % 2]
                        dve.wait_ge(exp_ready, u + 1)
                        link(nc.vector.tensor_tensor(sc[:, 5:6], sc[:, 2:3], sc[:, 3:4], ADD))
                        link(nc.vector.reciprocal(sc[:, 6:7], sc[:, 5:6]))
                        nc.vector.tensor_scalar(pr[u % 2][:, 0:w], pr[u % 2][:, 0:w], sc[:, 6:7], None, MUL)\
                            .then_inc(p_ready, 1)

                    sink_n = [0]
                    maximum(0)
                    for u in range(len(units)):
                        if u + 1 < len(units):
                            maximum(u + 1)
                        normalise(u)
                        if u % (2 * NQ) == 2 * NQ - 1:
                            i = u // (2 * NQ)
                            dve.wait_ge(o_done, u + 1)
                            nc.vector.tensor_copy(attT[:, 2 * kv + i, :], bank(6 + i))
    att_in.close()

    NCH = 2 * N // Q
    ND = N // Q
    LVL = 5
    drw = ExitStack()
    lws = sb(drw, "lws", [P, 2, P])
    vs = sb(drw, "vs", [P, 2, N])
    AR = sb(drw, "AR", [P, G, 2, P])
    bt = sb(drw, "bt", [P, 2, N])
    kt = sb(drw, "kt", [P, 2, N])
    PC = sb(drw, "PC", [P, NCH])

    def chunked(ap):
        return ap.rearrange("p (n t) -> p n t", t=Q)

    def tiled(ap):
        return ap.rearrange("p (g t) -> p g t", t=P)

    with nc.Fori(0, PAIRS) as p:
        with ExitStack() as st:
            names = ("sg", "cum", "al", "Pp", "Pn", "Pv", "kp", "bb")
            sg, cum, al, Pp, Pn, Pv, kp, bb = (sb(st, n, [P, 2, N]) for n in names)
            oka = sb(st, "oka", [P, 1])
            kkS, rS = sb(st, "kkS", [P, N]), sb(st, "rS", [P, T])
            S = sems(st, "lw_in", "lora_done", "sig_ready", "cum_ready", "exc_ready", "exp_ready", "kp_ready",
                     "bb_ready", "vs_ready", "bsum_in", "bsum_done", "dve_chain")
            (lw_in, lora_done, sig_ready, cum_ready, exc_ready, exp_ready, kp_ready, bb_ready, vs_ready, bsum_in,
             bsum_done, dve_chain) = S
            with clear_then_block(S) as block:
                @block.sync
                def _(sp):
                    sp.dma_start(lws[:], A["lw"][p]).then_inc(lw_in, 16)

                @block.tensor
                def _(pe):
                    pe.wait_ge(lw_in, 16)
                    for kind in range(2):
                        for d in range(2):
                            r = slice(d * HD, (d + 1) * HD)
                            for lo, hi in ((0, 512), (512, N)):
                                last = nc.tensor.matmul(psum[2 * kind + d][:, lo:hi], lws[r, kind, :],
                                                        lora[r, kind, lo:hi], start=True, stop=True)
                            last.then_inc(lora_done, 1)
                    pe.wait_ge(bsum_in, 1)
                    pe.wait_ge(sig_ready, 4)
                    nc.tensor.matmul(bank(0), K("onesh"), bb[:, 0, 0:T], start=True, stop=True).then_inc(bsum_done, 1)

                @block.scalar
                def _(act):
                    for kind, (dst, bias) in enumerate(((sg, "w0"), (al, "a0"))):
                        for d in range(2):
                            act.wait_ge(lora_done, 2 * kind + d + 1)
                            nc.scalar.activation(dst[:, d, :], psum[2 * kind + d][:, 0:N], ACT.Sigmoid,
                                                 bias=prm[:, bass.ds(prm_at[bias][0] + 4 * d + p, 1)])\
                                .then_inc(sig_ready, 1)
                    nc.scalar.activation(vs[:, 0, :], vT[:, p, :], ACT.Copy)
                    nc.scalar.activation(kkS[:], kkT[:, p, :], ACT.Copy)
                    nc.scalar.activation(rS[:], rT[:, p, :], ACT.Copy).then_inc(vs_ready, 1)
                    act.wait_ge(vs_ready, 1)
                    nc.scalar.activation(vs[:, 1, 0:C], vs[:, 0, 0:C][:, ::-1], ACT.Copy)
                    nc.scalar.activation(vs[:, 1, C:N], vs[:, 0, C:N][:, ::-1], ACT.Copy).then_inc(vs_ready, 1)
                    act.wait_ge(cum_ready, 1)
                    nc.scalar.activation(Pn[:], cum[:], ACT.Exp, scale=DECAY).then_inc(exp_ready, 1)
                    nc.scalar.activation(Pp[:], cum[:], ACT.Exp, scale=-DECAY).then_inc(exp_ready, 1)
                    act.wait_ge(exc_ready, 1)
                    nc.scalar.activation(Pv[:], sg[:], ACT.Exp, scale=-DECAY).then_inc(exp_ready, 1)

                @block.gpsimd
                def _(pool):
                    pool.wait_ge(sig_ready, 4)
                    for d in range(2):
                        i = nc.gpsimd.tensor_tensor(bb[:, d, :], kkT[:, p, :], al[:, d, :], MUL)
                    i.then_inc(bb_ready, 1)
                    pool.wait_ge(cum_ready, 1)
                    nc.gpsimd.tensor_tensor(sg[:], cum[:], sg[:], SUB).then_inc(exc_ready, 1)

                @block.vector
                def _(dve):
                    link = Chain(dve, dve_chain)
                    dve.wait_ge(sig_ready, 2)
                    nc.vector.tensor_tensor_scan(cum[:, 0, :], K("scan"), sg[:, 0, :], 0.0, MUL, ADD)
                    nc.vector.tensor_tensor_scan(cum[:, 1, :][:, ::-1], K("scan"), sg[:, 1, :][:, ::-1], 0.0, MUL,
                                                 ADD).then_inc(cum_ready, 1)
                    ka = prm[:, bass.ds(prm_at["ka"][0] + p, 1)]
                    link(nc.vector.tensor_scalar(oka[:], ka, -1.0, 1.0, MUL, ADD))
                    dve.wait_ge(sig_ready, 4)
                    link(nc.vector.tensor_scalar(kp[:], al[:], ka, oka[:], MUL, ADD))
                    for d in range(2):
                        i = nc.vector.tensor_tensor(kp[:, d, :], kp[:, d, :], kT[:, p, :], MUL)
                    link(i)

                    def ordered(out, fn):
                        fn(out[:, 0, :], lambda ap: ap[:, 0:N], 0)
                        fn(out[:, 1, 0:C], lambda ap: ap[:, 0:C][:, ::-1], 1)
                        return fn(out[:, 1, C:N], lambda ap: ap[:, C:N][:, ::-1], 1)

                    dve.wait_ge(exp_ready, 1)
                    ordered(kt, lambda o, rd, d: nc.vector.tensor_tensor(o, rd(kp[:, d, :]), rd(Pn[:, d, :]), MUL))
                    dve.wait_ge(bb_ready, 1)
                    link(ordered(bt, lambda o, rd, d: nc.vector.tensor_tensor(o, rd(bb[:, d, :]), rd(Pn[:, d, :]), MUL)))
                    dve.wait_ge(exp_ready, 2)
                    dve.wait_ge(vs_ready, 2)
                    nc.vector.tensor_tensor(AR[:, GC:GD, 1, :], tiled(rS[:]), tiled(Pp[:, 0, C:N]), MUL)
                    nc.vector.tensor_tensor(AR[:, GD + GC:G, 1, :], tiled(rS[:][:, ::-1]),
                                            tiled(Pp[:, 1, C:N][:, ::-1]), MUL)
                    nc.vector.tensor_copy(PC[:, 0:ND], chunked(Pp[:, 0, :])[:, :, Q - 1])
                    nc.vector.tensor_copy(PC[:, ND:ND + C // Q], chunked(Pp[:, 1, 0:C][:, ::-1])[:, :, Q - 1])
                    nc.vector.tensor_copy(PC[:, ND + C // Q:NCH], chunked(Pp[:, 1, C:N][:, ::-1])[:, :, Q - 1])
                    link(nc.vector.tensor_tensor(bb[:, 1, 0:T], kp[:, 0, C:N], kp[:, 1, C:N], ADD))
                    link(nc.vector.scalar_tensor_tensor(bb[:, 0, 0:T], bb[:, 1, 0:T],
                                                        prm[:, bass.ds(prm_at["rk"][0] + p, 1)], rT[:, p, :], MUL, MUL))
                    dve.sem_inc(bsum_in, 1)
                    dve.wait_ge(exp_ready, 3)
                    for d, n0, n1, rd in ((0, 0, GD, lambda ap: ap[:, 0:N]),
                                          (1, GD, GD + GC, lambda ap: ap[:, 0:C][:, ::-1]),
                                          (1, GD + GC, G, lambda ap: ap[:, C:N][:, ::-1])):
                        nc.vector.scalar_tensor_tensor(AR[:, n0:n1, 0, :], tiled(rd(kkS[:])), -1.0,
                                                       tiled(rd(Pv[:, d, :])), MUL, MUL)
                    dve.wait_ge(bsum_done, 1)
                    nc.vector.tensor_tensor(vT[:, p, C:N], bank(0), vT[:, p, C:N], MUL)

        with ExitStack() as st:
            att_, btt, ktt, vtt = (sb(st, n, [P, G, P]) for n in ("at_tok", "b_tok", "k_tok", "v_tok"))
            LT, X, XT, W1, MT = (sb(st, n, [P, 2 * G, Q]) for n in ("LT", "X", "XT", "W1", "MT"))
            RBT, RKT = (sb(st, n, [P, 4 * (GD - GC), Q]) for n in ("RBT", "RKT"))
            yS = sb(st, "yS", [P, T])
            Z = sb(st, "Z", [P, 2, ND + 1, Q])
            F, E, GP, U = LT, X, MT, W1
            S = sems(st, "t_done", "t_ready", "pb_done", "pk_done", "l_done", "pb_used", "pk_used", "l_used",
                     "xt0_ready", "x_ready", "w_done", "w_ready", "xx_done", "me_done", "me_ready", "fg_done", "fg_ready",
                     "u_done", "u_ready", "zp_done", "z_ready", "y_done", "dve_chain", "pool_chain")
            (t_done, t_ready, pb_done, pk_done, l_done, pb_used, pk_used, l_used, xt0_ready, x_ready, w_done, w_ready,
             xx_done, me_done, me_ready, fg_done, fg_ready, u_done, u_ready, zp_done, z_ready, y_done, dve_chain,
             pool_chain) = S
            NBT = 3

            def half(i):
                return slice(i * Q, (i + 1) * Q)

            def is_lat(g):
                return g % GD >= GC

            def lat(k):
                return k - 2 * GC * (1 + k // (2 * GD))

            def lat_blocks(b):
                ks = [2 * g + h for g in range(4 * b, 4 * b + 4) for h in range(2) if is_lat(g)]
                return ks[0], ks[-1] + 1

            def units(b):
                return [(g, h, c) for g in range(4 * b, 4 * b + 4) for h in range(2) for c in range(2)]

            def cols(i, b):
                return bank(i).rearrange("p (k j) -> p k j", j=Q)

            def chunk_bank(b, c):
                return bank((2 * b + 1, 6 + b % 2)[c], 0, 4 * Q)

            def of_chunks(t, b):
                return t[:, 8 * b:8 * b + 8, :].rearrange("p (g c) j -> p g c j", c=2)

            def by_head(t, k0, k1):
                return t[:, k0:k1, :].rearrange("p (g h) j -> p h g j", h=2)

            with clear_then_block(S) as block:
                @block.tensor
                def _(pe):
                    for b in range(NBT):
                        if b:
                            pe.wait_ge(l_used, b)
                        for i in range(4):
                            for g in range(4 * b, 4 * b + 4):
                                src = (AR[:, g, 0, :], bt[:, g // GD, (g % GD) * P:(g % GD + 1) * P],
                                       kt[:, g // GD, (g % GD) * P:(g % GD + 1) * P],
                                       vs[:, g // GD, (g % GD) * P:(g % GD + 1) * P])[i]
                                last = nc.tensor.transpose(bank(i, (g - 4 * b) * P, (g - 4 * b + 1) * P), src,
                                                           K("ident"))
                        last.then_inc(t_done, 1)
                        for kk_, (src, tile, done, used) in enumerate(((bt, 2, pb_done, pb_used),
                                                                      (kt, 3, pk_done, pk_used))):
                            if b:
                                pe.wait_ge(used, b)
                            for g, h, c in units(b):
                                at = 512 * h + (g - 4 * b) * P
                                w = 2 if is_lat(g) else 1
                                t0 = (g % GD) * P + c * Q
                                last = nc.tensor.matmul(psum[tile][half(c), at:at + w * Q],
                                                        src[half(h), g // GD, t0:t0 + Q], AR[half(h), g, 0:w, half(c)],
                                                        start=True, stop=True)
                            last.then_inc(done, 1)
                        pe.wait_ge(t_ready, b + 1)
                        for g, h, c in units(b):
                            t0, at = (g % GD) * P + c * Q, (g - 4 * b) * Q
                            last = nc.tensor.matmul(bank(h, at, at + Q)[half(c)], AR[half(h), g, 0, half(c)],
                                                    bt[half(h), g // GD, t0:t0 + Q], start=True, stop=True)
                        last.then_inc(l_done, 1)
                    pe.wait_ge(pb_used, NBT)
                    pe.wait_ge(pk_used, NBT)
                    pe.wait_ge(l_used, NBT)
                    for lv in range(LVL):
                        for b in range(NBT):
                            pe.wait_ge(x_ready, NBT * lv + b + 1)
                            for g, h, c in units(b):
                                k = 2 * g + h
                                last = nc.tensor.matmul(bank(2 * b, (k - 8 * b) * Q, (k - 8 * b + 1) * Q)[half(c)],
                                                        LT[half(c), k, :], X[half(c), k, :], start=True, stop=True)
                            last.then_inc(w_done, 1)
                        for b in range(NBT):
                            pe.wait_ge(w_ready, NBT * lv + b + 1)
                            for i in range(1 if lv == LVL - 1 else 0, 2):
                                for g, h, c in units(b):
                                    k = 2 * g + h
                                    lhs, rhs = ((XT, W1), (W1, XT))[i]
                                    last = nc.tensor.matmul(
                                        bank(2 * b + i, (k - 8 * b) * Q, (k - 8 * b + 1) * Q)[half(c)],
                                        lhs[half(c), k, :], rhs[half(c), k, :], start=True, stop=True)
                            last.then_inc(xx_done, 1)
                    def by_chunk(n, b):
                        at = (n // 2 - 4 * b) * Q
                        return chunk_bank(b, n % 2)[:, at:at + Q]

                    for b in range(NBT):
                        pe.wait_ge(x_ready, NBT * LVL + b + 1)
                        if b == 2:
                            pe.wait_ge(me_ready, 1)
                        for g, h, c in units(b):
                            k = 2 * g + h
                            nc.tensor.matmul(bank(2 * b, (k - 8 * b) * Q, (k - 8 * b + 1) * Q)[half(c)],
                                             MT[half(c), k, :], vtt[half(c), g, h * Q:(h + 1) * Q], start=True,
                                             stop=True)
                        for g, h, c in units(b):
                            k, n = 2 * g + h, 2 * g + c
                            last = nc.tensor.matmul(by_chunk(n, b)[half(h)],
                                                    att_[half(c), g, h * Q:(h + 1) * Q], XT[half(c), k, :],
                                                    start=True, stop=True)
                        last.then_inc(me_done, 1)
                    for b in range(NBT):
                        pe.wait_ge(me_ready, NBT)
                        if b == 2:
                            pe.wait_ge(fg_ready, 1)
                        for g, h, c in units(b):
                            k = 2 * g + h
                            nc.tensor.matmul(bank(2 * b, (k - 8 * b) * Q, (k - 8 * b + 1) * Q)[half(c)],
                                             XT[half(c), k, :], F[half(c), k, :], start=True, stop=True)
                        for g, h, c in units(b):
                            n = 2 * g + c
                            last = nc.tensor.matmul(by_chunk(n, b)[half(h)],
                                                    ktt[half(c), g, h * Q:(h + 1) * Q],
                                                    vtt[half(c), g, h * Q:(h + 1) * Q], start=True, stop=True)
                        last.then_inc(fg_done, 1)
                    pe.wait_ge(fg_ready, NBT)
                    for s in range(ND):
                        pe.wait_ge(z_ready, s + 1)
                        for d in range(2):
                            n = ND * d + s
                            for h in range(2):
                                at = (2 * (s % 2) + d) * Q
                                last = nc.tensor.matmul(bank(6 + h, at, at + Q)[half(n % 2)], E[half(h), n, :],
                                                        Z[half(h), d, s, :], start=True, stop=True)
                        last.then_inc(u_done, 1)
                        pe.wait_ge(u_ready, s + 1)
                        for d in range(2):
                            n = ND * d + s
                            g, c = n // 2, n % 2
                            for h in range(2):
                                last = nc.tensor.matmul(bank(s % 2, d * Q, (d + 1) * Q)[half(h)],
                                                        btt[half(c), g, h * Q:(h + 1) * Q], U[half(c), 2 * g + h, :],
                                                        start=True, stop=True)
                        last.then_inc(zp_done, 1)
                    for d in range(2):
                        for s in range(C // Q, ND):
                            n, at = ND * d + s, (s - C // Q) * Q
                            for h in range(2):
                                nc.tensor.matmul(bank(2 + d, at, at + Q)[half(h)], Z[half(h), d, s, :],
                                                 AR[half(h), n // 2, 1, half(n % 2)], start=True, stop=True)
                        for s in range(C // Q, ND):
                            n = ND * d + s
                            g, c = n // 2, n % 2
                            at = (s - C // Q) // 2 * Q
                            for h in range(2):
                                o = bank(4 + 2 * d + c, at, at + Q)[half(h)]
                                nc.tensor.matmul(o, U[half(c), 2 * g + h, :], RBT[half(c), lat(2 * g + h), :],
                                                 start=True, stop=False)
                                last = nc.tensor.matmul(o, vtt[half(c), g, h * Q:(h + 1) * Q],
                                                        RKT[half(c), lat(2 * g + h), :], start=False, stop=True)
                        last.then_inc(y_done, 1)

                @block.scalar
                def _(act):
                    for b in range(NBT):
                        act.wait_ge(t_done, b + 1)
                        for i, dst in enumerate((att_, btt, ktt, vtt)):
                            j = nc.scalar.activation(dst[:, 4 * b:4 * b + 4, :],
                                                     bank(i).rearrange("p (g c) -> p g c", c=P), ACT.Copy)
                        j.then_inc(t_ready, 1)
                    for b in range(NBT):
                        act.wait_ge(me_done, b + 1)
                        nc.scalar.activation(F[:, 8 * b:8 * b + 8, :], cols(2 * b, b), ACT.Copy)
                        for c in range(2):
                            i = nc.scalar.activation(of_chunks(E, b)[:, :, c, :],
                                                     chunk_bank(b, c).rearrange("p (g j) -> p g j", j=Q), ACT.Copy)
                        i.then_inc(me_ready, 1)

                @block.gpsimd
                def _(pool):
                    for b in range(NBT):
                        k = slice(8 * b, 8 * b + 8)
                        pool.wait_ge(pb_used, b + 1)
                        nc.gpsimd.tensor_tensor(XT[:, k, :], LT[:, k, :],
                                                K("lvl1t").unsqueeze(1).to_broadcast([P, 8, Q]), MUL)\
                            .then_inc(pool_chain, 1)
                        pool.wait_ge(pool_chain, b + 1)
                        nc.gpsimd.tensor_tensor(XT[:, k, :], XT[:, k, :],
                                                K("eye64").unsqueeze(1).to_broadcast([P, 8, Q]), ADD)\
                            .then_inc(xt0_ready, 1)

                @block.vector
                def _(dve):
                    link = Chain(dve, dve_chain)

                    def wide(name, n, lo=0, hi=None):
                        return K(name, lo, hi).unsqueeze(1).to_broadcast([P, n, Q])

                    def wide2(name, n):
                        return K(name).unsqueeze(1).unsqueeze(1).to_broadcast([P, 2, n, Q])

                    nc.vector.memset(Z[:, :, 0, :], 0.0)
                    for b in range(NBT):
                        k0, k1 = lat_blocks(b)
                        for tile, done, used, lt, rt in ((2, pb_done, pb_used, LT, RBT), (3, pk_done, pk_used, MT, RKT)):
                            pp = psum[tile][:, :].rearrange("p (h g j) -> p h g j", h=2, j=P)
                            g0, g1 = k0 // 2 - 4 * b, k1 // 2 - 4 * b
                            dve.wait_ge(done, b + 1)
                            nc.vector.tensor_tensor(by_head(rt, lat(k0), lat(k1 - 1) + 1), pp[:, :, g0:g1, Q:P],
                                                    wide2("upper_eq", g1 - g0), MUL)
                            nc.vector.tensor_tensor(by_head(lt, 8 * b, 8 * b + 8), pp[:, :, :, 0:Q], wide2("upper", 4),
                                                    MUL).then_inc(used, 1)
                        dve.wait_ge(l_done, b + 1)
                        link(nc.vector.tensor_tensor(by_head(X, 8 * b, 8 * b + 8),
                                                     psum[0][:, :].rearrange("p (h w) -> p h w", h=2)[:, :, 0:4 * Q]
                                                     .rearrange("p h (g j) -> p h g j", j=Q), wide2("lvl1", 4), MUL))
                        dve.sem_inc(l_used, 1)
                        dve.wait_ge(xt0_ready, b + 1)
                        nc.vector.tensor_tensor(X[:, 8 * b:8 * b + 8, :], X[:, 8 * b:8 * b + 8, :], wide("eye64", 8),
                                                ADD).then_inc(x_ready, 1)
                    for lv in range(LVL):
                        for b in range(NBT):
                            dve.wait_ge(w_done, NBT * lv + b + 1)
                            nc.vector.tensor_tensor(W1[:, 8 * b:8 * b + 8, :], cols(2 * b, b),
                                                    wide("lvl", 8, lv * Q, (lv + 1) * Q), MUL).then_inc(w_ready, 1)
                        for b in range(NBT):
                            k = slice(8 * b, 8 * b + 8)
                            dve.wait_ge(xx_done, NBT * lv + b + 1)
                            if lv < LVL - 1:
                                nc.vector.tensor_tensor(X[:, k, :], X[:, k, :], cols(2 * b, b), ADD)
                            nc.vector.tensor_tensor(XT[:, k, :], XT[:, k, :], cols(2 * b + 1, b), ADD)\
                                .then_inc(x_ready, 1)
                    for b in range(NBT):
                        k = slice(8 * b, 8 * b + 8)
                        dve.wait_ge(fg_done, b + 1)
                        nc.vector.tensor_copy(F[:, k, :], cols(2 * b, b))
                        for c in range(2):
                            i = nc.vector.tensor_tensor(of_chunks(GP, b)[:, :, c, :],
                                                        chunk_bank(b, c).rearrange("p (g j) -> p g j", j=Q),
                                                        PC[:, k].rearrange("p (g c) -> p g c", c=2)[:, :, c]
                                                        .unsqueeze(2).to_broadcast([P, 4, Q]), MUL)
                        i.then_inc(fg_ready, 1)
                    dve.wait_ge(fg_ready, NBT)
                    dve.sem_inc(z_ready, 1)
                    for s in range(ND):
                        for d in range(2):
                            n = ND * d + s
                            i = nc.vector.scalar_tensor_tensor(Z[:, d, s + 1, :], Z[:, d, s, :], PC[:, n:n + 1],
                                                               GP[:, n, :], MUL, ADD)
                        link(i)
                        dve.wait_ge(u_done, s + 1)
                        c = s % 2
                        uf = [t[half(c), :, :].rearrange("p (d g h) v -> p d g h v", d=2, h=2)[:, :, s // 2, :, :]
                              for t in (U, F)]
                        up_ = psum[3][half(c), :].rearrange("p (h w) -> p h w", h=2)[:, :, 2 * Q * c:2 * Q * c + 2 * Q]
                        nc.vector.tensor_tensor(uf[0], up_.rearrange("p h (d v) -> p d h v", d=2), uf[1], ADD)\
                            .then_inc(u_ready, 1)
                        dve.wait_ge(zp_done, s + 1)
                        for d in range(2):
                            n = ND * d + s
                            i = nc.vector.scalar_tensor_tensor(Z[:, d, s + 1, :], bank(c, d * Q, (d + 1) * Q),
                                                               PC[:, n:n + 1], Z[:, d, s + 1, :], MUL, ADD)
                        i.then_inc(z_ready, 1)
                        dve.wait_ge(z_ready, s + 2)
                    for d in range(2):
                        dve.wait_ge(y_done, d + 1)
                        y = yS[:] if d == 0 else yS[:][:, ::-1]
                        if d == 0:
                            link(nc.vector.tensor_copy(y, bank(2)))
                        else:
                            link(nc.vector.tensor_tensor(y, bank(3), y, ADD))
                        own_ = psum[2 + d][:, :].rearrange("p (c w) -> p c w", c=2)[:, :, 0:4 * Q]\
                            .rearrange("p c (s j) -> p s c j", j=Q)
                        y4 = y.rearrange("p (s c j) -> p s c j", c=2, j=Q)
                        link(nc.vector.tensor_tensor(y4, own_, y4, ADD))
                    nc.vector.tensor_copy(rT[:, p, :], yS[:])
    drw.close()

    out_proj = ExitStack()
    W = [[sb(out_proj, f"wo{i}{s}", [P, KT, 256], F32R) for s in range(2)] for i in range(2)]
    h = [sb(out_proj, f"ho{i}", [P, KT, T], F32R) for i in range(2)]
    with ExitStack() as st:
        g2 = sb(st, "g2", [P, PAIRS * P])
        sq = [sb(st, f"gsq{i}", [P, T]) for i in range(2)]
        rg = [sb(st, f"grs{i}", [P, T]) for i in range(2)]
        S = sems(st, "g2_in", "mean_done", "yc_ready", "gsq_ready", "var_done", "root_ready", "yn_ready", "ys_ready",
                 "gate_done", "o_ready", "hi_made", "dve_chain", "lo_made")
        (g2_in, mean_done, yc_ready, gsq_ready, var_done, root_ready, yn_ready, ys_ready, gate_done, o_ready, hi_made,
         dve_chain, lo_made) = S
        with clear_then_block(S) as block:
            @block.sync
            def _(sp):
                sp.dma_start(g2[:], A["g2"]).then_inc(g2_in, 16)

            @block.tensor
            def _(pe):
                for i in range(PAIRS):
                    nc.tensor.matmul(bank(i), K("onesh"), rT[:, i, :], start=True, stop=True).then_inc(mean_done, 1)
                pe.wait_ge(g2_in, 16)
                for i in range(PAIRS):
                    nc.tensor.matmul(bank(4 + i), g2[:, i * P:(i + 1) * P], gT[:], start=True, stop=True)\
                        .then_inc(gate_done, 1)
                for i in range(PAIRS):
                    pe.wait_ge(gsq_ready, i + 1)
                    nc.tensor.matmul(bank(i), K("onesh"), sq[i % 2][:], start=True, stop=True).then_inc(var_done, 1)

            @block.scalar
            def _(act):
                for i in range(PAIRS):
                    act.wait_ge(yc_ready, i + 1)
                    if i >= 2:
                        act.wait_ge(var_done, i - 1)
                    nc.scalar.activation(sq[i % 2][:], rT[:, i, :], ACT.Square).then_inc(gsq_ready, 1)
                nc.scalar.activation(h[0][:, 0:PAIRS, :], attT, ACT.Copy).then_inc(hi_made, 1)
                for i in range(PAIRS):
                    act.wait_ge(var_done, i + 1)
                    if i >= 2:
                        act.wait_ge(yn_ready, i - 1)
                    nc.scalar.activation(rg[i % 2][:], bank(i), ACT.Sqrt, bias=small[:, 1:2], scale=1.0 / HD)\
                        .then_inc(root_ready, 1)
                for i in range(PAIRS):
                    act.wait_ge(yn_ready, i + 1)
                    nc.scalar.activation(rT[:, i, :], rT[:, i, :], ACT.Identity, scale=R("lnw", i, i + 1),
                                         bias=R("lnb", i, i + 1)).then_inc(ys_ready, 1)
                for i in range(PAIRS):
                    act.wait_ge(o_ready, i + 1)
                    nc.scalar.activation(h[0][:, PAIRS + i, :], rT[:, i, :], ACT.Copy).then_inc(hi_made, 1)

            @block.vector
            def _(dve):
                link = Chain(dve, dve_chain)
                for i in range(PAIRS):
                    dve.wait_ge(mean_done, i + 1)
                    nc.vector.scalar_tensor_tensor(rT[:, i, :], bank(i), -1.0 / HD, rT[:, i, :], MUL, ADD)\
                        .then_inc(yc_ready, 1)
                for i in range(PAIRS):
                    dve.wait_ge(root_ready, i + 1)
                    link(nc.vector.reciprocal(rg[i % 2][:], rg[i % 2][:]))
                    nc.vector.tensor_tensor(rT[:, i, :], rT[:, i, :], rg[i % 2][:], MUL).then_inc(yn_ready, 1)
                for i in range(PAIRS):
                    dve.wait_ge(ys_ready, i + 1)
                    link(nc.vector.tensor_tensor(rT[:, i, :], rT[:, i, :], vT[:, i, C:N], ADD))
                    dve.wait_ge(gate_done, i + 1)
                    nc.vector.tensor_tensor(rT[:, i, :], bank(4 + i), rT[:, i, :], MUL).then_inc(o_ready, 1)

            @block.gpsimd
            def _(pool):
                pool.wait_ge(hi_made, 1)
                nc.gpsimd.tensor_tensor(h[1][:, 0:PAIRS, :], attT, h[0][:, 0:PAIRS, :].bitcast(F32), SUB)
                for i in range(PAIRS):
                    pool.wait_ge(hi_made, i + 2)
                    nc.gpsimd.tensor_tensor(h[1][:, PAIRS + i, :], rT[:, i, :], h[0][:, PAIRS + i, :].bitcast(F32),
                                            SUB).then_inc(lo_made, 1)

    one = ((lambda s, m: 2 * s + m, (0, T)),)

    def dense(n0, nb, evac, W, h):
        with nc.Block() as block:
            @block.sync
            def _(sp):
                with sp.Fori(0, nb // 2) as turn:
                    up = 2 * turn
                    for j in range(2):
                        sp_next(sp, n0 + j, up)

            @block.gpsimd
            def _(pool):
                with pool.Fori(0, nb // 2) as turn:
                    up = 2 * turn
                    for j in range(2):
                        pool_lo(pool, n0 + j, W, up)

            @block.tensor
            def _(pe):
                with pe.Fori(0, nb // 2) as turn:
                    up = 2 * turn
                    for j in range(2):
                        pe_block(pe, n0 + j, W, h, up=up, parts=((one[0]),))

            @block.scalar
            def _(act):
                act_hi(act, n0, W)
                act_hi(act, n0 + 1, W)
                for j in range(nb):
                    n = n0 + j
                    for m in range(2):
                        act.wait_ge(tile_done[n % 2][m], nth(n))
                        nc.scalar.activation(evac(2 * j + m), bank(2 * (n % 2) + m), ACT.Copy)\
                            .then_inc(tile_free[n % 2][m], 1)
                    if j + 2 < nb:
                        act_hi(act, n + 2, W)

    def norms(layer, g_post, gate_tile, g_pre=None, pre_layer=None, pre_tile=None):
        with ExitStack() as st:
            sq = [sb(st, f"nsq{i}", [P, T]) for i in range(2)]
            rst = [sb(st, f"nrst{i}", [P, T]) for i in range(2)]
            hf = [sb(st, f"nhf{i}", [P, T]) for i in range(2)]
            S = sems(st, "sq_ready", "sq_used", "root_ready", "x_ready", "hf_ready", "hs_ready", "hhi_ready", "hf_used",
                     "dve_chain", "out_done")
            sq_ready, sq_used, root_ready, x_ready, hf_ready, hs_ready, hhi_ready, hf_used, dve_chain, out_done = S
            rounds = 2 if g_pre else 1
            with clear_then_block(S) as block:
                @block.scalar
                def _(act):
                    for r in range(rounds):
                        for k in range(KT):
                            i = r * KT + k
                            if r:
                                act.wait_ge(x_ready, k + 1)
                            if i >= 2:
                                act.wait_ge(sq_used, i - 1)
                            nc.scalar.activation(sq[i % 2][:], (yb, x)[r][:, k, :], ACT.Square).then_inc(sq_ready, 1)
                        act.wait_ge(sq_used, (r + 1) * KT)
                        nc.scalar.activation(rst[r][:], bank(6 + r), ACT.Sqrt, bias=small[:, 0:1], scale=1.0 / D)\
                            .then_inc(root_ready, 1)
                    if rounds == 1:
                        for k in range(KT):
                            act.wait_ge(x_ready, k + 1)
                            act.dma_start(A["out"][:, k, :], x[:, k, :]).then_inc(out_done, 16)
                        act.wait_ge(out_done, 16 * KT)
                        return
                    for k in range(KT):
                        act.wait_ge(hf_ready, k + 1)
                        f = hf[k % 2]
                        nc.scalar.activation(f[:], f[:], ACT.Identity, scale=nsc[:, 3, k:k + 1],
                                             bias=mod[:, pre_layer, pre_tile + k, 0:1]).then_inc(hs_ready, 1)
                        act.wait_ge(hs_ready, k + 1)
                        nc.scalar.activation(h[0][:, k], f[:], ACT.Copy).then_inc(hhi_ready, 1)

                @block.tensor
                def _(pe):
                    for i in range(rounds * KT):
                        pe.wait_ge(sq_ready, i + 1)
                        nc.tensor.matmul(bank(6 + i // KT), K("ones"), sq[i % 2][:], start=i % KT == 0,
                                         stop=i % KT == KT - 1).then_inc(sq_used, 1)

                @block.vector
                def _(dve):
                    link = Chain(dve, dve_chain)
                    nc.vector.tensor_tensor(nsc[:, 2, :], mod[:, layer, gate_tile:gate_tile + KT, 0], R(g_post), MUL)
                    if g_pre:
                        nc.vector.scalar_tensor_tensor(nsc[:, 3, :], mod[:, pre_layer, pre_tile + KT:pre_tile + 2 * KT, 0],
                                                       1.0, R(g_pre), ADD, MUL)
                    dve.wait_ge(root_ready, 1)
                    link(nc.vector.reciprocal(rst[0][:], rst[0][:]))
                    for k in range(KT):
                        link(nc.vector.tensor_tensor(yb[:, k, :], yb[:, k, :], rst[0][:], MUL))
                        nc.vector.scalar_tensor_tensor(x[:, k, :], yb[:, k, :], nsc[:, 2, k:k + 1], x[:, k, :], MUL, ADD)\
                            .then_inc(x_ready, 1)
                    if rounds == 1:
                        return
                    dve.wait_ge(root_ready, 2)
                    link(nc.vector.reciprocal(rst[1][:], rst[1][:]))
                    for k in range(KT):
                        if k >= 2:
                            dve.wait_ge(hf_used, k - 1)
                        nc.vector.tensor_tensor(hf[k % 2][:], x[:, k, :], rst[1][:], MUL).then_inc(hf_ready, 1)

                if rounds == 2:
                    @block.gpsimd
                    def _(pool):
                        for k in range(KT):
                            pool.wait_ge(hhi_ready, k + 1)
                            nc.gpsimd.tensor_tensor(h[1][:, k], hf[k % 2][:], h[0][:, k].bitcast(F32), SUB)\
                                .then_inc(hf_used, 1)

    def mlp(n0, last_phase):
        with ExitStack() as st:
            hid = [sb(st, f"hid{i}", [P, KT, T], F32R) for i in range(2)]
            rl = [sb(st, f"rl{i}", [P, T]) for i in range(2)]
            sq = [sb(st, f"rs{i}", [P, T]) for i in range(2)]
            S = sems(st, "sq_ready", "hid_hi", "hid_ready", "dve_chain")
            sq_ready, hid_hi, hid_ready, dve_chain = S
            NB = 32
            with clear_then_block(S) as block:
                @block.sync
                def _(sp):
                    with sp.Fori(0, (NB - 2 * last_phase) // 2) as turn:
                        up = 2 * turn
                        for j in range(2):
                            sp_next(sp, n0 + j, up)

                @block.gpsimd
                def _(pool):
                    with pool.Fori(0, NB // 2) as turn:
                        up = 2 * turn
                        for j in range(2):
                            pool_lo(pool, n0 + j, W, up)

                @block.tensor
                def _(pe):
                    with pe.Fori(0, NB // 8) as turn:
                        up = 8 * turn
                        for j in range(8):
                            pe_block(pe, n0 + j, W, h if j < 4 else hid, up=up, parts=one,
                                     ready=(hid_ready, lambda k: up + k + 1) if j == 4 else None)

                @block.scalar
                def _(act):
                    act_hi(act, n0, W)
                    act_hi(act, n0 + 1, W)

                    def quarter(up, ahead):
                        for j in range(8):
                            n = n0 + j
                            if j < 4:
                                for m in range(2):
                                    t = 2 * j + m
                                    act.wait_ge(tile_done[n % 2][m], nth(n) + up // 2)
                                    nc.scalar.activation(rl[t % 2][:], bank(2 * (n % 2) + m), ACT.Relu)\
                                        .then_inc(tile_free[n % 2][m], 1)
                                    act.wait_ge(sq_ready, up + t + 1)
                                    nc.scalar.activation(hid[0][:, t], sq[t % 2][:], ACT.Copy).then_inc(hid_hi, 1)
                            if j < 6 or ahead:
                                act_hi(act, n + 2, W, up)

                    with act.Fori(0, (NB - 8) // 8) as turn:
                        up = 8 * turn
                        quarter(up, True)
                    quarter(NB - 8, False)

                @block.vector
                def _(dve):
                    link = Chain(dve, dve_chain)
                    link(nc.vector.memset(yb[:], 0.0))
                    with dve.Fori(0, NB // 8) as turn:
                        up = 8 * turn
                        for j in range(8):
                            n = n0 + j
                            for m in range(2):
                                if j < 4:
                                    t = 2 * j + m
                                    dve.wait_ge(tile_free[n % 2][m], nth(n) + up // 2)
                                    nc.vector.tensor_tensor(sq[t % 2][:], rl[t % 2][:], rl[t % 2][:], MUL)\
                                        .then_inc(sq_ready, 1)
                                    dve.wait_ge(hid_hi, up + t + 1)
                                    nc.vector.tensor_tensor(hid[1][:, t], sq[t % 2][:], hid[0][:, t].bitcast(F32), SUB)\
                                        .then_inc(hid_ready, 1)
                                else:
                                    c = 2 * (j - 4) + m
                                    dve.wait_ge(tile_done[n % 2][m], nth(n) + up // 2)
                                    nc.vector.tensor_tensor(yb[:, c, :], bank(2 * (n % 2) + m), yb[:, c, :], ADD)\
                                        .then_inc(tile_free[n % 2][m], 1)

    dense(S_OUT, 4, lambda t: yb[:, t, :], W, h)
    out_proj.close()
    mix.close()
    tail = ExitStack()
    W = [[sb(tail, f"v{i}{s}", [P, KT, 256], F32R) for s in range(2)] for i in range(2)]
    h = [sb(tail, f"hm{i}", [P, KT, T], F32R) for i in range(2)]
    norms(0, "g01", 16, "g02", 0, 24)
    mlp(S_MLP0, False)
    norms(0, "g03", 40, "g10", 1, 0)

    with ExitStack() as st:
        gates = sb(st, "gates", [P, 2 * KT, T])
        u = sb(st, "u", [P, KT, T + 2])
        cv = [sb(st, f"cv{i}", [P, T]) for i in range(2)]
        S = sems(st, "u_ready", "c1_ready", "cv_ready", "chi_ready", "cv_used", "dve_chain")
        u_ready, c1_ready, cv_ready, chi_ready, cv_used, dve_chain = S
        dense(S_CIN, 12, lambda t: gates[:, t, :] if t < 2 * KT else u[:, t - 2 * KT, 1:T + 1], W, h)
        with clear_then_block(S) as block:
            @block.vector
            def _(dve):
                link = Chain(dve, dve_chain)
                nc.vector.memset(u[:, :, 0], 0.0)
                link(nc.vector.memset(u[:, :, T + 1], 0.0))
                for k in range(KT):
                    link(nc.vector.tensor_tensor(u[:, k, 1:T + 1], u[:, k, 1:T + 1], gates[:, KT + k, :], MUL))
                    dve.sem_inc(u_ready, 1)
                    dve.wait_ge(c1_ready, k + 1)
                    c = cv[k % 2]
                    for tap, o in ((0, 0), (2, 2)):
                        link(nc.vector.scalar_tensor_tensor(c[:], u[:, k, o:o + T],
                                                            R("cw", tap * KT + k, tap * KT + k + 1), c[:], MUL, ADD))
                    nc.vector.tensor_tensor(c[:], c[:], gates[:, k, :], MUL).then_inc(cv_ready, 1)

            @block.scalar
            def _(act):
                for k in range(KT):
                    act.wait_ge(u_ready, k + 1)
                    if k >= 2:
                        act.wait_ge(cv_used, k - 1)
                    nc.scalar.activation(cv[k % 2][:], u[:, k, 1:T + 1], ACT.Copy,
                                         scale=R("cw", KT + k, KT + k + 1)).then_inc(c1_ready, 1)
                    act.wait_ge(cv_ready, k + 1)
                    nc.scalar.activation(h[0][:, k], cv[k % 2][:], ACT.Copy).then_inc(chi_ready, 1)

            @block.gpsimd
            def _(pool):
                for k in range(KT):
                    pool.wait_ge(chi_ready, k + 1)
                    nc.gpsimd.tensor_tensor(h[1][:, k], cv[k % 2][:], h[0][:, k].bitcast(F32), SUB)\
                        .then_inc(cv_used, 1)
        dense(S_COUT, 4, lambda t: yb[:, t, :], W, h)
    norms(1, "g11", 16, "g12", 1, 24)
    mlp(S_MLP1, True)
    norms(1, "g13", 40)
    tail.close()
    top.close()


def kernel(**inputs):
    import numpy as np
    import concourse.bacc as bacc
    from concourse import mybir
    from concourse.bass_utils import run_bass_kernel_spmd

    v = {k: np.asarray(a) for k, a in inputs.items()}
    T, C, D = v["x"].shape[1], v["ctx"].shape[1], v["x"].shape[2]
    KT = D // 128

    def columns(a):
        return np.ascontiguousarray(a.reshape(-1, 128).T)

    def blocks(w):
        k, m = w.shape
        if m % 256:
            w = np.concatenate([w, np.zeros((k, 256 - m % 256), w.dtype)], axis=1)
            m = w.shape[1]
        return w.reshape(k // 128, 128, m // 256, 256).transpose(2, 1, 0, 3).reshape(m // 256, 128, k * 2)

    def mlp(i):
        w1 = blocks(v["mlp_w1"][i])
        out = []
        for q in range(4):
            out += [w1[4 * q:4 * q + 4], blocks(v["mlp_w2"][i][q * D:(q + 1) * D])]
        return out

    stream = [blocks(v["mod_w"][0][:, :2 * D]), blocks(v["ab_w_in"][0]), blocks(v["mod_w"][0][:, 2 * D:]),
              blocks(v["mod_w"][1]), blocks(v["ab_w_out"][0])] + mlp(0) + \
             [blocks(v["conv_w_in"][0]), blocks(v["conv_w_out"][0])] + mlp(1)
    f = np.float32
    g = v["norm_g"]
    parts = dict(modb0=columns(v["mod_b"][0]), modb1=columns(v["mod_b"][1]), mu=columns(v["rwkv_mu"][0]),
                 w0=columns(v["rwkv_w0"][0]), a0=columns(v["rwkv_a0"][0]), kk=columns(v["rwkv_kk"][0]),
                 ka=columns(v["rwkv_ka"][0]), rk=columns(v["rwkv_rk"][0]), lnw=columns(v["rwkv_ln_w"][0]),
                 lnb=columns(v["rwkv_ln_b"][0]), cw=columns(v["conv_w"][0]),
                 sink=np.broadcast_to(v["att_sink"][0][None, :], (128, 8)),
                 c=np.stack([v["c"][0], v["c_ctx"]], -1).reshape(KT, 128, 2).transpose(1, 0, 2).reshape(128, 2 * KT))
    for i in range(2):
        for j in range(4):
            parts[f"g{i}{j}"] = columns(g[i, j])
    at, n = _columns(_PRM)
    prm = np.concatenate([parts[name].reshape(128, -1) for name, _ in _PRM], axis=1)
    assert prm.shape == (128, n)
    lw = np.stack([v["rwkv_w2"][0], v["rwkv_a2"][0]], 0).reshape(2, 128, 4, 128).transpose(2, 1, 0, 3)
    xT = v["x"][0].T.reshape(KT, 128, T).transpose(1, 0, 2)
    cT = v["ctx"][0].T.reshape(KT, 128, C).transpose(1, 0, 2)
    arrays = {"w": np.concatenate(stream), "prm": prm, "cst": _constants(np, T, C, _CST), "csa": _constants(np, T, C, _CSA),
              "x": xT, "ctx": cT,
              "lw": lw, "g2": v["rwkv_g2"][0]}
    arrays = {k: np.ascontiguousarray(a) for k, a in arrays.items()}
    nc = bacc.Bacc("TRN2", target_bir_lowering=False, num_devices=1)
    A = {k: nc.dram_tensor(k + "_in", a.shape, mybir.dt.from_np(a.dtype), kind="ExternalInput").ap()
         for k, a in arrays.items()}
    A["out"] = nc.dram_tensor("out_T", (128, KT, T), mybir.dt.float32, kind="ExternalOutput").ap()
    build(nc, A)
    r = run_bass_kernel_spmd(nc, [{k + "_in": a for k, a in arrays.items()}], core_ids=[0])
    o = r.results[0]["out_T"]
    return np.ascontiguousarray(o.transpose(1, 0, 2).reshape(D, T).T)[None]
```

```python
_PRM = [("modb0", 48), ("modb1", 48), ("g00", 8), ("g01", 8), ("g02", 8), ("g03", 8), ("g10", 8), ("g11", 8),
        ("g12", 8), ("g13", 8), ("mu", 15), ("w0", 8), ("a0", 8), ("kk", 4), ("ka", 4), ("rk", 4), ("lnw", 4),
        ("lnb", 4), ("cw", 24), ("sink", 8), ("c", 16)]
_CST = [("ident", 128), ("ones", 128), ("onesh", 128), ("scan", 768), ("upper", 64), ("upper_eq", 64), ("lower", 64),
        ("lvl1", 64), ("lvl1t", 64), ("eye64", 64), ("lvl", 5 * 64)]
_CSA = [("rot", 128), ("sel", 512), ("cos", 512), ("sin", 512), ("band_lo", 128), ("band_hi", 128)]


def _columns(table):
    at, out = 0, {}
    for name, n in table:
        out[name] = (at, n)
        at += n
    return out, at

def _constants(np, T, C, table):
    f = np.float32
    r, c = np.arange(128)[:, None], np.arange(128)[None, :]
    out = {"ident": r == c, "ones": np.ones((128, 128)), "onesh": r // 64 == c // 64}
    rot = np.where((c % 32 < 16) & (r == c + 16), -1.0, 0.0) + np.where((c % 32 >= 16) & (r == c - 16), 1.0, 0.0)
    out["rot"] = rot
    sel = []
    for kv in range(2):
        s = (r == kv * 64 + c % 64).astype(f)
        sel += [s, rot @ s]
    out["sel"] = np.concatenate(sel, 1)
    m = 16
    inv = (10000.0 ** (-np.arange(m, dtype=f) / m)).astype(f)
    t = np.arange(T)
    ch = np.arange(128)
    pos = np.where((ch % 64 < 32)[:, None], (t // 64)[None, :], (t % 64)[None, :]).astype(f)
    ang = (pos * inv[ch % 16][:, None]).astype(f)
    out["cos"], out["sin"] = np.cos(ang), np.sin(ang)
    out["band_lo"] = np.where(c >= r, 0.0, -1e30)
    out["band_hi"] = np.where(c <= r, 0.0, -1e30)
    out["scan"] = np.broadcast_to((np.arange(T + C) % 64 != 0)[None, :], (128, T + C))
    i, j = np.arange(128)[:, None] % 64, np.arange(64)[None, :]
    out["upper"], out["upper_eq"], out["lower"] = i < j, i <= j, i > j
    l1 = (i // 2 == j // 2) & (i > j)
    out["lvl1"], out["lvl1t"], out["eye64"] = l1, (i // 2 == j // 2) & (i < j), i == j
    out["lvl"] = np.concatenate([(i // (2 * n) == j // (2 * n)) & (i // n > j // n) for n in (2, 4, 8, 16, 32)], 1)
    return np.concatenate([np.asarray(out[name]).astype(f) for name, _ in table], axis=1)


def build(nc, A):
    from contextlib import ExitStack
    import concourse.bass as bass
    from concourse import mybir

    F32, F32R = mybir.dt.float32, mybir.dt.float32r
    ALU, ACT, AX = mybir.AluOpType, mybir.ActivationFunctionType, mybir.AxisListType
    MUL, ADD, SUB, MAX, MIN = ALU.mult, ALU.add, ALU.subtract, ALU.max, ALU.min

    P = 128
    T = A["x"].shape[2]
    C = A["ctx"].shape[2]
    KT = A["x"].shape[1]
    N = C + T
    D = KT * P
    EPS, GN_EPS = 1e-6, 64e-5
    DECAY = 0.6065306597126334
    HD = 64
    PAIRS = 4
    Q = 64
    G = 2 * N // P
    GD = N // P
    GC = C // P
    NBLK = A["w"].shape[0]
    S_MOD0A, S_IN, S_MOD, S_OUT, S_MLP0, S_CIN, S_COUT, S_MLP1 = 0, 8, 19, 59, 63, 95, 107, 111
    assert NBLK == S_MLP1 + 32

    prm_at, NPRM = _columns(_PRM)
    cst_at, NCST = _columns(_CST)
    csa_at, NCSA = _columns(_CSA)
    top = ExitStack()

    taken = {}

    def own(name):
        taken[name] = taken.get(name, 0) + 1
        return name if taken[name] == 1 else f"{name}_{taken[name]}"

    def sb(stack, name, shape, dt=F32):
        return stack.enter_context(nc.sbuf_tensor(own(name), shape, dt))

    def sems(stack, *names):
        return [stack.enter_context(nc.semaphore(own(n))) for n in names]

    class Chain:

        def __init__(self, eng, sem):
            self.eng, self.sem, self.n = eng, sem, 0

        def __call__(self, ins):
            self.n += 1
            ins.then_inc(self.sem, 1)
            self.eng.wait_ge(self.sem, self.n)

    cst = sb(top, "cst", [P, NCST])
    prm = sb(top, "prm", [P, NPRM])
    x = sb(top, "xres", [P, KT, T])
    yb = sb(top, "yb", [P, KT, T])
    raw = [sb(top, f"raw{s}", [P, KT, 256]) for s in range(2)]
    mod0 = sb(top, "mod0", [P, 16, 2])
    mod = sb(top, "mod", [P, 96])
    cs = sb(top, "cs", [P, KT, 2])
    nsc = sb(top, "nsc", [P, 4, KT])
    small = sb(top, "small", [P, 64])
    psum = [top.enter_context(nc.psum_tensor(f"bank{i}", [P, 1024], F32)) for i in range(4)]

    def bank(i, lo=0, hi=512):
        return psum[i // 2][:, (i % 2) * 512 + lo:(i % 2) * 512 + hi]

    def K(name, lo=0, hi=None):
        a, n = cst_at[name]
        return cst[:, a + lo:a + (n if hi is None else hi)]

    def KA(name):
        a, n = csa_at[name]
        return csa[:, a:a + n]

    def R(name, lo=0, hi=None):
        a, n = prm_at[name]
        return prm[:, a + lo:a + (n if hi is None else hi)]

    raw_loaded = sems(top, "raw_loaded0", "raw_loaded1")
    hi_ready = sems(top, "hi_ready0", "hi_ready1")
    split_ready = sems(top, "split_ready0", "split_ready1")
    mod_used = sems(top, "mod_used0", "mod_used1")
    tile_done = [sems(top, f"tile_done{s}0", f"tile_done{s}1") for s in range(2)]
    tile_free = [sems(top, f"tile_free{s}0", f"tile_free{s}1") for s in range(2)]

    def is_mod(n):
        return n < S_IN or S_MOD <= n < S_OUT

    def nth(n):
        return sum(is_mod(m) == is_mod(n) for m in range(n % 2, n + 1, 2))

    def clear(stack_sems):
        with nc.Block() as block:
            @block.gpsimd
            def _(pool):
                for s in stack_sems:
                    pool.sem_clear(s)

    def keep_warm(n, out, width=512):
        for _ in range(n):
            nc.tensor.matmul(out[:, 0:width], K("ones"), cst[:, 0:width], start=True, stop=True)

    def sp_load(sp, n, up=0):
        sp.dma_start(raw[n % 2][:].rearrange("p k m -> p (k m)"), A["w"][n + up]).then_inc(raw_loaded[n % 2], 16)

    def sp_next(sp, n, up=0):
        if is_mod(n):
            sp.wait_ge(mod_used[n % 2], nth(n) + up // 2)
        else:
            sp.wait_ge(split_ready[n % 2], nth(n) + up // 2)
        sp_load(sp, n + 2, up)

    def act_hi(act, n, W, up=0):
        act.wait_ge(raw_loaded[n % 2], 16 * (n // 2 + 1) + 8 * up)
        if nth(n) > 1:
            act.wait_ge(tile_done[n % 2][1], nth(n) - 1 + up // 2)
        nc.scalar.activation(W[0][n % 2][:], raw[n % 2][:], ACT.Copy).then_inc(hi_ready[n % 2], 1)

    def pool_lo(pool, n, W, up=0):
        pool.wait_ge(hi_ready[n % 2], nth(n) + up // 2)
        nc.gpsimd.tensor_tensor(W[1][n % 2][:], raw[n % 2][:], W[0][n % 2][:].bitcast(F32), SUB)\
            .then_inc(split_ready[n % 2], 1)

    def pe_block(pe, n, W, H, up=0, tiles=2, parts=((0, None),), ready=None, start_k=0):
        s = n % 2
        pe.wait_ge(split_ready[s], nth(n) + up // 2)
        for m in range(tiles):
            if nth(n) > 1:
                pe.wait_ge(tile_free[s][m], nth(n) - 1 + up // 2)
            for k in range(KT):
                if ready is not None and m == 0:
                    pe.wait_ge(ready[0], ready[1](k))
                for w, h in ((0, 0), (0, 1), (1, 0)):
                    for b, (lo, hi) in parts:
                        last = nc.tensor.matmul(bank(b(s, m), 0, hi - lo), W[w][s][:, k, m * P:(m + 1) * P],
                                                H[h][:, k, lo:hi], start=(k == 0 and w == h == 0),
                                                stop=(k == KT - 1 and w == 1))
            last.then_inc(tile_done[s][m], 1)

    def clear_then_block(stack_sems):
        clear(stack_sems)
        return nc.Block()

    mix = ExitStack()
    qT, rT = yb[:, 0:PAIRS, :], yb[:, PAIRS:KT, :]
    attT = qT
    kT = sb(mix, "kT", [P, PAIRS, N])
    vT = sb(mix, "vT", [P, PAIRS, N])
    lora = sb(mix, "lora", [P, 2, N])
    gT = sb(mix, "gT", [P, T])
    kkT = sb(mix, "kkT", [P, PAIRS, N])
    att_in = ExitStack()
    csa = sb(att_in, "csa", [P, NCSA])
    kvT = sb(att_in, "kvT", [P, 2, N])
    proj = ExitStack()
    hT = [sb(proj, f"h{i}", [P, KT, N], F32R) for i in range(2)]
    W = [[sb(proj, f"w{i}{s}", [P, KT, 256], F32R) for s in range(2)] for i in range(2)]
    with ExitStack() as st:
        ctxT = kkT[:].rearrange("p a n -> p (a n)")[:, 0:KT * C].rearrange("p (k c) -> p k c", c=C)
        sq, rst = [kT[:, i, :] for i in range(2)], kT[:, 2, :]
        hf = [vT[:, i, :] for i in range(2)]
        S = sems(st, "const_in", "x_in", "csig", "cs_ready", "mod_done", "mod_ready", "sq_ready", "sq_used",
                 "ssum_done", "root_ready", "rst_ready", "hf_ready", "hs_ready", "hhi_ready", "hf_used", "dve_chain",
                 "csa_in")
        (const_in, x_in, csig, cs_ready, mod_done, mod_ready, sq_ready, sq_used, ssum_done, root_ready,
         rst_ready, hf_ready, hs_ready, hhi_ready, hf_used, dve_chain, csa_in) = S
        with nc.Block() as block:
            @block.sync
            def _(sp):
                sp.dma_start(prm[:], A["prm"]).then_inc(const_in, 16)
                sp_load(sp, 0)
                sp_load(sp, 1)
                with sp.Fori(0, S_IN // 2) as turn:
                    n = 2 * turn
                    for s in range(2):
                        sp_next(sp, s, n)
                sp.wait_ge(csa_in, 16)

            @block.scalar
            def _(act):
                act.dma_start(x[:], A["x"]).then_inc(x_in, 16)
                act.dma_start(ctxT, A["ctx"]).then_inc(x_in, 16)
                act.dma_start(cst[:], A["cst"]).then_inc(x_in, 16)
                act.dma_start(csa[:], A["csa"]).then_inc(csa_in, 16)
                act.wait_ge(const_in, 16)
                nc.scalar.activation(cs[:].rearrange("p k c -> p (k c)"), R("c"), ACT.Sigmoid).then_inc(csig, 1)
                act.wait_ge(x_in, 48)
                for k in range(KT):
                    if k >= 2:
                        act.wait_ge(sq_used, k - 1)
                    nc.scalar.activation(sq[k % 2][:, 0:C], ctxT[:, k], ACT.Square)
                    nc.scalar.activation(sq[k % 2][:, C:N], x[:, k], ACT.Square).then_inc(sq_ready, 1)
                act.wait_ge(ssum_done, 1)
                act.wait_ge(mod_ready, 1)
                nc.scalar.activation(rst[:, 0:C], bank(3, 0, C), ACT.Sqrt, bias=small[:, 0:1], scale=1.0 / D)
                nc.scalar.activation(rst[:, C:N], bank(2), ACT.Sqrt, bias=small[:, 0:1], scale=1.0 / D)\
                    .then_inc(root_ready, 1)
                act.wait_ge(mod_ready, 2)
                for k in range(KT):
                    act.wait_ge(hf_ready, k + 1)
                    f = hf[k % 2]
                    nc.scalar.activation(f[:, 0:C], f[:, 0:C], ACT.Identity, scale=nsc[:, 1, k:k + 1],
                                         bias=mod0[:, k, 1:2])
                    nc.scalar.activation(f[:, C:N], f[:, C:N], ACT.Identity, scale=nsc[:, 0, k:k + 1],
                                         bias=mod0[:, k, 0:1]).then_inc(hs_ready, 1)
                    act.wait_ge(hs_ready, k + 1)
                    nc.scalar.activation(hT[0][:, k], f, ACT.Copy).then_inc(hhi_ready, 1)

            @block.tensor
            def _(pe):
                pe.wait_ge(x_in, 48)
                for k in range(KT):
                    pe.wait_ge(sq_ready, k + 1)
                    nc.tensor.matmul(bank(2), K("ones"), sq[k % 2][:, C:N], start=k == 0, stop=k == KT - 1)
                    nc.tensor.matmul(bank(3, 0, C), K("ones"), sq[k % 2][:, 0:C], start=k == 0, stop=k == KT - 1)\
                        .then_inc(sq_used if k < KT - 1 else ssum_done, 1)
                pe.wait_ge(cs_ready, 1)
                for n in range(S_IN):
                    pe.wait_ge(raw_loaded[n % 2], 16 * (n // 2 + 1))
                    for m in range(2):
                        for k in range(KT):
                            last = nc.tensor.matmul(bank(0, 4 * n + 2 * m, 4 * n + 2 * m + 2),
                                                    raw[n % 2][:, k, m * P:(m + 1) * P], cs[:, k, :],
                                                    start=k == 0, stop=k == KT - 1)
                    last.then_inc(mod_used[n % 2], 1)

            @block.vector
            def _(dve):
                link = Chain(dve, dve_chain)
                nc.vector.memset(small[:, 0:1], EPS)
                nc.vector.memset(small[:, 1:2], GN_EPS).then_inc(mod_ready, 1)
                dve.wait_ge(csig, 1)
                link(nc.vector.tensor_tensor(cs[:].rearrange("p k c -> p (k c)"), cs[:].rearrange("p k c -> p (k c)"),
                                             R("c"), MUL))
                dve.sem_inc(cs_ready, 1)
                for s in range(2):
                    dve.wait_ge(mod_used[s], S_IN // 2)
                link(nc.vector.tensor_tensor(mod0[:], bank(0, 0, 32).rearrange("p (m c) -> p m c", c=2),
                                             R("modb0", 0, 16).unsqueeze(2).to_broadcast([P, 16, 2]), ADD))
                for c in range(2):
                    i = nc.vector.scalar_tensor_tensor(nsc[:, c, :], mod0[:, 8:16, c], 1.0, R("g00"), ADD, MUL)
                i.then_inc(mod_ready, 1)
                dve.wait_ge(root_ready, 1)
                link(nc.vector.reciprocal(rst, rst))
                for k in range(KT):
                    if k >= 2:
                        dve.wait_ge(hf_used, k - 1)
                    nc.vector.tensor_tensor(hf[k % 2][:, 0:C], ctxT[:, k], rst[:, 0:C], MUL)
                    nc.vector.tensor_tensor(hf[k % 2][:, C:N], x[:, k], rst[:, C:N], MUL).then_inc(hf_ready, 1)

            @block.gpsimd
            def _(pool):
                for k in range(KT):
                    pool.wait_ge(hhi_ready, k + 1)
                    nc.gpsimd.tensor_tensor(hT[1][:, k], hf[k % 2], hT[0][:, k].bitcast(F32), SUB)\
                        .then_inc(hf_used, 1)

    with ExitStack() as st:
        pad = [sb(st, f"pad{i}", [P, N + 4]) for i in range(2)]
        nb = [sb(st, f"nb{i}", [P, N + 2]) for i in range(2)]
        mus = sb(st, "mus", [P, 2, 15])
        S = sems(st, "mus_ready", "pad_ready", "pad_used", "base_ready", "mixed", "dve_chain")
        mus_ready, pad_ready, pad_used, base_ready, mixed, dve_chain = S
        dest = [(qT[:, i, :], C) for i in range(4)] + [(kvT[:, i, :], 0) for i in range(2)] \
            + [(rT[:, i, :], C) for i in range(4)] + [(kT[:, i, :], 0) for i in range(4)] \
            + [(vT[:, i, :], 0) for i in range(4)] + [(lora[:, i, :], 0) for i in range(2)] + [(gT[:], C)]
        NB = S_MOD - S_IN

        def acc(n, m, lo, hi):
            t = psum[2 * (n % 2) + m]
            return t[:, 512 + lo:512 + hi] if lo < C else t[:, lo - C:hi - C]

        with clear_then_block(S) as block:
            @block.sync
            def _(sp):
                sp_next(sp, S_IN)
                with sp.Fori(0, (NB - 1) // 2) as turn:
                    up = 2 * turn
                    for j in range(2):
                        sp_next(sp, S_IN + 1 + j, up)

            @block.tensor
            def _(pe):
                b = lambda s, m: 2 * (2 * s + m)
                bc = lambda s, m: 2 * (2 * s + m) + 1
                both = ((b, (C, N)), (bc, (0, C)))
                for n in range(S_IN, S_IN + 2):
                    pe_block(pe, n, W, hT, parts=both[:1])
                with pe.Fori(0, (NB - 3) // 2) as turn:
                    up = 2 * turn
                    for j in range(2):
                        pe_block(pe, S_IN + 2 + j, W, hT, up=up, parts=both)
                pe_block(pe, S_MOD - 1, W, hT, tiles=1, parts=both[:1])
                pe.sem_inc(tile_done[(S_MOD - 1) % 2][1], 1)

            @block.gpsimd
            def _(pool):
                pool_lo(pool, S_IN, W)
                with pool.Fori(0, (NB - 1) // 2) as turn:
                    up = 2 * turn
                    for j in range(2):
                        pool_lo(pool, S_IN + 1 + j, W, up)

            @block.scalar
            def _(act):
                act_hi(act, S_IN, W)
                act_hi(act, S_IN + 1, W)
                for n in range(S_IN, S_MOD):
                    for m in range(2):
                        t = 2 * (n - S_IN) + m
                        if t > 20:
                            act.sem_inc(tile_free[n % 2][1], 1)
                            continue
                        act.wait_ge(tile_done[n % 2][m], nth(n))
                        d, first = dest[t]
                        segs = ((0, C), (C, N))[first > 0:]
                        if t < 6:
                            for lo, hi in segs:
                                i = nc.scalar.activation(d[:, lo - first:hi - first], acc(n, m, lo, hi), ACT.Copy)
                        else:
                            j = t - 6
                            if j == 0:
                                act.wait_ge(mus_ready, 1)
                            if j >= 2:
                                act.wait_ge(pad_used, j - 1)
                            for lo, hi in segs:
                                o = 1 + 2 * (lo > 0)
                                i = nc.scalar.activation(pad[j % 2][:, o + lo:o + hi], acc(n, m, lo, hi), ACT.Copy)
                            i.then_inc(pad_ready, 1)
                            for lo, hi in segs:
                                i = nc.scalar.activation(d[:, lo - first:hi - first], acc(n, m, lo, hi), ACT.Copy,
                                                         scale=mus[:, 0, j:j + 1])
                        i.then_inc(tile_free[n % 2][m], 1)
                    if n + 2 < S_MOD:
                        act_hi(act, n + 2, W)
                act.wait_ge(mixed, 15)
                nc.scalar.activation(lora[:, 0, :], lora[:, 0, :], ACT.Tanh)
                nc.scalar.activation(gT[:], gT[:], ACT.Sigmoid)

            @block.vector
            def _(dve):
                link = Chain(dve, dve_chain)
                for i in range(2):
                    nc.vector.memset(pad[i][:], 0.0)
                nc.vector.tensor_scalar(mus[:, 1, :], R("mu"), 0.5, None, MUL)
                link(nc.vector.tensor_scalar(mus[:, 0, :], R("mu"), -1.0, 1.0, MUL, ADD))
                dve.sem_inc(mus_ready, 1)
                for j in range(15):
                    n, m = S_IN + (j + 6) // 2, j % 2
                    d, first = dest[j + 6]
                    segs = ((0, C), (C, N))[first > 0:]
                    dve.wait_ge(pad_ready, j + 1)
                    a = segs[0][0] + (2 if first else 0)
                    link(nc.vector.tensor_tensor(nb[j % 2][:, a:N + 2], pad[j % 2][:, a:N + 2],
                                                 pad[j % 2][:, a + 2:N + 4], ADD))
                    dve.sem_inc(pad_used, 1)
                    dve.wait_ge(tile_free[n % 2][m], nth(n))
                    for lo, hi in segs:
                        o = 2 * (lo > 0)
                        i = nc.vector.scalar_tensor_tensor(d[:, lo - first:hi - first], nb[j % 2][:, o + lo:o + hi],
                                                           mus[:, 1, j:j + 1], d[:, lo - first:hi - first], MUL, ADD)
                    i.then_inc(mixed, 1)
    proj.close()

    vtok = sb(att_in, "vtok", [P, GD, P])
    with ExitStack() as st:
        sq = [sb(st, f"ksq{i}", [P, N]) for i in range(2)]
        nrm = sb(st, "knorm", [P, PAIRS, N])
        S = sems(st, "ksq_ready", "knorm_sum", "knorm_used", "knorm_ready", "vt_done", "dve_chain")
        ksq_ready, knorm_sum, knorm_used, knorm_ready, vt_done, dve_chain = S
        with clear_then_block(S) as block:
            @block.tensor
            def _(pe):
                for g in range(GD):
                    last = nc.tensor.transpose(psum[3][:, g * P:(g + 1) * P], kvT[:, 1, g * P:(g + 1) * P], K("ident"))
                last.then_inc(vt_done, 1)
                for p in range(PAIRS):
                    pe.wait_ge(ksq_ready, p + 1)
                    if p >= 2:
                        pe.wait_ge(knorm_used, p - 1)
                    for lo, hi in ((0, 512), (512, N)):
                        last = nc.tensor.matmul(psum[1 + p % 2][:, lo:hi], K("onesh"), sq[p % 2][:, lo:hi],
                                                start=True, stop=True)
                    last.then_inc(knorm_sum, 1)

            @block.scalar
            def _(act):
                for p in range(PAIRS):
                    act.wait_ge(knorm_sum, p + 1)
                    nc.scalar.activation(nrm[:, p, :], psum[1 + p % 2][:, 0:N], ACT.Sqrt).then_inc(knorm_used, 1)
                act.wait_ge(vt_done, 1)
                nc.scalar.activation(vtok[:].rearrange("p g c -> p (g c)"), psum[3][:, 0:N], ACT.Copy)

            @block.vector
            def _(dve):
                link = Chain(dve, dve_chain)
                for p in range(PAIRS):
                    if p >= 2:
                        dve.wait_ge(knorm_sum, p - 1)
                    nc.vector.tensor_scalar(kkT[:, p, :], kT[:, p, :], R("kk", p, p + 1), None, MUL)
                    link(nc.vector.tensor_scalar(sq[p % 2][:], kT[:, p, :], R("kk", p, p + 1), None, MUL))
                    nc.vector.tensor_tensor(sq[p % 2][:], sq[p % 2][:], sq[p % 2][:], MUL).then_inc(ksq_ready, 1)
                for p in range(PAIRS):
                    dve.wait_ge(knorm_used, p + 1)
                    link(nc.vector.tensor_scalar(nrm[:, p, :], nrm[:, p, :], 1e-12, None, MAX))
                    link(nc.vector.reciprocal(nrm[:, p, :], nrm[:, p, :]))
                    link(nc.vector.tensor_tensor(kkT[:, p, :], kkT[:, p, :], nrm[:, p, :], MUL))

    NQ = T // P
    with ExitStack() as st:
        selS = sb(st, "selS", [P, 2, P])
        kd = sb(st, "kd", [P, N])
        vS = sb(st, "vS", [P, GD, HD])
        qs = [sb(st, f"qs{i}", [P, T]) for i in range(2)]
        tmp = [sb(st, f"rot{i}", [P, T]) for i in range(2)]
        pr = [sb(st, f"prob{i}", [P, 5 * P]) for i in range(2)]
        pt = [sb(st, f"probT{i}", [P, 5 * P]) for i in range(2)]
        oS = sb(st, "oS", [P, 2, NQ, P])
        mx, nmx, rs, es, den = (sb(st, n, [P, 4]) for n in ("mx", "nmx", "rs", "es", "den"))
        sinks = sb(st, "sinks", [P, 2, 4])
        S = sems(st, "sel_ready", "kd_done", "q_done", "kd_ready", "q_ready", "vs_ready", "s_done", "banded",
                 "max_ready", "exp_ready", "pt_done", "pt_ready", "o_done", "o_ready", "ot_done", "dve_chain")
        (sel_ready, kd_done, q_done, kd_ready, q_ready, vs_ready, s_done, banded, max_ready, exp_ready, pt_done,
         pt_ready, o_done, o_ready, ot_done, dve_chain) = S
        units = [(i, b, h) for i in range(2) for b in range(NQ) for h in range(2)]
        NU = len(units)

        def keys(b):
            return [j for j in (b - 1, b, b + 1) if 0 <= j < NQ]

        def width(u):
            return (2 + len(keys(units[u][1]))) * P

        def transposed_at(u, c):
            return bank(4 + u % 2, c * P, (c + 1) * P) if c < 4 else bank(6 + u % 2, 0, P)

        def out_at(u):
            return bank(6 + u % 2, P, P + HD)

        with nc.Fori(0, 2) as kv:
            with clear_then_block(S) as block:
                @block.scalar
                def _(act):
                    nc.scalar.activation(selS[:].rearrange("p a c -> p (a c)"),
                                         csa[:, bass.ds(csa_at["sel"][0] + kv * 256, 256)], ACT.Copy)\
                        .then_inc(sel_ready, 1)
                    nc.scalar.activation(vS[:], vtok[:, :, bass.ds(kv * HD, HD)], ACT.Copy).then_inc(vs_ready, 1)
                    act.wait_ge(kd_done, 1)
                    nc.scalar.activation(kd[:, 0:C], psum[0][:, 0:C], ACT.Copy).then_inc(sel_ready, 1)

                    def exponentials(u):
                        i, b, h = units[u]
                        e = u % 4
                        act.wait_ge(max_ready, u + 1)
                        if u >= 2:
                            act.wait_ge(pt_done, u - 1)
                        if u >= 4:
                            act.wait_ge(o_ready, u - 3)
                        nc.scalar.activation(pr[u % 2][:, 0:width(u)], psum[u % 2][:, 0:width(u)], ACT.Exp,
                                             bias=nmx[:, e:e + 1], scale=HD ** -0.5,
                                             accum_out=rs[:, e:e + 1]).then_inc(exp_ready, 1)
                        nc.scalar.activation(es[:, e:e + 1], sinks[:, 0, 2 * i + h:2 * i + h + 1], ACT.Exp,
                                             bias=nmx[:, e:e + 1], scale=1.0).then_inc(exp_ready, 1)

                    def transposed(u):
                        act.wait_ge(pt_done, u + 1)
                        if u >= 2:
                            act.wait_ge(o_done, u - 1)
                        n = width(u) // P
                        i = nc.scalar.activation(pt[u % 2][:, 0:min(n, 4) * P], bank(4 + u % 2, 0, min(n, 4) * P),
                                                 ACT.Copy)
                        if n == 5:
                            i = nc.scalar.activation(pt[u % 2][:, 4 * P:5 * P], transposed_at(u, 4), ACT.Copy)
                        i.then_inc(pt_ready, 1)

                    for u in range(NU + 1):
                        if u < NU:
                            exponentials(u)
                        if u >= 1:
                            transposed(u - 1)

                @block.tensor
                def _(pe):
                    pe.wait_ge(sel_ready, 1)
                    for lo, hi in ((0, C), (C, 512), (512, N)):
                        nc.tensor.matmul(psum[0][:, lo:hi], selS[:, 0, :], kvT[:, 0, lo:hi], start=True, stop=True)
                    for a, lo, hi in ((0, C, 512), (256, 512, N)):
                        last = nc.tensor.matmul(psum[1][:, a:a + hi - lo], selS[:, 1, :], kvT[:, 0, lo:hi],
                                                start=True, stop=True)
                    last.then_inc(kd_done, 1)
                    for i in range(2):
                        last = nc.tensor.matmul(bank(4 + i), KA("rot"), qT[:, 2 * kv + i, :], start=True,
                                                stop=True)
                        last.then_inc(q_done, 1)

                    keep_warm(6, bank(6))

                    def scores(u):
                        i, b, h = units[u]
                        r = slice(h * HD, (h + 1) * HD)
                        lhs = qs[i][r, b * P:(b + 1) * P]
                        js = keys(b)
                        if u % (2 * NQ) == 0:
                            pe.wait_ge(q_ready, i + 1)
                        t = psum[u % 2]
                        nc.tensor.matmul(t[:, 0:C], lhs, kd[r, 0:C], start=True, stop=True)
                        at = C + js[0] * P
                        n0 = min(len(js) * P, 512 - C)
                        last = nc.tensor.matmul(t[:, C:C + n0], lhs, kd[r, at:at + n0], start=True, stop=True)
                        if len(js) == 3:
                            last = nc.tensor.matmul(t[:, 512:512 + P], lhs, kd[r, at + n0:at + n0 + P], start=True,
                                                    stop=True)
                        last.then_inc(s_done, 1)

                    def products(u):
                        i, b, h = units[u]
                        n = width(u) // P
                        pe.wait_ge(pt_ready, u + 1)
                        for c in range(n):
                            g = c if c < 2 else GC + keys(b)[c - 2]
                            last = nc.tensor.matmul(out_at(u), pt[u % 2][:, c * P:(c + 1) * P], vS[:, g, :],
                                                    start=c == 0, stop=c == n - 1)
                        last.then_inc(o_done, 1)

                    pe.wait_ge(kd_ready, 1)
                    scores(0)
                    scores(1)
                    pe.wait_ge(q_ready, 2)
                    pe.wait_ge(vs_ready, 1)
                    keep_warm(4, bank(6))
                    for u in range(NU):
                        if u in (1, 2):
                            keep_warm(2, bank(7))
                        pe.wait_ge(exp_ready, 2 * u + 1)
                        n = width(u) // P
                        if u >= 2:
                            pe.wait_ge(pt_ready, u - 1)
                        for c in range(4):
                            last = nc.tensor.transpose(transposed_at(u, c), pr[u % 2][:, c * P:(c + 1) * P],
                                                       K("ident"))
                        if n == 4:
                            last.then_inc(pt_done, 1)
                        if u + 2 < NU:
                            scores(u + 2)
                        if u >= 2:
                            pe.wait_ge(o_ready, u - 1)
                        if n == 5:
                            nc.tensor.transpose(transposed_at(u, 4), pr[u % 2][:, 4 * P:5 * P], K("ident"))\
                                .then_inc(pt_done, 1)
                        if u >= 1:
                            products(u - 1)
                    products(NU - 1)
                    for i in range(2):
                        pe.wait_ge(o_ready, NU)
                        for b in range(NQ):
                            last = nc.tensor.transpose(bank(i, b * P, (b + 1) * P), oS[:, i, b, :], K("ident"))
                        last.then_inc(ot_done, 1)

                @block.vector
                def _(dve):
                    link = Chain(dve, dve_chain)
                    nc.vector.tensor_copy(sinks[:, 0, :], prm[:, bass.ds(prm_at["sink"][0] + kv * 4, 4)])\
                        .then_inc(banded, 1)
                    link(nc.vector.tensor_scalar(sinks[:, 1, :], prm[:, bass.ds(prm_at["sink"][0] + kv * 4, 4)], -1.0,
                                                 None, MUL))
                    dve.wait_ge(kd_done, 1)
                    dve.wait_ge(sel_ready, 2)
                    nc.vector.tensor_tensor(tmp[0][:], psum[0][:, C:N], KA("cos"), MUL)
                    link(nc.vector.tensor_tensor(tmp[1][:], psum[1][:, 0:T], KA("sin"), MUL))
                    link(nc.vector.tensor_tensor(kd[:, C:N], tmp[0][:], tmp[1][:], ADD))
                    dve.sem_inc(kd_ready, 1)
                    for i in range(2):
                        dve.wait_ge(q_done, i + 1)
                        nc.vector.tensor_tensor(tmp[0][:], qT[:, 2 * kv + i, :], KA("cos"), MUL)
                        link(nc.vector.tensor_tensor(tmp[1][:], bank(4 + i), KA("sin"), MUL))
                        link(nc.vector.tensor_tensor(qs[i][:], tmp[0][:], tmp[1][:], ADD))
                        dve.sem_inc(q_ready, 1)

                    bands = [1]

                    def maximum(u):
                        i, b, h = units[u]
                        e, t = u % 4, psum[u % 2]
                        dve.wait_ge(s_done, u + 1)
                        for c, j in enumerate(keys(b)):
                            if j != b:
                                a = C + c * P
                                nc.vector.tensor_tensor(t[:, a:a + P], t[:, a:a + P],
                                                        KA("band_lo" if j < b else "band_hi"), ADD)\
                                    .then_inc(banded, 1)
                                bands[0] += 1
                        dve.wait_ge(banded, bands[0])
                        link(nc.vector.reduce_max(mx[:, e:e + 1], t[:, 0:width(u)], AX.X))
                        nc.vector.tensor_scalar(nmx[:, e:e + 1], mx[:, e:e + 1], -(HD ** -0.5),
                                                sinks[:, 1, 2 * i + h:2 * i + h + 1], MUL, MIN)\
                            .then_inc(max_ready, 1)

                    def denominator(u):
                        e = u % 4
                        dve.wait_ge(exp_ready, 2 * u + 2)
                        link(nc.vector.tensor_tensor(den[:, e:e + 1], rs[:, e:e + 1], es[:, e:e + 1], ADD))
                        link(nc.vector.reciprocal(den[:, e:e + 1], den[:, e:e + 1]))

                    def output(u):
                        i, b, h = units[u]
                        e = u % 4
                        dve.wait_ge(o_done, u + 1)
                        nc.vector.tensor_scalar(oS[:, i, b, h * HD:(h + 1) * HD], out_at(u), den[:, e:e + 1], None,
                                                MUL).then_inc(o_ready, 1)

                    maximum(0)
                    maximum(1)
                    for u in range(NU):
                        denominator(u)
                        if u + 2 < NU:
                            maximum(u + 2)
                        if u >= 1:
                            output(u - 1)
                    output(NU - 1)
                    for i in range(2):
                        dve.wait_ge(ot_done, i + 1)
                        nc.vector.tensor_copy(attT[:, 2 * kv + i, :], bank(i))
    att_in.close()

    NCH = 2 * N // Q
    ND = N // Q
    TURNS = (S_OUT - S_MOD) // PAIRS // 2
    WARM = 256
    LVL = 5
    drw = ExitStack()
    lws = sb(drw, "lws", [P, 2, P])
    vs = sb(drw, "vs", [P, 2, N])
    AR = sb(drw, "AR", [P, G, 2, P])
    bt = sb(drw, "bt", [P, 2, N])
    kt = sb(drw, "kt", [P, 2, N])
    PC = sb(drw, "PC", [P, NCH])

    def chunked(ap):
        return ap.rearrange("p (n t) -> p n t", t=Q)

    def tiled(ap):
        return ap.rearrange("p (g t) -> p g t", t=P)

    with nc.Fori(0, PAIRS) as p:
        with ExitStack() as st:
            names = ("sg", "cum", "al", "Pp", "Pn", "Pv", "kp", "bb")
            sg, cum, al, Pp, Pn, Pv, kp, bb = (sb(st, n, [P, 2, N]) for n in names)
            oka = sb(st, "oka", [P, 1])
            kkS, rS = sb(st, "kkS", [P, N]), sb(st, "rS", [P, T])
            S = sems(st, "lw_in", "lora_done", "sig_ready", "cum_ready", "exc_ready", "exp_ready", "kp_ready",
                     "bb_ready", "vs_ready", "bsum_in", "bsum_done", "dve_chain")
            (lw_in, lora_done, sig_ready, cum_ready, exc_ready, exp_ready, kp_ready, bb_ready, vs_ready, bsum_in,
             bsum_done, dve_chain) = S
            with clear_then_block(S) as block:
                @block.sync
                def _(sp):
                    sp.dma_start(lws[:], A["lw"][p]).then_inc(lw_in, 16)

                @block.tensor
                def _(pe):
                    pe.wait_ge(lw_in, 16)
                    for kind in range(2):
                        for d in range(2):
                            r = slice(d * HD, (d + 1) * HD)
                            for lo, hi in ((0, 512), (512, N)):
                                last = nc.tensor.matmul(psum[2 * kind + d][:, lo:hi], lws[r, kind, :],
                                                        lora[r, kind, lo:hi], start=True, stop=True)
                            last.then_inc(lora_done, 1)
                    pe.wait_ge(exp_ready, 1)
                    pe.wait_ge(sig_ready, 4)
                    keep_warm(4, bank(7))
                    pe.wait_ge(bsum_in, 1)
                    nc.tensor.matmul(bank(0), K("onesh"), bb[:, 0, 0:T], start=True, stop=True).then_inc(bsum_done, 1)
                    keep_warm(1, bank(7))

                @block.scalar
                def _(act):
                    for kind, (dst, bias) in enumerate(((sg, "w0"), (al, "a0"))):
                        for d in range(2):
                            act.wait_ge(lora_done, 2 * kind + d + 1)
                            nc.scalar.activation(dst[:, d, :], psum[2 * kind + d][:, 0:N], ACT.Sigmoid,
                                                 bias=prm[:, bass.ds(prm_at[bias][0] + 4 * d + p, 1)])\
                                .then_inc(sig_ready, 1)
                    nc.scalar.activation(vs[:, 0, :], vT[:, p, :], ACT.Copy)
                    nc.scalar.activation(kkS[:], kkT[:, p, :], ACT.Copy)
                    nc.scalar.activation(rS[:], rT[:, p, :], ACT.Copy).then_inc(vs_ready, 1)
                    act.wait_ge(vs_ready, 1)
                    nc.scalar.activation(vs[:, 1, 0:C], vs[:, 0, 0:C][:, ::-1], ACT.Copy)
                    nc.scalar.activation(vs[:, 1, C:N], vs[:, 0, C:N][:, ::-1], ACT.Copy).then_inc(vs_ready, 1)
                    act.wait_ge(cum_ready, 1)
                    nc.scalar.activation(Pn[:], cum[:], ACT.Exp, scale=DECAY).then_inc(exp_ready, 1)
                    nc.scalar.activation(Pp[:], cum[:], ACT.Exp, scale=-DECAY).then_inc(exp_ready, 1)
                    act.wait_ge(exc_ready, 1)
                    nc.scalar.activation(Pv[:], sg[:], ACT.Exp, scale=-DECAY).then_inc(exp_ready, 1)

                @block.gpsimd
                def _(pool):
                    pool.wait_ge(sig_ready, 4)
                    for d in range(2):
                        i = nc.gpsimd.tensor_tensor(bb[:, d, :], kkT[:, p, :], al[:, d, :], MUL)
                    i.then_inc(bb_ready, 1)
                    pool.wait_ge(cum_ready, 1)
                    nc.gpsimd.tensor_tensor(sg[:], cum[:], sg[:], SUB).then_inc(exc_ready, 1)

                @block.vector
                def _(dve):
                    link = Chain(dve, dve_chain)
                    dve.wait_ge(sig_ready, 2)
                    nc.vector.tensor_tensor_scan(cum[:, 0, :], K("scan"), sg[:, 0, :], 0.0, MUL, ADD)
                    nc.vector.tensor_tensor_scan(cum[:, 1, :][:, ::-1], K("scan"), sg[:, 1, :][:, ::-1], 0.0, MUL,
                                                 ADD).then_inc(cum_ready, 1)
                    ka = prm[:, bass.ds(prm_at["ka"][0] + p, 1)]
                    link(nc.vector.tensor_scalar(oka[:], ka, -1.0, 1.0, MUL, ADD))
                    dve.wait_ge(sig_ready, 4)
                    link(nc.vector.tensor_scalar(kp[:], al[:], ka, oka[:], MUL, ADD))
                    for d in range(2):
                        i = nc.vector.tensor_tensor(kp[:, d, :], kp[:, d, :], kT[:, p, :], MUL)
                    link(i)

                    def ordered(out, fn):
                        fn(out[:, 0, :], lambda ap: ap[:, 0:N], 0)
                        fn(out[:, 1, 0:C], lambda ap: ap[:, 0:C][:, ::-1], 1)
                        return fn(out[:, 1, C:N], lambda ap: ap[:, C:N][:, ::-1], 1)

                    dve.wait_ge(exp_ready, 1)
                    ordered(kt, lambda o, rd, d: nc.vector.tensor_tensor(o, rd(kp[:, d, :]), rd(Pn[:, d, :]), MUL))
                    dve.wait_ge(bb_ready, 1)
                    link(ordered(bt, lambda o, rd, d: nc.vector.tensor_tensor(o, rd(bb[:, d, :]), rd(Pn[:, d, :]), MUL)))
                    dve.wait_ge(exp_ready, 2)
                    dve.wait_ge(vs_ready, 2)
                    nc.vector.tensor_tensor(AR[:, GC:GD, 1, :], tiled(rS[:]), tiled(Pp[:, 0, C:N]), MUL)
                    nc.vector.tensor_tensor(AR[:, GD + GC:G, 1, :], tiled(rS[:][:, ::-1]),
                                            tiled(Pp[:, 1, C:N][:, ::-1]), MUL)
                    nc.vector.tensor_copy(PC[:, 0:ND], chunked(Pp[:, 0, :])[:, :, Q - 1])
                    nc.vector.tensor_copy(PC[:, ND:ND + C // Q], chunked(Pp[:, 1, 0:C][:, ::-1])[:, :, Q - 1])
                    nc.vector.tensor_copy(PC[:, ND + C // Q:NCH], chunked(Pp[:, 1, C:N][:, ::-1])[:, :, Q - 1])
                    link(nc.vector.tensor_tensor(bb[:, 1, 0:T], kp[:, 0, C:N], kp[:, 1, C:N], ADD))
                    link(nc.vector.scalar_tensor_tensor(bb[:, 0, 0:T], bb[:, 1, 0:T],
                                                        prm[:, bass.ds(prm_at["rk"][0] + p, 1)], rT[:, p, :], MUL, MUL))
                    dve.sem_inc(bsum_in, 1)
                    dve.wait_ge(exp_ready, 3)
                    for d, n0, n1, rd in ((0, 0, GD, lambda ap: ap[:, 0:N]),
                                          (1, GD, GD + GC, lambda ap: ap[:, 0:C][:, ::-1]),
                                          (1, GD + GC, G, lambda ap: ap[:, C:N][:, ::-1])):
                        nc.vector.scalar_tensor_tensor(AR[:, n0:n1, 0, :], tiled(rd(kkS[:])), -1.0,
                                                       tiled(rd(Pv[:, d, :])), MUL, MUL)
                    dve.wait_ge(bsum_done, 1)
                    nc.vector.tensor_tensor(vT[:, p, C:N], bank(0), vT[:, p, C:N], MUL)

        with ExitStack() as st:
            att_, btt, ktt, vtt = (sb(st, n, [P, G, P]) for n in ("at_tok", "b_tok", "k_tok", "v_tok"))
            LT, X, XT, W1, MT = (sb(st, n, [P, 2 * G, Q]) for n in ("LT", "X", "XT", "W1", "MT"))
            RBT, RKT = (sb(st, n, [P, 4 * (GD - GC), Q]) for n in ("RBT", "RKT"))
            yS = sb(st, "yS", [P, T])
            Z = sb(st, "Z", [P, 2, ND + 1, Q])
            F, E, GP, U = LT, X, MT, W1
            S = sems(st, "t_done", "t_ready", "pk_done", "lt_done", "l_done", "rb_done", "pk_used", "lt_used",
                     "l_used", "rb_used", "x0_ready", "x0t_done", "xt0_ready", "x_ready", "xt_ready", "tr_done", "w_done", "w_ready", "xx_done", "me_done", "me_ready", "fg_done", "fg_ready",
                     "u_done", "u_ready", "zp_done", "z_ready", "y_done", "dve_chain", "pool_chain", "mprod_ready",
                     "mod_done")
            (t_done, t_ready, pk_done, lt_done, l_done, rb_done, pk_used, lt_used, l_used, rb_used, x0_ready, x0t_done,
             xt0_ready, x_ready, xt_ready, tr_done, w_done, w_ready,
             xx_done, me_done, me_ready, fg_done, fg_ready, u_done, u_ready, zp_done, z_ready, y_done, dve_chain,
             pool_chain, mprod_ready, mod_done) = S
            msum = [t[:].rearrange("p d n -> p (d n)") for t in (kt, vs)]
            NBT = 3

            def half(i):
                return slice(i * Q, (i + 1) * Q)

            def is_lat(g):
                return g % GD >= GC

            def lat(k):
                return k - 2 * GC * (1 + k // (2 * GD))

            def lat_blocks(b):
                ks = [2 * g + h for g in range(4 * b, 4 * b + 4) for h in range(2) if is_lat(g)]
                return ks[0], ks[-1] + 1

            def units(b):
                return [(g, h, c) for g in range(4 * b, 4 * b + 4) for h in range(2) for c in range(2)]

            def by_rows(b):
                return [(g, c, h) for g in range(4 * b, 4 * b + 4) for c in range(2) for h in range(2)]

            def cols(i, b):
                return bank(i).rearrange("p (k j) -> p k j", j=Q)

            def chunk_bank(b, c):
                return bank((2 * b + 1, 6 + b % 2)[c], 0, 4 * Q)

            def of_chunks(t, b):
                return t[:, 8 * b:8 * b + 8, :].rearrange("p (g c) j -> p g c j", c=2)

            def by_head(t, k0, k1):
                return t[:, k0:k1, :].rearrange("p (g h) j -> p h g j", h=2)

            with clear_then_block(S) as block:
                @block.sync
                def _(sp):
                    with sp.Fori(0, TURNS) as t:
                        for s in range(2):
                            n = S_MOD + s
                            sp.wait_ge(mod_used[n % 2], TURNS * p + t + nth(n))
                            sp_load(sp, n + 2, 2 * TURNS * p + 2 * t)

                @block.tensor
                def _(pe):
                    def transposes(src, b, out):
                        for g in range(4 * b, 4 * b + 4):
                            at = (g - 4 * b) * P
                            i = nc.tensor.transpose(out[:, at:at + P],
                                                    src[:, 2 * g:2 * g + 2, :].rearrange("p k j -> p (k j)"),
                                                    K("ident"))
                        return i

                    def first_transposes(b):
                        pe.wait_ge(x0_ready, b + 1)
                        if b:
                            pe.wait_ge(xt0_ready, b)
                        transposes(X, b, bank(5)).then_inc(x0t_done, 1)

                    for b in range(NBT):
                        if b:
                            pe.wait_ge(l_used, b)
                            pe.wait_ge(rb_used, b)
                        for i in range(4):
                            for g in range(4 * b, 4 * b + 4):
                                src = (AR[:, g, 0, :], bt[:, g // GD, (g % GD) * P:(g % GD + 1) * P],
                                       kt[:, g // GD, (g % GD) * P:(g % GD + 1) * P],
                                       vs[:, g // GD, (g % GD) * P:(g % GD + 1) * P])[i]
                                last = nc.tensor.transpose(bank(i, (g - 4 * b) * P, (g - 4 * b + 1) * P), src,
                                                           K("ident"))
                        last.then_inc(t_done, 1)
                        if b:
                            pe.wait_ge(pk_used, b)
                        for g, h, c in units(b):
                            at = 512 * h + (g - 4 * b) * P
                            w = 2 if is_lat(g) else 1
                            t0 = (g % GD) * P + c * Q
                            last = nc.tensor.matmul(psum[3][half(c), at:at + w * Q], kt[half(h), g // GD, t0:t0 + Q],
                                                    AR[half(h), g, 0:w, half(c)], start=True, stop=True)
                        last.then_inc(pk_done, 1)
                        if b:
                            pe.wait_ge(lt_used, b)
                        for g, c, h in by_rows(b):
                            t0, at = (g % GD) * P + c * Q, (2 * (g - 4 * b) + c) * Q
                            last = nc.tensor.matmul(bank(4, at, at + Q)[half(h)], bt[half(h), g // GD, t0:t0 + Q],
                                                    AR[half(h), g, 0, half(c)], start=True, stop=True)
                        last.then_inc(lt_done, 1)
                        pe.wait_ge(t_ready, b + 1)
                        for g, c, h in by_rows(b):
                            t0, at = (g % GD) * P + c * Q, (2 * (g - 4 * b) + c) * Q
                            last = nc.tensor.matmul(bank(0, at, at + Q)[half(h)], AR[half(h), g, 0, half(c)],
                                                    bt[half(h), g // GD, t0:t0 + Q], start=True, stop=True)
                        last.then_inc(l_done, 1)
                        for g, c, h in by_rows(b):
                            if is_lat(g):
                                t0, at = (g % GD) * P + c * Q, (g - 4 * b) * Q
                                last = nc.tensor.matmul(bank(2 + h, at, at + Q)[half(c)],
                                                        bt[half(h), g // GD, t0:t0 + Q], AR[half(h), g, 1, half(c)],
                                                        start=True, stop=True)
                        last.then_inc(rb_done, 1)
                        if b:
                            first_transposes(b - 1)
                        keep_warm(1, bank(1))
                    pe.wait_ge(pk_used, NBT)
                    keep_warm(4, bank(6))
                    first_transposes(NBT - 1)
                    pe.wait_ge(rb_used, NBT)
                    pe.wait_ge(xt0_ready, NBT)

                    def next_x(lv, b):
                        pe.wait_ge(xt_ready, NBT * lv + b + 1)
                        transposes(XT, b, bank(2 * b + 1)).then_inc(tr_done, 1)

                    for lv in range(LVL):
                        for b in range(NBT):
                            if lv:
                                pe.wait_ge(x_ready, NBT * (lv - 1) + b + 1)
                            for g, c, h in by_rows(b):
                                n, at = 2 * g + c, (g - 4 * b) * Q
                                last = nc.tensor.matmul(bank(2 * b + h, at, at + Q)[half(c)], LT[half(h), n, :],
                                                        X[half(h), n, :], start=True, stop=True)
                            last.then_inc(w_done, 1)
                            if WARM:
                                keep_warm(1, bank(6), WARM)
                        for b in range(NBT):
                            pe.wait_ge(w_ready, NBT * lv + b + 1)
                            for g, h, c in units(b):
                                k = 2 * g + h
                                last = nc.tensor.matmul(bank(2 * b, (k - 8 * b) * Q, (k - 8 * b + 1) * Q)[half(c)],
                                                        W1[half(c), k, :], XT[half(c), k, :], start=True, stop=True)
                            last.then_inc(xx_done, 1)
                            if WARM:
                                keep_warm(1, bank(6), WARM)
                            if b and lv < LVL - 1:
                                next_x(lv, b - 1)
                        if lv < LVL - 1:
                            next_x(lv, NBT - 1)
                    def by_chunk(n, b):
                        at = (n // 2 - 4 * b) * Q
                        return chunk_bank(b, n % 2)[:, at:at + Q]

                    for b in range(NBT):
                        pe.wait_ge(xt_ready, NBT * (LVL - 1) + b + 1)
                        if b == 2:
                            pe.wait_ge(me_ready, 1)
                        keep_warm(1, bank(2 * b), 256)
                        for g, h, c in units(b):
                            k = 2 * g + h
                            nc.tensor.matmul(bank(2 * b, (k - 8 * b) * Q, (k - 8 * b + 1) * Q)[half(c)],
                                             MT[half(c), k, :], vtt[half(c), g, h * Q:(h + 1) * Q], start=True,
                                             stop=True)
                        for g, h, c in units(b):
                            k, n = 2 * g + h, 2 * g + c
                            last = nc.tensor.matmul(by_chunk(n, b)[half(h)],
                                                    att_[half(c), g, h * Q:(h + 1) * Q], XT[half(c), k, :],
                                                    start=True, stop=True)
                        last.then_inc(me_done, 1)
                    for b in range(NBT):
                        pe.wait_ge(me_ready, b + 1)
                        keep_warm(1, bank(2 * b), 256)
                        for g, h, c in units(b):
                            k = 2 * g + h
                            nc.tensor.matmul(bank(2 * b, (k - 8 * b) * Q, (k - 8 * b + 1) * Q)[half(c)],
                                             XT[half(c), k, :], F[half(c), k, :], start=True, stop=True)
                        if b == 0:
                            pe.wait_ge(me_ready, NBT)
                        if b == 2:
                            pe.wait_ge(fg_ready, 1)
                        for g, h, c in units(b):
                            n = 2 * g + c
                            last = nc.tensor.matmul(by_chunk(n, b)[half(h)],
                                                    ktt[half(c), g, h * Q:(h + 1) * Q],
                                                    vtt[half(c), g, h * Q:(h + 1) * Q], start=True, stop=True)
                        last.then_inc(fg_done, 1)
                    pe.wait_ge(fg_ready, NBT)

                    def state_out(s):
                        for d in range(2):
                            n, at = ND * d + s, (s - C // Q) * Q
                            for h in range(2):
                                nc.tensor.matmul(bank(2 + d, at, at + Q)[half(h)], Z[half(h), d, s, :],
                                                 AR[half(h), n // 2, 1, half(n % 2)], start=True, stop=True)

                    def own_out(s):
                        for d in range(2):
                            n = ND * d + s
                            g, c = n // 2, n % 2
                            at = (4 * d + (s - C // Q) // 2) * Q
                            for h in range(2):
                                o = bank(4 + c, at, at + Q)[half(h)]
                                nc.tensor.matmul(o, U[half(c), 2 * g + h, :], RBT[half(c), lat(2 * g + h), :],
                                                 start=True, stop=False)
                                last = nc.tensor.matmul(o, vtt[half(c), g, h * Q:(h + 1) * Q],
                                                        RKT[half(c), lat(2 * g + h), :], start=False, stop=True)
                        return last

                    for s in range(ND):
                        pe.wait_ge(z_ready, s + 1)
                        for d in range(2):
                            n = ND * d + s
                            for h in range(2):
                                at = (2 * (s % 2) + d) * Q
                                last = nc.tensor.matmul(bank(6 + h, at, at + Q)[half(n % 2)], E[half(h), n, :],
                                                        Z[half(h), d, s, :], start=True, stop=True)
                        last.then_inc(u_done, 1)
                        if s >= C // Q:
                            state_out(s)
                        pe.wait_ge(u_ready, s + 1)
                        for d in range(2):
                            n = ND * d + s
                            g, c = n // 2, n % 2
                            for h in range(2):
                                last = nc.tensor.matmul(bank(s % 2, d * Q, (d + 1) * Q)[half(h)],
                                                        btt[half(c), g, h * Q:(h + 1) * Q], U[half(c), 2 * g + h, :],
                                                        start=True, stop=True)
                        last.then_inc(zp_done, 1)
                        if s >= C // Q:
                            last = own_out(s)
                    last.then_inc(y_done, 1)
                    for s in range(2):
                        pe.wait_ge(mod_used[s], TURNS * p + (S_IN // 2 + TURNS))
                    pe.wait_ge(z_ready, ND + 1)
                    for t in range(TURNS):
                        for s in range(2):
                            for m in range(2):
                                at = 4 * t + 2 * s + m
                                last = nc.tensor.matmul(bank(0, at, at + 1),
                                                        msum[s][:, 256 * t + m * P:256 * t + (m + 1) * P],
                                                        K("ones", 0, 1), start=True, stop=True)
                    last.then_inc(mod_done, 1)

                @block.scalar
                def _(act):
                    def first_xt(b):
                        act.wait_ge(x0t_done, b + 1)
                        nc.scalar.activation(XT[:, 8 * b:8 * b + 8, :], cols(5, b), ACT.Copy).then_inc(xt0_ready, 1)

                    for b in range(NBT):
                        act.wait_ge(t_done, b + 1)
                        for i, dst in enumerate((att_, btt, ktt, vtt)):
                            j = nc.scalar.activation(dst[:, 4 * b:4 * b + 4, :],
                                                     bank(i).rearrange("p (g c) -> p g c", c=P), ACT.Copy)
                        j.then_inc(t_ready, 1)
                        if b:
                            first_xt(b - 1)
                    first_xt(NBT - 1)
                    for lv in range(LVL - 1):
                        for b in range(NBT):
                            act.wait_ge(tr_done, NBT * lv + b + 1)
                            nc.scalar.activation(X[:, 8 * b:8 * b + 8, :], cols(2 * b + 1, b), ACT.Copy)\
                                .then_inc(x_ready, 1)
                    for b in range(NBT):
                        act.wait_ge(me_done, b + 1)
                        nc.scalar.activation(F[:, 8 * b:8 * b + 8, :], cols(2 * b, b), ACT.Copy)
                        for c in range(2):
                            i = nc.scalar.activation(of_chunks(E, b)[:, :, c, :],
                                                     chunk_bank(b, c).rearrange("p (g j) -> p g j", j=Q), ACT.Copy)
                        i.then_inc(me_ready, 1)

                @block.gpsimd
                def _(pool):
                    pool.wait_ge(pk_done, NBT)
                    with pool.Fori(0, TURNS) as t:
                        for s in range(2):
                            n = S_MOD + s
                            r = raw[n % 2]
                            pool.wait_ge(raw_loaded[n % 2], 16 * TURNS * p + 16 * t + 16 * (n // 2 + 1))
                            nc.gpsimd.tensor_tensor(r[:], r[:], cs[:, :, 0].unsqueeze(2).to_broadcast([P, KT, 256]),
                                                    MUL).then_inc(mprod_ready, 1)
                            for i, w in enumerate((4, 2)):
                                pool.wait_ge(mprod_ready, 6 * t + (3 * s + i + 1))
                                nc.gpsimd.tensor_tensor(r[:, 0:w, :], r[:, 0:w, :], r[:, w:2 * w, :], ADD)\
                                    .then_inc(mprod_ready, 1)
                            pool.wait_ge(mprod_ready, 6 * t + (3 * s + 3))
                            nc.gpsimd.tensor_tensor(msum[s][:, bass.ds(256 * t, 256)], r[:, 0, :], r[:, 1, :], ADD)\
                                .then_inc(mod_used[n % 2], 1)

                @block.vector
                def _(dve):
                    link = Chain(dve, dve_chain)

                    def wide(name, n, lo=0, hi=None):
                        return K(name, lo, hi).unsqueeze(1).to_broadcast([P, n, Q])

                    def wide2(name, n):
                        return K(name).unsqueeze(1).unsqueeze(1).to_broadcast([P, 2, n, Q])

                    nc.vector.memset(Z[:, :, 0, :], 0.0)
                    for b in range(NBT):
                        k0, k1 = lat_blocks(b)
                        g0, g1 = k0 // 2 - 4 * b, k1 // 2 - 4 * b
                        k = slice(8 * b, 8 * b + 8)
                        pp = psum[3][:, :].rearrange("p (h g j) -> p h g j", h=2, j=P)
                        dve.wait_ge(pk_done, b + 1)
                        nc.vector.tensor_tensor(by_head(RKT, lat(k0), lat(k1 - 1) + 1), pp[:, :, g0:g1, Q:P],
                                                wide2("upper_eq", g1 - g0), MUL)
                        nc.vector.tensor_tensor(by_head(MT, 8 * b, 8 * b + 8), pp[:, :, :, 0:Q], wide2("upper", 4),
                                                MUL).then_inc(pk_used, 1)
                        dve.wait_ge(lt_done, b + 1)
                        nc.vector.tensor_tensor(LT[:, k, :], cols(4, b), wide("upper", 8), MUL).then_inc(lt_used, 1)
                        dve.wait_ge(l_done, b + 1)
                        link(nc.vector.tensor_tensor(X[:, k, :], cols(0, b), wide("lvl1", 8), MUL))
                        dve.sem_inc(l_used, 1)
                        nc.vector.tensor_tensor(X[:, k, :], X[:, k, :], wide("eye64", 8), ADD).then_inc(x0_ready, 1)
                        dve.wait_ge(rb_done, b + 1)
                        rb = psum[1][:, :].rearrange("p (h w) -> p h w", h=2)[:, :, g0 * Q:g1 * Q]\
                            .rearrange("p h (g j) -> p h g j", j=Q)
                        nc.vector.tensor_tensor(by_head(RBT, lat(k0), lat(k1 - 1) + 1), rb,
                                                wide2("upper_eq", g1 - g0), MUL).then_inc(rb_used, 1)
                    for lv in range(LVL):
                        for b in range(NBT):
                            dve.wait_ge(w_done, NBT * lv + b + 1)
                            ww = psum[b][:, :].rearrange("p (h w) -> p h w", h=2)[:, :, 0:4 * Q]\
                                .rearrange("p h (g j) -> p h g j", j=Q)
                            m = K("lvl", lv * Q, (lv + 1) * Q).unsqueeze(1).unsqueeze(1).to_broadcast([P, 2, 4, Q])
                            nc.vector.tensor_tensor(by_head(W1, 8 * b, 8 * b + 8), ww, m, MUL).then_inc(w_ready, 1)
                        for b in range(NBT):
                            k = slice(8 * b, 8 * b + 8)
                            if lv == 0:
                                dve.wait_ge(xt0_ready, b + 1)
                            dve.wait_ge(xx_done, NBT * lv + b + 1)
                            nc.vector.tensor_tensor(XT[:, k, :], XT[:, k, :], cols(2 * b, b), ADD)\
                                .then_inc(xt_ready, 1)
                    for b in range(NBT):
                        k = slice(8 * b, 8 * b + 8)
                        dve.wait_ge(fg_done, b + 1)
                        nc.vector.tensor_copy(F[:, k, :], cols(2 * b, b))
                        for c in range(2):
                            i = nc.vector.tensor_tensor(of_chunks(GP, b)[:, :, c, :],
                                                        chunk_bank(b, c).rearrange("p (g j) -> p g j", j=Q),
                                                        PC[:, k].rearrange("p (g c) -> p g c", c=2)[:, :, c]
                                                        .unsqueeze(2).to_broadcast([P, 4, Q]), MUL)
                        i.then_inc(fg_ready, 1)
                    dve.wait_ge(fg_ready, NBT)
                    dve.sem_inc(z_ready, 1)
                    for s in range(ND):
                        for d in range(2):
                            n = ND * d + s
                            i = nc.vector.scalar_tensor_tensor(Z[:, d, s + 1, :], Z[:, d, s, :], PC[:, n:n + 1],
                                                               GP[:, n, :], MUL, ADD)
                        link(i)
                        dve.wait_ge(u_done, s + 1)
                        c = s % 2
                        uf = [t[half(c), :, :].rearrange("p (d g h) v -> p d g h v", d=2, h=2)[:, :, s // 2, :, :]
                              for t in (U, F)]
                        up_ = psum[3][half(c), :].rearrange("p (h w) -> p h w", h=2)[:, :, 2 * Q * c:2 * Q * c + 2 * Q]
                        nc.vector.tensor_tensor(uf[0], up_.rearrange("p h (d v) -> p d h v", d=2), uf[1], ADD)\
                            .then_inc(u_ready, 1)
                        dve.wait_ge(zp_done, s + 1)
                        for d in range(2):
                            n = ND * d + s
                            i = nc.vector.scalar_tensor_tensor(Z[:, d, s + 1, :], bank(c, d * Q, (d + 1) * Q),
                                                               PC[:, n:n + 1], Z[:, d, s + 1, :], MUL, ADD)
                        i.then_inc(z_ready, 1)
                        dve.wait_ge(z_ready, s + 2)
                    dve.wait_ge(y_done, 1)
                    own_ = psum[2][:, :].rearrange("p (c d s j) -> p d s c j", c=2, d=2, j=Q)
                    for d in range(2):
                        y = yS[:] if d == 0 else yS[:][:, ::-1]
                        if d == 0:
                            link(nc.vector.tensor_copy(y, bank(2)))
                        else:
                            link(nc.vector.tensor_tensor(y, bank(3), y, ADD))
                        y4 = y.rearrange("p (s c j) -> p s c j", c=2, j=Q)
                        link(nc.vector.tensor_tensor(y4, own_[:, d], y4, ADD))
                    nc.vector.tensor_copy(rT[:, p, :], yS[:])
                    dve.wait_ge(mod_done, 1)
                    nc.vector.tensor_tensor(mod[:, bass.ds(4 * TURNS * p + 16, 4 * TURNS)], bank(0, 0, 4 * TURNS),
                                            prm[:, bass.ds(4 * TURNS * p + 16, 4 * TURNS)], ADD)
    drw.close()

    out_proj = ExitStack()
    W = [[sb(out_proj, f"wo{i}{s}", [P, KT, 256], F32R) for s in range(2)] for i in range(2)]
    h = [sb(out_proj, f"ho{i}", [P, KT, T], F32R) for i in range(2)]
    with ExitStack() as st:
        g2 = sb(st, "g2", [P, PAIRS * P])
        sq = [sb(st, f"gsq{i}", [P, T]) for i in range(2)]
        rg = [sb(st, f"grs{i}", [P, T]) for i in range(2)]
        S = sems(st, "g2_in", "mean_done", "yc_ready", "gsq_ready", "var_done", "root_ready", "yn_ready", "ys_ready",
                 "gate_done", "o_ready", "hi_made", "dve_chain", "lo_made")
        (g2_in, mean_done, yc_ready, gsq_ready, var_done, root_ready, yn_ready, ys_ready, gate_done, o_ready, hi_made,
         dve_chain, lo_made) = S
        with clear_then_block(S) as block:
            @block.sync
            def _(sp):
                sp.dma_start(g2[:], A["g2"]).then_inc(g2_in, 16)

            @block.tensor
            def _(pe):
                for i in range(PAIRS):
                    nc.tensor.matmul(bank(i), K("onesh"), rT[:, i, :], start=True, stop=True).then_inc(mean_done, 1)
                pe.wait_ge(g2_in, 16)
                for i in range(PAIRS):
                    nc.tensor.matmul(bank(4 + i), g2[:, i * P:(i + 1) * P], gT[:], start=True, stop=True)\
                        .then_inc(gate_done, 1)
                for i in range(PAIRS):
                    pe.wait_ge(gsq_ready, i + 1)
                    nc.tensor.matmul(bank(i), K("onesh"), sq[i % 2][:], start=True, stop=True).then_inc(var_done, 1)

            @block.scalar
            def _(act):
                for i in range(PAIRS):
                    act.wait_ge(yc_ready, i + 1)
                    if i >= 2:
                        act.wait_ge(var_done, i - 1)
                    nc.scalar.activation(sq[i % 2][:], rT[:, i, :], ACT.Square).then_inc(gsq_ready, 1)
                nc.scalar.activation(h[0][:, 0:PAIRS, :], attT, ACT.Copy).then_inc(hi_made, 1)
                for i in range(PAIRS):
                    act.wait_ge(var_done, i + 1)
                    if i >= 2:
                        act.wait_ge(yn_ready, i - 1)
                    nc.scalar.activation(rg[i % 2][:], bank(i), ACT.Sqrt, bias=small[:, 1:2], scale=1.0 / HD)\
                        .then_inc(root_ready, 1)
                for i in range(PAIRS):
                    act.wait_ge(yn_ready, i + 1)
                    nc.scalar.activation(rT[:, i, :], rT[:, i, :], ACT.Identity, scale=R("lnw", i, i + 1),
                                         bias=R("lnb", i, i + 1)).then_inc(ys_ready, 1)
                for i in range(PAIRS):
                    act.wait_ge(o_ready, i + 1)
                    nc.scalar.activation(h[0][:, PAIRS + i, :], rT[:, i, :], ACT.Copy).then_inc(hi_made, 1)

            @block.vector
            def _(dve):
                link = Chain(dve, dve_chain)
                for i in range(PAIRS):
                    dve.wait_ge(mean_done, i + 1)
                    nc.vector.scalar_tensor_tensor(rT[:, i, :], bank(i), -1.0 / HD, rT[:, i, :], MUL, ADD)\
                        .then_inc(yc_ready, 1)
                for i in range(PAIRS):
                    dve.wait_ge(root_ready, i + 1)
                    link(nc.vector.reciprocal(rg[i % 2][:], rg[i % 2][:]))
                    nc.vector.tensor_tensor(rT[:, i, :], rT[:, i, :], rg[i % 2][:], MUL).then_inc(yn_ready, 1)
                for i in range(PAIRS):
                    dve.wait_ge(ys_ready, i + 1)
                    link(nc.vector.tensor_tensor(rT[:, i, :], rT[:, i, :], vT[:, i, C:N], ADD))
                    dve.wait_ge(gate_done, i + 1)
                    nc.vector.tensor_tensor(rT[:, i, :], bank(4 + i), rT[:, i, :], MUL).then_inc(o_ready, 1)

            @block.gpsimd
            def _(pool):
                pool.wait_ge(hi_made, 1)
                nc.gpsimd.tensor_tensor(h[1][:, 0:PAIRS, :], attT, h[0][:, 0:PAIRS, :].bitcast(F32), SUB)
                for i in range(PAIRS):
                    pool.wait_ge(hi_made, i + 2)
                    nc.gpsimd.tensor_tensor(h[1][:, PAIRS + i, :], rT[:, i, :], h[0][:, PAIRS + i, :].bitcast(F32),
                                            SUB).then_inc(lo_made, 1)

    one = ((lambda s, m: 2 * s + m, (0, T)),)

    def dense(n0, nb, evac, W, h):
        with nc.Block() as block:
            @block.sync
            def _(sp):
                with sp.Fori(0, nb // 2) as turn:
                    up = 2 * turn
                    for j in range(2):
                        sp_next(sp, n0 + j, up)

            @block.gpsimd
            def _(pool):
                with pool.Fori(0, nb // 2) as turn:
                    up = 2 * turn
                    for j in range(2):
                        pool_lo(pool, n0 + j, W, up)

            @block.tensor
            def _(pe):
                with pe.Fori(0, nb // 2) as turn:
                    up = 2 * turn
                    for j in range(2):
                        pe_block(pe, n0 + j, W, h, up=up, parts=((one[0]),))

            @block.scalar
            def _(act):
                act_hi(act, n0, W)
                act_hi(act, n0 + 1, W)
                for j in range(nb):
                    n = n0 + j
                    for m in range(2):
                        act.wait_ge(tile_done[n % 2][m], nth(n))
                        nc.scalar.activation(evac(2 * j + m), bank(2 * (n % 2) + m), ACT.Copy)\
                            .then_inc(tile_free[n % 2][m], 1)
                    if j + 2 < nb:
                        act_hi(act, n + 2, W)

    def norms(layer, g_post, gate_tile, g_pre=None, pre_layer=None, pre_tile=None):
        with ExitStack() as st:
            sq = [sb(st, f"nsq{i}", [P, T]) for i in range(2)]
            rst = [sb(st, f"nrst{i}", [P, T]) for i in range(2)]
            hf = [sb(st, f"nhf{i}", [P, T]) for i in range(2)]
            S = sems(st, "sq_ready", "sq_used", "root_ready", "x_ready", "hf_ready", "hs_ready", "hhi_ready", "hf_used",
                     "dve_chain", "out_done")
            sq_ready, sq_used, root_ready, x_ready, hf_ready, hs_ready, hhi_ready, hf_used, dve_chain, out_done = S
            rounds = 2 if g_pre else 1
            pre_at = 48 * pre_layer + pre_tile if g_pre else None
            with clear_then_block(S) as block:
                @block.scalar
                def _(act):
                    for r in range(rounds):
                        for k in range(KT):
                            i = r * KT + k
                            if r:
                                act.wait_ge(x_ready, k + 1)
                            if i >= 2:
                                act.wait_ge(sq_used, i - 1)
                            nc.scalar.activation(sq[i % 2][:], (yb, x)[r][:, k, :], ACT.Square).then_inc(sq_ready, 1)
                        act.wait_ge(sq_used, (r + 1) * KT)
                        nc.scalar.activation(rst[r][:], bank(6 + r), ACT.Sqrt, bias=small[:, 0:1], scale=1.0 / D)\
                            .then_inc(root_ready, 1)
                    if rounds == 1:
                        for k in range(KT):
                            act.wait_ge(x_ready, k + 1)
                            act.dma_start(A["out"][:, k, :], x[:, k, :]).then_inc(out_done, 16)
                        act.wait_ge(out_done, 16 * KT)
                        return
                    for k in range(KT):
                        act.wait_ge(hf_ready, k + 1)
                        f = hf[k % 2]
                        nc.scalar.activation(f[:], f[:], ACT.Identity, scale=nsc[:, 3, k:k + 1],
                                             bias=mod[:, pre_at + k:pre_at + k + 1]).then_inc(hs_ready, 1)
                        act.wait_ge(hs_ready, k + 1)
                        nc.scalar.activation(h[0][:, k], f[:], ACT.Copy).then_inc(hhi_ready, 1)

                @block.tensor
                def _(pe):
                    for i in range(rounds * KT):
                        pe.wait_ge(sq_ready, i + 1)
                        nc.tensor.matmul(bank(6 + i // KT), K("ones"), sq[i % 2][:], start=i % KT == 0,
                                         stop=i % KT == KT - 1).then_inc(sq_used, 1)

                @block.vector
                def _(dve):
                    link = Chain(dve, dve_chain)
                    nc.vector.tensor_tensor(nsc[:, 2, :], mod[:, 48 * layer + gate_tile:48 * layer + gate_tile + KT], R(g_post), MUL)
                    if g_pre:
                        nc.vector.scalar_tensor_tensor(nsc[:, 3, :], mod[:, pre_at + KT:pre_at + 2 * KT],
                                                       1.0, R(g_pre), ADD, MUL)
                    dve.wait_ge(root_ready, 1)
                    link(nc.vector.reciprocal(rst[0][:], rst[0][:]))
                    for k in range(KT):
                        link(nc.vector.tensor_tensor(yb[:, k, :], yb[:, k, :], rst[0][:], MUL))
                        nc.vector.scalar_tensor_tensor(x[:, k, :], yb[:, k, :], nsc[:, 2, k:k + 1], x[:, k, :], MUL, ADD)\
                            .then_inc(x_ready, 1)
                    if rounds == 1:
                        return
                    dve.wait_ge(root_ready, 2)
                    link(nc.vector.reciprocal(rst[1][:], rst[1][:]))
                    for k in range(KT):
                        if k >= 2:
                            dve.wait_ge(hf_used, k - 1)
                        nc.vector.tensor_tensor(hf[k % 2][:], x[:, k, :], rst[1][:], MUL).then_inc(hf_ready, 1)

                if rounds == 2:
                    @block.gpsimd
                    def _(pool):
                        for k in range(KT):
                            pool.wait_ge(hhi_ready, k + 1)
                            nc.gpsimd.tensor_tensor(h[1][:, k], hf[k % 2][:], h[0][:, k].bitcast(F32), SUB)\
                                .then_inc(hf_used, 1)

    def mlp(n0, last_phase):
        with ExitStack() as st:
            hid = [sb(st, f"hid{i}", [P, KT, T], F32R) for i in range(2)]
            rl = [sb(st, f"rl{i}", [P, T]) for i in range(2)]
            sq = [sb(st, f"rs{i}", [P, T]) for i in range(2)]
            S = sems(st, "sq_ready", "hid_hi", "hid_ready", "dve_chain")
            sq_ready, hid_hi, hid_ready, dve_chain = S
            NB = 32
            with clear_then_block(S) as block:
                @block.sync
                def _(sp):
                    with sp.Fori(0, (NB - 2 * last_phase) // 2) as turn:
                        up = 2 * turn
                        for j in range(2):
                            sp_next(sp, n0 + j, up)

                @block.gpsimd
                def _(pool):
                    with pool.Fori(0, NB // 2) as turn:
                        up = 2 * turn
                        for j in range(2):
                            pool_lo(pool, n0 + j, W, up)

                @block.tensor
                def _(pe):
                    with pe.Fori(0, NB // 8) as turn:
                        up = 8 * turn
                        for j in range(8):
                            pe_block(pe, n0 + j, W, h if j < 4 else hid, up=up, parts=one,
                                     ready=(hid_ready, lambda k: up + k + 1) if j == 4 else None)

                @block.scalar
                def _(act):
                    act_hi(act, n0, W)
                    act_hi(act, n0 + 1, W)

                    def quarter(up, ahead):
                        for j in range(8):
                            n = n0 + j
                            if j < 4:
                                for m in range(2):
                                    t = 2 * j + m
                                    act.wait_ge(tile_done[n % 2][m], nth(n) + up // 2)
                                    nc.scalar.activation(rl[t % 2][:], bank(2 * (n % 2) + m), ACT.Relu)\
                                        .then_inc(tile_free[n % 2][m], 1)
                                    act.wait_ge(sq_ready, up + t + 1)
                                    nc.scalar.activation(hid[0][:, t], sq[t % 2][:], ACT.Copy).then_inc(hid_hi, 1)
                            if j < 6 or ahead:
                                act_hi(act, n + 2, W, up)

                    with act.Fori(0, (NB - 8) // 8) as turn:
                        up = 8 * turn
                        quarter(up, True)
                    quarter(NB - 8, False)

                @block.vector
                def _(dve):
                    link = Chain(dve, dve_chain)
                    link(nc.vector.memset(yb[:], 0.0))
                    with dve.Fori(0, NB // 8) as turn:
                        up = 8 * turn
                        for j in range(8):
                            n = n0 + j
                            for m in range(2):
                                if j < 4:
                                    t = 2 * j + m
                                    dve.wait_ge(tile_free[n % 2][m], nth(n) + up // 2)
                                    nc.vector.tensor_tensor(sq[t % 2][:], rl[t % 2][:], rl[t % 2][:], MUL)\
                                        .then_inc(sq_ready, 1)
                                    dve.wait_ge(hid_hi, up + t + 1)
                                    nc.vector.tensor_tensor(hid[1][:, t], sq[t % 2][:], hid[0][:, t].bitcast(F32), SUB)\
                                        .then_inc(hid_ready, 1)
                                else:
                                    c = 2 * (j - 4) + m
                                    dve.wait_ge(tile_done[n % 2][m], nth(n) + up // 2)
                                    nc.vector.tensor_tensor(yb[:, c, :], bank(2 * (n % 2) + m), yb[:, c, :], ADD)\
                                        .then_inc(tile_free[n % 2][m], 1)

    dense(S_OUT, 4, lambda t: yb[:, t, :], W, h)
    out_proj.close()
    mix.close()
    tail = ExitStack()
    W = [[sb(tail, f"v{i}{s}", [P, KT, 256], F32R) for s in range(2)] for i in range(2)]
    h = [sb(tail, f"hm{i}", [P, KT, T], F32R) for i in range(2)]
    norms(0, "g01", 16, "g02", 0, 24)
    mlp(S_MLP0, False)
    norms(0, "g03", 40, "g10", 1, 0)

    with ExitStack() as st:
        gates = sb(st, "gates", [P, 2 * KT, T])
        u = sb(st, "u", [P, KT, T + 2])
        cv = [sb(st, f"cv{i}", [P, T]) for i in range(2)]
        S = sems(st, "u_ready", "c1_ready", "cv_ready", "chi_ready", "cv_used", "dve_chain")
        u_ready, c1_ready, cv_ready, chi_ready, cv_used, dve_chain = S
        dense(S_CIN, 12, lambda t: gates[:, t, :] if t < 2 * KT else u[:, t - 2 * KT, 1:T + 1], W, h)
        with clear_then_block(S) as block:
            @block.vector
            def _(dve):
                link = Chain(dve, dve_chain)
                nc.vector.memset(u[:, :, 0], 0.0)
                link(nc.vector.memset(u[:, :, T + 1], 0.0))
                for k in range(KT):
                    link(nc.vector.tensor_tensor(u[:, k, 1:T + 1], u[:, k, 1:T + 1], gates[:, KT + k, :], MUL))
                    dve.sem_inc(u_ready, 1)
                    dve.wait_ge(c1_ready, k + 1)
                    c = cv[k % 2]
                    for tap, o in ((0, 0), (2, 2)):
                        link(nc.vector.scalar_tensor_tensor(c[:], u[:, k, o:o + T],
                                                            R("cw", tap * KT + k, tap * KT + k + 1), c[:], MUL, ADD))
                    nc.vector.tensor_tensor(c[:], c[:], gates[:, k, :], MUL).then_inc(cv_ready, 1)

            @block.scalar
            def _(act):
                for k in range(KT):
                    act.wait_ge(u_ready, k + 1)
                    if k >= 2:
                        act.wait_ge(cv_used, k - 1)
                    nc.scalar.activation(cv[k % 2][:], u[:, k, 1:T + 1], ACT.Copy,
                                         scale=R("cw", KT + k, KT + k + 1)).then_inc(c1_ready, 1)
                    act.wait_ge(cv_ready, k + 1)
                    nc.scalar.activation(h[0][:, k], cv[k % 2][:], ACT.Copy).then_inc(chi_ready, 1)

            @block.gpsimd
            def _(pool):
                for k in range(KT):
                    pool.wait_ge(chi_ready, k + 1)
                    nc.gpsimd.tensor_tensor(h[1][:, k], cv[k % 2][:], h[0][:, k].bitcast(F32), SUB)\
                        .then_inc(cv_used, 1)
        dense(S_COUT, 4, lambda t: yb[:, t, :], W, h)
    norms(1, "g11", 16, "g12", 1, 24)
    mlp(S_MLP1, True)
    norms(1, "g13", 40)
    tail.close()
    top.close()


def kernel(**inputs):
    import numpy as np
    import concourse.bacc as bacc
    from concourse import mybir
    from concourse.bass_utils import run_bass_kernel_spmd

    v = {k: np.asarray(a) for k, a in inputs.items()}
    T, C, D = v["x"].shape[1], v["ctx"].shape[1], v["x"].shape[2]
    KT = D // 128

    def columns(a):
        return np.ascontiguousarray(a.reshape(-1, 128).T)

    def blocks(w):
        k, m = w.shape
        if m % 256:
            w = np.concatenate([w, np.zeros((k, 256 - m % 256), w.dtype)], axis=1)
            m = w.shape[1]
        return w.reshape(k // 128, 128, m // 256, 256).transpose(2, 1, 0, 3).reshape(m // 256, 128, k * 2)

    def mlp(i):
        w1 = blocks(v["mlp_w1"][i])
        out = []
        for q in range(4):
            out += [w1[4 * q:4 * q + 4], blocks(v["mlp_w2"][i][q * D:(q + 1) * D])]
        return out

    stream = [blocks(v["mod_w"][0][:, :2 * D]), blocks(v["ab_w_in"][0]), blocks(v["mod_w"][0][:, 2 * D:]),
              blocks(v["mod_w"][1]), blocks(v["ab_w_out"][0])] + mlp(0) + \
             [blocks(v["conv_w_in"][0]), blocks(v["conv_w_out"][0])] + mlp(1)
    f = np.float32
    g = v["norm_g"]
    parts = dict(modb0=columns(v["mod_b"][0]), modb1=columns(v["mod_b"][1]), mu=columns(v["rwkv_mu"][0]),
                 w0=columns(v["rwkv_w0"][0]), a0=columns(v["rwkv_a0"][0]), kk=columns(v["rwkv_kk"][0]),
                 ka=columns(v["rwkv_ka"][0]), rk=columns(v["rwkv_rk"][0]), lnw=columns(v["rwkv_ln_w"][0]),
                 lnb=columns(v["rwkv_ln_b"][0]), cw=columns(v["conv_w"][0]),
                 sink=np.broadcast_to(v["att_sink"][0][None, :], (128, 8)),
                 c=np.stack([v["c"][0], v["c_ctx"]], -1).reshape(KT, 128, 2).transpose(1, 0, 2).reshape(128, 2 * KT))
    for i in range(2):
        for j in range(4):
            parts[f"g{i}{j}"] = columns(g[i, j])
    at, n = _columns(_PRM)
    prm = np.concatenate([parts[name].reshape(128, -1) for name, _ in _PRM], axis=1)
    assert prm.shape == (128, n)
    lw = np.stack([v["rwkv_w2"][0], v["rwkv_a2"][0]], 0).reshape(2, 128, 4, 128).transpose(2, 1, 0, 3)
    xT = v["x"][0].T.reshape(KT, 128, T).transpose(1, 0, 2)
    cT = v["ctx"][0].T.reshape(KT, 128, C).transpose(1, 0, 2)
    arrays = {"w": np.concatenate(stream), "prm": prm, "cst": _constants(np, T, C, _CST), "csa": _constants(np, T, C, _CSA),
              "x": xT, "ctx": cT,
              "lw": lw, "g2": v["rwkv_g2"][0]}
    arrays = {k: np.ascontiguousarray(a) for k, a in arrays.items()}
    nc = bacc.Bacc("TRN2", target_bir_lowering=False, num_devices=1)
    A = {k: nc.dram_tensor(k + "_in", a.shape, mybir.dt.from_np(a.dtype), kind="ExternalInput").ap()
         for k, a in arrays.items()}
    A["out"] = nc.dram_tensor("out_T", (128, KT, T), mybir.dt.float32, kind="ExternalOutput").ap()
    build(nc, A)
    r = run_bass_kernel_spmd(nc, [{k + "_in": a for k, a in arrays.items()}], core_ids=[0])
    o = r.results[0]["out_T"]
    return np.ascontiguousarray(o.transpose(1, 0, 2).reshape(D, T).T)[None]
```

```python
_PRM = [("modb0", 48), ("modb1", 48), ("g00", 8), ("g01", 8), ("g02", 8), ("g03", 8), ("g10", 8), ("g11", 8),
        ("g12", 8), ("g13", 8), ("mu", 15), ("w0", 8), ("a0", 8), ("kk", 4), ("ka", 4), ("rk", 4), ("lnw", 4),
        ("lnb", 4), ("cw", 24), ("sink", 8), ("c", 16)]
_CST = [("ident", 128), ("ones", 128), ("onesh", 128), ("scan", 768), ("upper", 64), ("upper_eq", 64), ("lower", 64),
        ("lvl1", 64), ("lvl1t", 64), ("eye64", 64), ("lvl", 5 * 64)]
_CSA = [("rot", 128), ("sel", 512), ("cos", 512), ("sin", 512), ("band_lo", 128), ("band_hi", 128)]


def _columns(table):
    at, out = 0, {}
    for name, n in table:
        out[name] = (at, n)
        at += n
    return out, at

def _constants(np, T, C, table):
    f = np.float32
    r, c = np.arange(128)[:, None], np.arange(128)[None, :]
    out = {"ident": r == c, "ones": np.ones((128, 128)), "onesh": r // 64 == c // 64}
    rot = np.where((c % 32 < 16) & (r == c + 16), -1.0, 0.0) + np.where((c % 32 >= 16) & (r == c - 16), 1.0, 0.0)
    out["rot"] = rot
    sel = []
    for kv in range(2):
        s = (r == kv * 64 + c % 64).astype(f)
        sel += [s, rot @ s]
    out["sel"] = np.concatenate(sel, 1)
    m = 16
    inv = (10000.0 ** (-np.arange(m, dtype=f) / m)).astype(f)
    t = np.arange(T)
    ch = np.arange(128)
    pos = np.where((ch % 64 < 32)[:, None], (t // 64)[None, :], (t % 64)[None, :]).astype(f)
    ang = (pos * inv[ch % 16][:, None]).astype(f)
    out["cos"], out["sin"] = np.cos(ang), np.sin(ang)
    out["band_lo"] = np.where(c >= r, 0.0, -1e30)
    out["band_hi"] = np.where(c <= r, 0.0, -1e30)
    out["scan"] = np.broadcast_to((np.arange(T + C) % 64 != 0)[None, :], (128, T + C))
    i, j = np.arange(128)[:, None] % 64, np.arange(64)[None, :]
    out["upper"], out["upper_eq"], out["lower"] = i < j, i <= j, i > j
    l1 = (i // 2 == j // 2) & (i > j)
    out["lvl1"], out["lvl1t"], out["eye64"] = l1, (i // 2 == j // 2) & (i < j), i == j
    out["lvl"] = np.concatenate([(i // (2 * n) == j // (2 * n)) & (i // n > j // n) for n in (2, 4, 8, 16, 32)], 1)
    return np.concatenate([np.asarray(out[name]).astype(f) for name, _ in table], axis=1)


def build(nc, A):
    from contextlib import ExitStack
    import concourse.bass as bass
    from concourse import mybir

    F32, F32R = mybir.dt.float32, mybir.dt.float32r
    ALU, ACT, AX = mybir.AluOpType, mybir.ActivationFunctionType, mybir.AxisListType
    MUL, ADD, SUB, MAX, MIN = ALU.mult, ALU.add, ALU.subtract, ALU.max, ALU.min

    P = 128
    T = A["x"].shape[2]
    C = A["ctx"].shape[2]
    KT = A["x"].shape[1]
    N = C + T
    D = KT * P
    EPS, GN_EPS = 1e-6, 64e-5
    DECAY = 0.6065306597126334
    HD = 64
    PAIRS = 4
    Q = 64
    G = 2 * N // P
    GD = N // P
    GC = C // P
    NBLK = A["w"].shape[0]
    S_MOD0A, S_IN, S_MOD, S_OUT, S_MLP0, S_CIN, S_COUT, S_MLP1 = 0, 8, 19, 59, 63, 95, 107, 111
    assert NBLK == S_MLP1 + 32

    prm_at, NPRM = _columns(_PRM)
    cst_at, NCST = _columns(_CST)
    csa_at, NCSA = _columns(_CSA)
    top = ExitStack()

    taken = {}

    def own(name):
        taken[name] = taken.get(name, 0) + 1
        return name if taken[name] == 1 else f"{name}_{taken[name]}"

    def sb(stack, name, shape, dt=F32):
        return stack.enter_context(nc.sbuf_tensor(own(name), shape, dt))

    def sems(stack, *names):
        return [stack.enter_context(nc.semaphore(own(n))) for n in names]

    class Chain:

        def __init__(self, eng, sem):
            self.eng, self.sem, self.n = eng, sem, 0

        def __call__(self, ins):
            self.n += 1
            ins.then_inc(self.sem, 1)
            self.eng.wait_ge(self.sem, self.n)

    cst = sb(top, "cst", [P, NCST])
    prm = sb(top, "prm", [P, NPRM])
    x = sb(top, "xres", [P, KT, T])
    yb = sb(top, "yb", [P, KT, T])
    raw = [sb(top, f"raw{s}", [P, KT, 256]) for s in range(2)]
    mod0 = sb(top, "mod0", [P, 16, 2])
    mod = sb(top, "mod", [P, 96])
    cs = sb(top, "cs", [P, KT, 2])
    nsc = sb(top, "nsc", [P, 4, KT])
    small = sb(top, "small", [P, 64])
    psum = [top.enter_context(nc.psum_tensor(f"bank{i}", [P, 1024], F32)) for i in range(4)]

    def bank(i, lo=0, hi=512):
        return psum[i // 2][:, (i % 2) * 512 + lo:(i % 2) * 512 + hi]

    def K(name, lo=0, hi=None):
        a, n = cst_at[name]
        return cst[:, a + lo:a + (n if hi is None else hi)]

    def KA(name):
        a, n = csa_at[name]
        return csa[:, a:a + n]

    def R(name, lo=0, hi=None):
        a, n = prm_at[name]
        return prm[:, a + lo:a + (n if hi is None else hi)]

    raw_loaded = sems(top, "raw_loaded0", "raw_loaded1")
    hi_ready = sems(top, "hi_ready0", "hi_ready1")
    split_ready = sems(top, "split_ready0", "split_ready1")
    mod_used = sems(top, "mod_used0", "mod_used1")
    tile_done = [sems(top, f"tile_done{s}0", f"tile_done{s}1") for s in range(2)]
    tile_free = [sems(top, f"tile_free{s}0", f"tile_free{s}1") for s in range(2)]

    def is_mod(n):
        return n < S_IN or S_MOD <= n < S_OUT

    def nth(n):
        return sum(is_mod(m) == is_mod(n) for m in range(n % 2, n + 1, 2))

    def clear(stack_sems):
        with nc.Block() as block:
            @block.gpsimd
            def _(pool):
                for s in stack_sems:
                    pool.sem_clear(s)

    def keep_warm(n, out, width=512):
        for _ in range(n):
            nc.tensor.matmul(out[:, 0:width], K("ones"), cst[:, 0:width], start=True, stop=True)

    def sp_load(sp, n, up=0):
        sp.dma_start(raw[n % 2][:].rearrange("p k m -> p (k m)"), A["w"][n + up]).then_inc(raw_loaded[n % 2], 16)

    def sp_next(sp, n, up=0):
        if is_mod(n):
            sp.wait_ge(mod_used[n % 2], nth(n) + up // 2)
        else:
            sp.wait_ge(split_ready[n % 2], nth(n) + up // 2)
        sp_load(sp, n + 2, up)

    def act_hi(act, n, W, up=0):
        act.wait_ge(raw_loaded[n % 2], 16 * (n // 2 + 1) + 8 * up)
        if nth(n) > 1:
            act.wait_ge(tile_done[n % 2][1], nth(n) - 1 + up // 2)
        nc.scalar.activation(W[0][n % 2][:], raw[n % 2][:], ACT.Copy).then_inc(hi_ready[n % 2], 1)

    def dve_hi(dve, n, W):
        dve.wait_ge(raw_loaded[n % 2], 16 * (n // 2 + 1))
        dve.wait_ge(tile_done[n % 2][1], nth(n) - 1)
        nc.vector.tensor_copy(W[0][n % 2][:], raw[n % 2][:]).then_inc(hi_ready[n % 2], 1)

    def pool_lo(pool, n, W, up=0):
        pool.wait_ge(hi_ready[n % 2], nth(n) + up // 2)
        nc.gpsimd.tensor_tensor(W[1][n % 2][:], raw[n % 2][:], W[0][n % 2][:].bitcast(F32), SUB)\
            .then_inc(split_ready[n % 2], 1)

    def pe_block(pe, n, W, H, up=0, tiles=2, parts=(), ready=None):
        s = n % 2
        pe.wait_ge(split_ready[s], nth(n) + up // 2)
        for m in range(tiles):
            if nth(n) > 1:
                pe.wait_ge(tile_free[s][m], nth(n) - 1 + up // 2)
            for k in range(KT):
                if ready is not None and m == 0:
                    pe.wait_ge(*ready(k))
                for w, h in ((0, 0), (0, 1), (1, 0)):
                    for b, (lo, hi) in parts:
                        last = nc.tensor.matmul(bank(b(s, m), 0, hi - lo), W[w][s][:, k, m * P:(m + 1) * P],
                                                H[h][:, k, lo:hi], start=(k == 0 and w == h == 0),
                                                stop=(k == KT - 1 and w == 1))
            last.then_inc(tile_done[s][m], 1)

    def clear_then_block(stack_sems):
        clear(stack_sems)
        return nc.Block()

    mix = ExitStack()
    qT, rT = yb[:, 0:PAIRS, :], yb[:, PAIRS:KT, :]
    attT = qT
    kT = sb(mix, "kT", [P, PAIRS, N])
    vT = sb(mix, "vT", [P, PAIRS, N])
    lora = sb(mix, "lora", [P, 2, N])
    gT = sb(mix, "gT", [P, T])
    kkT = sb(mix, "kkT", [P, PAIRS, N])
    lw = sb(mix, "lw", [P, PAIRS, 2, P])
    att_in = ExitStack()
    csa = sb(att_in, "csa", [P, NCSA])
    kvT = sb(att_in, "kvT", [P, 2, N])
    proj = ExitStack()
    hT = [sb(proj, f"h{i}", [P, KT, N], F32R) for i in range(2)]
    W = [[sb(proj, f"w{i}{s}", [P, KT, 256], F32R) for s in range(2)] for i in range(2)]
    both = ((lambda s, m: 2 * (2 * s + m), (C, N)), (lambda s, m: 2 * (2 * s + m) + 1, (0, C)))
    with ExitStack() as st:
        ctxT = kkT[:].rearrange("p a n -> p (a n)")[:, 0:KT * C].rearrange("p (k c) -> p k c", c=C)
        sq, rst = [kT[:, i, :] for i in range(2)], kT[:, 2, :]
        hf = [vT[:, i, :] for i in range(4)]
        rows = yb[:].rearrange("p k t -> p (k t)")[0:2, 0:S_IN * 256]
        S = sems(st, "const_in", "x_in", "csig", "cs_ready", "eps_ready", "mod_ready", "sq_ready", "sq_used",
                 "ssum_done", "root_ready", "row_copied", "col_done", "hf_ready", "hs_ready", "hhi_ready", "h_even",
                 "h_odd", "dve_chain")
        (const_in, x_in, csig, cs_ready, eps_ready, mod_ready, sq_ready, sq_used, ssum_done, root_ready,
         row_copied, col_done, hf_ready, hs_ready, hhi_ready, h_even, h_odd, dve_chain) = S
        h_ready = (h_even, h_odd)
        streams = ((1, 0, C), (0, C, N))

        with nc.Block() as block:
            @block.sync
            def _(sp):
                sp.dma_start(prm[:], A["prm"]).then_inc(const_in, 16)
                sp_load(sp, 0)
                sp_load(sp, 1)
                with sp.Fori(0, S_IN // 2) as turn:
                    n = 2 * turn
                    for s in range(2):
                        sp_next(sp, s, n)
                sp_next(sp, S_IN)

            @block.scalar
            def _(act):
                act.dma_start(x[:], A["x"]).then_inc(x_in, 16)
                act.dma_start(ctxT, A["ctx"]).then_inc(x_in, 16)
                act.dma_start(cst[:], A["cst"]).then_inc(x_in, 16)
                act.wait_ge(const_in, 16)
                nc.scalar.activation(cs[:].rearrange("p k c -> p (k c)"), R("c"), ACT.Sigmoid).then_inc(csig, 1)
                act.wait_ge(x_in, 48)
                for k in range(KT):
                    if k >= 2:
                        act.wait_ge(sq_used, k - 1)
                    nc.scalar.activation(sq[k % 2][:, 0:C], ctxT[:, k], ACT.Square)
                    nc.scalar.activation(sq[k % 2][:, C:N], x[:, k], ACT.Square).then_inc(sq_ready, 1)
                act.wait_ge(ssum_done, 1)
                act.wait_ge(eps_ready, 1)
                nc.scalar.activation(rst[:, 0:C], bank(3, 0, C), ACT.Sqrt, bias=small[:, 0:1], scale=1.0 / D)
                nc.scalar.activation(rst[:, C:N], bank(2), ACT.Sqrt, bias=small[:, 0:1], scale=1.0 / D)\
                    .then_inc(root_ready, 1)
                for i in range(S_IN // 2):
                    for s in range(2):
                        act.wait_ge(mod_used[s], i + 1)
                    nc.scalar.activation(rows[:, 512 * i:512 * (i + 1)], bank(4 + i)[0:2], ACT.Copy)\
                        .then_inc(row_copied, 1)
                act.wait_ge(mod_ready, 1)
                for k in range(KT):
                    if k == KT // 2:
                        act_hi(act, S_IN, W)
                    act.wait_ge(hf_ready, k + 1)
                    odd = k % 2
                    for c, lo, hi in streams:
                        i = nc.scalar.activation((hf[k % 4] if odd else hT[0][:, k])[:, lo:hi], hf[k % 4][:, lo:hi],
                                                 ACT.Identity, bias=mod0[:, k, c:c + 1], scale=1.0)
                    if odd:
                        i.then_inc(hs_ready, 1)
                        act.wait_ge(hs_ready, k // 2 + 1)
                        i = nc.scalar.activation(hT[0][:, k], hf[k % 4], ACT.Copy)
                    i.then_inc(hhi_ready, 1)
                act_hi(act, S_IN + 1, W)

            @block.tensor
            def _(pe):
                def modulation(n):
                    pe.wait_ge(raw_loaded[n % 2], 16 * (n // 2 + 1))
                    at = (n % 2) * 256
                    for k in range(KT):
                        last = nc.tensor.matmul(bank(4 + n // 2, at, at + 256)[0:2], cs[:, k, :], raw[n % 2][:, k, :],
                                                start=k == 0, stop=k == KT - 1)
                    last.then_inc(mod_used[n % 2], 1)

                pe.wait_ge(cs_ready, 1)
                modulation(0)
                modulation(1)
                pe.wait_ge(x_in, 48)
                for k in range(KT):
                    pe.wait_ge(sq_ready, k + 1)
                    nc.tensor.matmul(bank(2), K("ones"), sq[k % 2][:, C:N], start=k == 0, stop=k == KT - 1)
                    nc.tensor.matmul(bank(3, 0, C), K("ones"), sq[k % 2][:, 0:C], start=k == 0, stop=k == KT - 1)\
                        .then_inc(sq_used if k < KT - 1 else ssum_done, 1)
                for n in range(2, S_IN):
                    modulation(n)
                for t in range(2 * S_IN):
                    pe.wait_ge(row_copied, t // 4 + 1)
                    last = nc.tensor.transpose(bank(1, 2 * t, 2 * t + 2), rows[:, t * P:(t + 1) * P],
                                               K("ident", 0, 2)[0:2])
                last.then_inc(col_done, 1)
                keep_warm(6, bank(6))
                pe.wait_ge(root_ready, 1)
                pe_block(pe, S_IN, W, hT, parts=both[:1], ready=lambda k: (h_ready[k % 2], k // 2 + 1))

            @block.vector
            def _(dve):
                link = Chain(dve, dve_chain)
                nc.vector.memset(small[:, 0:1], EPS)
                nc.vector.memset(small[:, 1:2], GN_EPS).then_inc(eps_ready, 1)
                dve.wait_ge(csig, 1)
                link(nc.vector.tensor_tensor(cs[:].rearrange("p k c -> p (k c)"), cs[:].rearrange("p k c -> p (k c)"),
                                             R("c"), MUL))
                dve.sem_inc(cs_ready, 1)
                dve.wait_ge(root_ready, 1)
                link(nc.vector.reciprocal(rst, rst))
                dve.wait_ge(col_done, 1)
                link(nc.vector.tensor_tensor(mod0[:], bank(1, 0, 32).rearrange("p (m c) -> p m c", c=2),
                                             R("modb0", 0, 16).unsqueeze(2).to_broadcast([P, 16, 2]), ADD))
                dve.sem_inc(mod_ready, 1)
                for c in range(2):
                    link(nc.vector.scalar_tensor_tensor(nsc[:, c, :], mod0[:, 8:16, c], 1.0, R("g00"), ADD, MUL))

                def scaled(k):
                    if k >= 4:
                        dve.wait_ge(h_ready[k % 2], (k - 4) // 2 + 1)
                    nc.vector.scalar_tensor_tensor(hf[k % 4][:, 0:C], ctxT[:, k], nsc[:, 1, k:k + 1], rst[:, 0:C],
                                                   MUL, MUL)
                    nc.vector.scalar_tensor_tensor(hf[k % 4][:, C:N], x[:, k], nsc[:, 0, k:k + 1], rst[:, C:N],
                                                   MUL, MUL).then_inc(hf_ready, 1)

                scaled(0)
                for k in range(0, KT, 2):
                    for j in (k + 1, k + 2):
                        if j < KT:
                            scaled(j)
                    dve.wait_ge(hhi_ready, k + 1)
                    for c, lo, hi in streams:
                        i = nc.vector.scalar_tensor_tensor(hT[1][:, k, lo:hi], hf[k % 4][:, lo:hi],
                                                           mod0[:, k, c:c + 1], hT[0][:, k, lo:hi].bitcast(F32), ADD,
                                                           SUB)
                    i.then_inc(h_even, 1)

            @block.gpsimd
            def _(pool):
                for k in range(1, KT, 2):
                    if k == 5:
                        pool_lo(pool, S_IN, W)
                    pool.wait_ge(hhi_ready, k + 1)
                    nc.gpsimd.tensor_tensor(hT[1][:, k], hf[k % 4], hT[0][:, k].bitcast(F32), SUB)\
                        .then_inc(h_odd, 1)
                pool_lo(pool, S_IN + 1, W)

    with ExitStack() as st:
        pad = [sb(st, f"pad{i}", [P, N + 4]) for i in range(2)]
        nb = sb(st, "nb", [P, N + 2])
        mus = small[:, 2:32].rearrange("p (a j) -> p a j", a=2)
        S = sems(st, "later_in", "mus_ready", "pad_ready", "pad_used", "mixed", "dve_chain")
        later_in, mus_ready, pad_ready, pad_used, mixed, dve_chain = S
        dest = [(qT[:, i, :], C) for i in range(4)] + [(kvT[:, i, :], 0) for i in range(2)] \
            + [(rT[:, i, :], C) for i in range(4)] + [(kT[:, i, :], 0) for i in range(4)] \
            + [(vT[:, i, :], 0) for i in range(4)] + [(lora[:, i, :], 0) for i in range(2)] + [(gT[:], C)]
        NB = S_MOD - S_IN

        def acc(n, m, lo, hi):
            t = psum[2 * (n % 2) + m]
            return t[:, 512 + lo:512 + hi] if lo < C else t[:, lo - C:hi - C]

        with clear_then_block(S) as block:
            @block.sync
            def _(sp):
                sp.dma_start(csa[:], A["csa"]).then_inc(later_in, 16)
                for i in range(PAIRS):
                    sp.dma_start(lw[:, i], A["lw"][i]).then_inc(later_in, 16)
                with sp.Fori(0, (NB - 1) // 2) as turn:
                    up = 2 * turn
                    for j in range(2):
                        sp_next(sp, S_IN + 1 + j, up)
                sp.wait_ge(later_in, 16 * (PAIRS + 1))

            @block.tensor
            def _(pe):
                pe_block(pe, S_IN + 1, W, hT, parts=both[:1])
                with pe.Fori(0, (NB - 3) // 2) as turn:
                    up = 2 * turn
                    for j in range(2):
                        pe_block(pe, S_IN + 2 + j, W, hT, up=up, parts=both)
                pe_block(pe, S_MOD - 1, W, hT, tiles=1, parts=both[:1])
                pe.sem_inc(tile_done[(S_MOD - 1) % 2][1], 1)

            @block.gpsimd
            def _(pool):
                with pool.Fori(0, (NB - 3) // 2) as turn:
                    up = 2 * turn
                    for j in range(2):
                        pool_lo(pool, S_IN + 2 + j, W, up)
                pool_lo(pool, S_MOD - 1, W)

            @block.scalar
            def _(act):
                for n in range(S_IN, S_MOD):
                    for m in range(2):
                        t = 2 * (n - S_IN) + m
                        if t > 20:
                            act.sem_inc(tile_free[n % 2][1], 1)
                            continue
                        act.wait_ge(tile_done[n % 2][m], nth(n))
                        d, first = dest[t]
                        segs = ((0, C), (C, N))[first > 0:]
                        if t < 6:
                            for lo, hi in segs:
                                i = nc.scalar.activation(d[:, lo - first:hi - first], acc(n, m, lo, hi), ACT.Copy)
                        else:
                            j = t - 6
                            if j == 0:
                                act.wait_ge(mus_ready, 1)
                            if j >= 2:
                                act.wait_ge(pad_used, j - 1)
                            for lo, hi in segs:
                                o = 1 + 2 * (lo > 0)
                                i = nc.scalar.activation(pad[j % 2][:, o + lo:o + hi], acc(n, m, lo, hi), ACT.Copy)
                            i.then_inc(pad_ready, 1)
                            for lo, hi in segs:
                                i = nc.scalar.activation(d[:, lo - first:hi - first], acc(n, m, lo, hi), ACT.Copy,
                                                         scale=mus[:, 0, j:j + 1])
                        i.then_inc(tile_free[n % 2][m], 1)
                    if n + 2 < S_MOD:
                        act_hi(act, n + 2, W)
                act.wait_ge(mixed, 15)
                nc.scalar.activation(lora[:, 0, :], lora[:, 0, :], ACT.Tanh)
                nc.scalar.activation(gT[:], gT[:], ACT.Sigmoid)

            @block.vector
            def _(dve):
                link = Chain(dve, dve_chain)
                for i in range(2):
                    nc.vector.memset(pad[i][:], 0.0)
                nc.vector.tensor_scalar(mus[:, 1, :], R("mu"), 0.5, None, MUL)
                link(nc.vector.tensor_scalar(mus[:, 0, :], R("mu"), -1.0, 1.0, MUL, ADD))
                dve.sem_inc(mus_ready, 1)
                for j in range(15):
                    n, m = S_IN + (j + 6) // 2, j % 2
                    d, first = dest[j + 6]
                    segs = ((0, C), (C, N))[first > 0:]
                    dve.wait_ge(pad_ready, j + 1)
                    if j:
                        dve.wait_ge(mixed, j)
                    a = segs[0][0] + (2 if first else 0)
                    link(nc.vector.tensor_tensor(nb[:, a:N + 2], pad[j % 2][:, a:N + 2],
                                                 pad[j % 2][:, a + 2:N + 4], ADD))
                    dve.sem_inc(pad_used, 1)
                    dve.wait_ge(tile_free[n % 2][m], nth(n))
                    for lo, hi in segs:
                        o = 2 * (lo > 0)
                        i = nc.vector.scalar_tensor_tensor(d[:, lo - first:hi - first], nb[:, o + lo:o + hi],
                                                           mus[:, 1, j:j + 1], d[:, lo - first:hi - first], MUL, ADD)
                    i.then_inc(mixed, 1)
    proj.close()

    vtok = sb(att_in, "vtok", [P, GD, P])
    nrm = sb(att_in, "knorm", [P, PAIRS, N])
    with ExitStack() as st:
        sq = [sb(st, f"ksq{i}", [P, N]) for i in range(2)]
        S = sems(st, "ksq_ready", "knorm_sum", "knorm_used", "vt_done", "dve_chain")
        ksq_ready, knorm_sum, knorm_used, vt_done, dve_chain = S
        with clear_then_block(S) as block:
            @block.tensor
            def _(pe):
                for g in range(GD):
                    last = nc.tensor.transpose(psum[3][:, g * P:(g + 1) * P], kvT[:, 1, g * P:(g + 1) * P], K("ident"))
                last.then_inc(vt_done, 1)
                for p in range(PAIRS):
                    pe.wait_ge(ksq_ready, p + 1)
                    if p >= 2:
                        pe.wait_ge(knorm_used, p - 1)
                    for lo, hi in ((0, 512), (512, N)):
                        last = nc.tensor.matmul(psum[1 + p % 2][:, lo:hi], K("onesh"), sq[p % 2][:, lo:hi],
                                                start=True, stop=True)
                    last.then_inc(knorm_sum, 1)

            @block.scalar
            def _(act):
                for p in range(PAIRS):
                    act.wait_ge(knorm_sum, p + 1)
                    nc.scalar.activation(nrm[:, p, :], psum[1 + p % 2][:, 0:N], ACT.Sqrt).then_inc(knorm_used, 1)
                act.wait_ge(vt_done, 1)
                nc.scalar.activation(vtok[:].rearrange("p g c -> p (g c)"), psum[3][:, 0:N], ACT.Copy)

            @block.vector
            def _(dve):
                link = Chain(dve, dve_chain)
                for p in range(PAIRS):
                    if p >= 2:
                        dve.wait_ge(knorm_sum, p - 1)
                    nc.vector.tensor_scalar(kkT[:, p, :], kT[:, p, :], R("kk", p, p + 1), None, MUL)
                    link(nc.vector.tensor_scalar(sq[p % 2][:], kT[:, p, :], R("kk", p, p + 1), None, MUL))
                    nc.vector.tensor_tensor(sq[p % 2][:], sq[p % 2][:], sq[p % 2][:], MUL).then_inc(ksq_ready, 1)
                for p in range(PAIRS):
                    dve.wait_ge(knorm_used, p + 1)
                    nc.vector.tensor_scalar(nrm[:, p, :], nrm[:, p, :], 1e-12, None, MAX)

    NQ = T // P
    with ExitStack() as st:
        selS = sb(st, "selS", [P, 2, P])
        kd = sb(st, "kd", [P, N])
        vS = sb(st, "vS", [P, GD, HD])
        qs = [sb(st, f"qs{i}", [P, T]) for i in range(2)]
        tmp = [sb(st, f"rot{i}", [P, T]) for i in range(2)]
        pr = [sb(st, f"prob{i}", [P, 5 * P]) for i in range(2)]
        pt = [sb(st, f"probT{i}", [P, 5 * P]) for i in range(2)]
        oS = sb(st, "oS", [P, 2, NQ, P])
        mx, nmx, rs, es, den = (sb(st, n, [P, 4]) for n in ("mx", "nmx", "rs", "es", "den"))
        sinks = sb(st, "sinks", [P, 2, 4])
        S = sems(st, "sel_ready", "kd_done", "q_done", "kd_ready", "q_ready", "vs_ready", "s_done", "banded",
                 "max_ready", "exp_ready", "pt_done", "pt_ready", "o_done", "o_ready", "ot_done", "inv_ready",
             "dve_chain")
        (sel_ready, kd_done, q_done, kd_ready, q_ready, vs_ready, s_done, banded, max_ready, exp_ready, pt_done,
         pt_ready, o_done, o_ready, ot_done, inv_ready, dve_chain) = S
        units = [(i, b, h) for i in range(2) for b in range(NQ) for h in range(2)]
        NU = len(units)
        SLICE = PAIRS * N // (2 * NU)
        nrm_flat, kk_flat = (t[:].rearrange("p a n -> p (a n)") for t in (nrm, kkT))

        def keys(b):
            return [j for j in (b - 1, b, b + 1) if 0 <= j < NQ]

        def width(u):
            return (2 + len(keys(units[u][1]))) * P

        def transposed_at(u, c):
            return bank(4 + u % 2, c * P, (c + 1) * P) if c < 4 else bank(6 + u % 2, 0, P)

        def out_at(u):
            return bank(6 + u % 2, P, P + HD)

        with nc.Fori(0, 2) as kv:
            with clear_then_block(S) as block:
                @block.scalar
                def _(act):
                    nc.scalar.activation(selS[:].rearrange("p a c -> p (a c)"),
                                         csa[:, bass.ds(csa_at["sel"][0] + kv * 256, 256)], ACT.Copy)\
                        .then_inc(sel_ready, 1)
                    nc.scalar.activation(vS[:], vtok[:, :, bass.ds(kv * HD, HD)], ACT.Copy).then_inc(vs_ready, 1)
                    act.wait_ge(kd_done, 1)
                    nc.scalar.activation(kd[:, 0:C], psum[0][:, 0:C], ACT.Copy).then_inc(sel_ready, 1)

                    def exponentials(u):
                        i, b, h = units[u]
                        e = u % 4
                        act.wait_ge(max_ready, u + 1)
                        if u >= 2:
                            act.wait_ge(pt_done, u - 1)
                        if u >= 4:
                            act.wait_ge(o_ready, u - 3)
                        nc.scalar.activation(pr[u % 2][:, 0:width(u)], psum[u % 2][:, 0:width(u)], ACT.Exp,
                                             bias=nmx[:, e:e + 1], scale=HD ** -0.5,
                                             accum_out=rs[:, e:e + 1]).then_inc(exp_ready, 1)
                        nc.scalar.activation(es[:, e:e + 1], sinks[:, 0, 2 * i + h:2 * i + h + 1], ACT.Exp,
                                             bias=nmx[:, e:e + 1], scale=1.0).then_inc(exp_ready, 1)

                    def transposed(u):
                        act.wait_ge(pt_done, u + 1)
                        if u >= 2:
                            act.wait_ge(o_done, u - 1)
                        n = width(u) // P
                        i = nc.scalar.activation(pt[u % 2][:, 0:min(n, 4) * P], bank(4 + u % 2, 0, min(n, 4) * P),
                                                 ACT.Copy)
                        if n == 5:
                            i = nc.scalar.activation(pt[u % 2][:, 4 * P:5 * P], transposed_at(u, 4), ACT.Copy)
                        i.then_inc(pt_ready, 1)

                    for u in range(NU + 1):
                        if u < NU:
                            exponentials(u)
                        if u >= 1:
                            transposed(u - 1)

                @block.gpsimd
                def _(pool):
                    for u in range(NU):
                        pool.wait_ge(inv_ready, u + 1)
                        at = bass.ds(kv * (NU * SLICE) + u * SLICE, SLICE)
                        nc.gpsimd.tensor_tensor(kk_flat[:, at], kk_flat[:, at], nrm_flat[:, at], MUL)

                @block.tensor
                def _(pe):
                    pe.wait_ge(sel_ready, 1)
                    for lo, hi in ((0, C), (C, 512), (512, N)):
                        nc.tensor.matmul(psum[0][:, lo:hi], selS[:, 0, :], kvT[:, 0, lo:hi], start=True, stop=True)
                    for a, lo, hi in ((0, C, 512), (256, 512, N)):
                        last = nc.tensor.matmul(psum[1][:, a:a + hi - lo], selS[:, 1, :], kvT[:, 0, lo:hi],
                                                start=True, stop=True)
                    last.then_inc(kd_done, 1)
                    for i in range(2):
                        last = nc.tensor.matmul(bank(4 + i), KA("rot"), qT[:, 2 * kv + i, :], start=True,
                                                stop=True)
                        last.then_inc(q_done, 1)

                    keep_warm(6, bank(6))

                    def scores(u):
                        i, b, h = units[u]
                        r = slice(h * HD, (h + 1) * HD)
                        lhs = qs[i][r, b * P:(b + 1) * P]
                        js = keys(b)
                        if u % (2 * NQ) == 0:
                            pe.wait_ge(q_ready, i + 1)
                        t = psum[u % 2]
                        nc.tensor.matmul(t[:, 0:C], lhs, kd[r, 0:C], start=True, stop=True)
                        at = C + js[0] * P
                        n0 = min(len(js) * P, 512 - C)
                        last = nc.tensor.matmul(t[:, C:C + n0], lhs, kd[r, at:at + n0], start=True, stop=True)
                        if len(js) == 3:
                            last = nc.tensor.matmul(t[:, 512:512 + P], lhs, kd[r, at + n0:at + n0 + P], start=True,
                                                    stop=True)
                        last.then_inc(s_done, 1)

                    def products(u):
                        i, b, h = units[u]
                        n = width(u) // P
                        pe.wait_ge(pt_ready, u + 1)
                        for c in range(n):
                            g = c if c < 2 else GC + keys(b)[c - 2]
                            last = nc.tensor.matmul(out_at(u), pt[u % 2][:, c * P:(c + 1) * P], vS[:, g, :],
                                                    start=c == 0, stop=c == n - 1)
                        last.then_inc(o_done, 1)

                    pe.wait_ge(kd_ready, 1)
                    scores(0)
                    scores(1)
                    pe.wait_ge(q_ready, 2)
                    pe.wait_ge(vs_ready, 1)
                    keep_warm(4, bank(6))
                    for u in range(NU):
                        if u in (1, 2):
                            keep_warm(2, bank(7))
                        pe.wait_ge(exp_ready, 2 * u + 1)
                        n = width(u) // P
                        if u >= 2:
                            pe.wait_ge(pt_ready, u - 1)
                        for c in range(4):
                            last = nc.tensor.transpose(transposed_at(u, c), pr[u % 2][:, c * P:(c + 1) * P],
                                                       K("ident"))
                        if n == 4:
                            last.then_inc(pt_done, 1)
                        if u + 2 < NU:
                            scores(u + 2)
                        if u >= 2:
                            pe.wait_ge(o_ready, u - 1)
                        if n == 5:
                            nc.tensor.transpose(transposed_at(u, 4), pr[u % 2][:, 4 * P:5 * P], K("ident"))\
                                .then_inc(pt_done, 1)
                        if u >= 1:
                            products(u - 1)
                    products(NU - 1)
                    for i in range(2):
                        pe.wait_ge(o_ready, NU)
                        for b in range(NQ):
                            last = nc.tensor.transpose(bank(i, b * P, (b + 1) * P), oS[:, i, b, :], K("ident"))
                        last.then_inc(ot_done, 1)

                @block.vector
                def _(dve):
                    link = Chain(dve, dve_chain)
                    nc.vector.tensor_copy(sinks[:, 0, :], prm[:, bass.ds(prm_at["sink"][0] + kv * 4, 4)])\
                        .then_inc(banded, 1)
                    link(nc.vector.tensor_scalar(sinks[:, 1, :], prm[:, bass.ds(prm_at["sink"][0] + kv * 4, 4)], -1.0,
                                                 None, MUL))
                    dve.wait_ge(kd_done, 1)
                    dve.wait_ge(sel_ready, 2)
                    nc.vector.tensor_tensor(tmp[0][:], psum[0][:, C:N], KA("cos"), MUL)
                    link(nc.vector.tensor_tensor(tmp[1][:], psum[1][:, 0:T], KA("sin"), MUL))
                    link(nc.vector.tensor_tensor(kd[:, C:N], tmp[0][:], tmp[1][:], ADD))
                    dve.sem_inc(kd_ready, 1)
                    for i in range(2):
                        dve.wait_ge(q_done, i + 1)
                        nc.vector.tensor_tensor(tmp[0][:], qT[:, 2 * kv + i, :], KA("cos"), MUL)
                        link(nc.vector.tensor_tensor(tmp[1][:], bank(4 + i), KA("sin"), MUL))
                        link(nc.vector.tensor_tensor(qs[i][:], tmp[0][:], tmp[1][:], ADD))
                        dve.sem_inc(q_ready, 1)

                    bands = [1]

                    def maximum(u):
                        i, b, h = units[u]
                        e, t = u % 4, psum[u % 2]
                        dve.wait_ge(s_done, u + 1)
                        for c, j in enumerate(keys(b)):
                            if j != b:
                                a = C + c * P
                                nc.vector.tensor_tensor(t[:, a:a + P], t[:, a:a + P],
                                                        KA("band_lo" if j < b else "band_hi"), ADD)\
                                    .then_inc(banded, 1)
                                bands[0] += 1
                        dve.wait_ge(banded, bands[0])
                        link(nc.vector.reduce_max(mx[:, e:e + 1], t[:, 0:width(u)], AX.X))
                        nc.vector.tensor_scalar(nmx[:, e:e + 1], mx[:, e:e + 1], -(HD ** -0.5),
                                                sinks[:, 1, 2 * i + h:2 * i + h + 1], MUL, MIN)\
                            .then_inc(max_ready, 1)

                    def denominator(u):
                        e = u % 4
                        dve.wait_ge(exp_ready, 2 * u + 2)
                        link(nc.vector.tensor_tensor(den[:, e:e + 1], rs[:, e:e + 1], es[:, e:e + 1], ADD))
                        link(nc.vector.reciprocal(den[:, e:e + 1], den[:, e:e + 1]))

                    def output(u):
                        i, b, h = units[u]
                        e = u % 4
                        dve.wait_ge(o_done, u + 1)
                        nc.vector.tensor_scalar(oS[:, i, b, h * HD:(h + 1) * HD], out_at(u), den[:, e:e + 1], None,
                                                MUL).then_inc(o_ready, 1)

                    maximum(0)
                    maximum(1)
                    for u in range(NU):
                        s = nrm_flat[:, bass.ds(kv * (NU * SLICE) + u * SLICE, SLICE)]
                        nc.vector.reciprocal(s, s).then_inc(inv_ready, 1)
                        denominator(u)
                        if u + 2 < NU:
                            maximum(u + 2)
                        if u >= 1:
                            output(u - 1)
                    output(NU - 1)
                    for i in range(2):
                        dve.wait_ge(ot_done, i + 1)
                        nc.vector.tensor_copy(attT[:, 2 * kv + i, :], bank(i))
    att_in.close()

    NCH = 2 * N // Q
    ND = N // Q
    TURNS = (S_OUT - S_MOD) // PAIRS // 2
    WARM = 192
    LVL = 5
    drw = ExitStack()
    lws = sb(drw, "lws", [P, 2, P])
    vs = sb(drw, "vs", [P, 2, N])
    AR = sb(drw, "AR", [P, G, 2, P])
    bt = sb(drw, "bt", [P, 2, N])
    kt = sb(drw, "kt", [P, 2, N])
    PC = sb(drw, "PC", [P, NCH])

    def chunked(ap):
        return ap.rearrange("p (n t) -> p n t", t=Q)

    def tiled(ap):
        return ap.rearrange("p (g t) -> p g t", t=P)

    with nc.Fori(0, PAIRS) as p:
        with ExitStack() as st:
            names = ("sg", "cum", "al", "Pp", "Pn", "Pv", "kp", "bb")
            sg, cum, al, Pp, Pn, Pv, kp, bb = (sb(st, n, [P, 2, N]) for n in names)
            oka = sb(st, "oka", [P, 1])
            kkS, rS = sb(st, "kkS", [P, N]), sb(st, "rS", [P, T])
            S = sems(st, "lw_in", "lora_done", "sig_ready", "cum_ready", "exc_ready", "exp_ready",
                     "bb_ready", "own_ready", "vs_ready", "bsum_in", "bsum_done", "dve_chain")
            (lw_in, lora_done, sig_ready, cum_ready, exc_ready, exp_ready, bb_ready, own_ready, vs_ready,
             bsum_in, bsum_done, dve_chain) = S
            with clear_then_block(S) as block:
                @block.tensor
                def _(pe):
                    pe.wait_ge(lw_in, 1)
                    for kind in range(2):
                        for d in range(2):
                            r = slice(d * HD, (d + 1) * HD)
                            for lo, hi in ((0, 512), (512, N)):
                                last = nc.tensor.matmul(psum[2 * kind + d][:, lo:hi], lws[r, kind, :],
                                                        lora[r, kind, lo:hi], start=True, stop=True)
                            last.then_inc(lora_done, 1)
                    pe.wait_ge(exp_ready, 1)
                    pe.wait_ge(sig_ready, 4)
                    keep_warm(5, bank(7))
                    pe.wait_ge(bsum_in, 1)
                    nc.tensor.matmul(bank(0), K("onesh"), bb[:, 0, 0:T], start=True, stop=True).then_inc(bsum_done, 1)
                    keep_warm(2, bank(7))

                @block.scalar
                def _(act):
                    nc.scalar.activation(lws[:], lw[:, p], ACT.Copy).then_inc(lw_in, 1)
                    for kind, (dst, bias) in enumerate(((sg, "w0"), (al, "a0"))):
                        for d in range(2):
                            act.wait_ge(lora_done, 2 * kind + d + 1)
                            nc.scalar.activation(dst[:, d, :], psum[2 * kind + d][:, 0:N], ACT.Sigmoid,
                                                 bias=prm[:, bass.ds(prm_at[bias][0] + 4 * d + p, 1)])\
                                .then_inc(sig_ready, 1)
                    act.wait_ge(cum_ready, 1)
                    nc.scalar.activation(Pn[:], cum[:], ACT.Exp, scale=DECAY).then_inc(exp_ready, 1)
                    nc.scalar.activation(Pp[:], cum[:], ACT.Exp, scale=-DECAY).then_inc(exp_ready, 1)
                    nc.scalar.activation(rS[:], rT[:, p, :], ACT.Copy)
                    nc.scalar.activation(kkS[:], kkT[:, p, :], ACT.Copy).then_inc(own_ready, 1)
                    act.wait_ge(exc_ready, 1)
                    nc.scalar.activation(Pv[:], sg[:], ACT.Exp, scale=-DECAY).then_inc(exp_ready, 1)
                    nc.scalar.activation(vs[:, 0, :], vT[:, p, :], ACT.Copy).then_inc(vs_ready, 1)
                    act.wait_ge(vs_ready, 1)
                    nc.scalar.activation(vs[:, 1, 0:C], vs[:, 0, 0:C][:, ::-1], ACT.Copy)
                    nc.scalar.activation(vs[:, 1, C:N], vs[:, 0, C:N][:, ::-1], ACT.Copy).then_inc(vs_ready, 1)

                @block.gpsimd
                def _(pool):
                    pool.wait_ge(cum_ready, 1)
                    nc.gpsimd.tensor_tensor(sg[:], cum[:], sg[:], SUB).then_inc(exc_ready, 1)
                    pool.wait_ge(sig_ready, 4)
                    for d in range(2):
                        i = nc.gpsimd.tensor_tensor(bb[:, d, :], kkT[:, p, :], al[:, d, :], MUL)
                    i.then_inc(bb_ready, 1)

                @block.vector
                def _(dve):
                    link = Chain(dve, dve_chain)
                    dve.wait_ge(sig_ready, 2)
                    nc.vector.tensor_tensor_scan(cum[:, 0, :], K("scan"), sg[:, 0, :], 0.0, MUL, ADD)
                    nc.vector.tensor_tensor_scan(cum[:, 1, :][:, ::-1], K("scan"), sg[:, 1, :][:, ::-1], 0.0, MUL,
                                                 ADD).then_inc(cum_ready, 1)
                    ka = prm[:, bass.ds(prm_at["ka"][0] + p, 1)]
                    link(nc.vector.tensor_scalar(oka[:], ka, -1.0, 1.0, MUL, ADD))
                    dve.wait_ge(sig_ready, 4)
                    link(nc.vector.tensor_scalar(kp[:], al[:], ka, oka[:], MUL, ADD))
                    for d in range(2):
                        i = nc.vector.tensor_tensor(kp[:, d, :], kp[:, d, :], kT[:, p, :], MUL)
                    link(i)

                    def ordered(out, fn):
                        fn(out[:, 0, :], lambda ap: ap[:, 0:N], 0)
                        fn(out[:, 1, 0:C], lambda ap: ap[:, 0:C][:, ::-1], 1)
                        return fn(out[:, 1, C:N], lambda ap: ap[:, C:N][:, ::-1], 1)

                    dve.wait_ge(exp_ready, 1)
                    ordered(kt, lambda o, rd, d: nc.vector.tensor_tensor(o, rd(kp[:, d, :]), rd(Pn[:, d, :]), MUL))
                    dve.wait_ge(exp_ready, 2)
                    dve.wait_ge(own_ready, 1)
                    nc.vector.tensor_tensor(AR[:, GC:GD, 1, :], tiled(rS[:]), tiled(Pp[:, 0, C:N]), MUL)
                    nc.vector.tensor_tensor(AR[:, GD + GC:G, 1, :], tiled(rS[:][:, ::-1]),
                                            tiled(Pp[:, 1, C:N][:, ::-1]), MUL)
                    nc.vector.tensor_copy(PC[:, 0:ND], chunked(Pp[:, 0, :])[:, :, Q - 1])
                    nc.vector.tensor_copy(PC[:, ND:ND + C // Q], chunked(Pp[:, 1, 0:C][:, ::-1])[:, :, Q - 1])
                    nc.vector.tensor_copy(PC[:, ND + C // Q:NCH], chunked(Pp[:, 1, C:N][:, ::-1])[:, :, Q - 1])
                    dve.wait_ge(bb_ready, 1)
                    link(ordered(bt, lambda o, rd, d: nc.vector.tensor_tensor(o, rd(bb[:, d, :]), rd(Pn[:, d, :]),
                                                                              MUL)))
                    link(nc.vector.tensor_tensor(bb[:, 1, 0:T], kp[:, 0, C:N], kp[:, 1, C:N], ADD))
                    link(nc.vector.scalar_tensor_tensor(bb[:, 0, 0:T], bb[:, 1, 0:T],
                                                        prm[:, bass.ds(prm_at["rk"][0] + p, 1)], rT[:, p, :], MUL, MUL))
                    dve.sem_inc(bsum_in, 1)
                    dve.wait_ge(exp_ready, 3)
                    for d, n0, n1, rd in ((0, 0, GD, lambda ap: ap[:, 0:N]),
                                          (1, GD, GD + GC, lambda ap: ap[:, 0:C][:, ::-1]),
                                          (1, GD + GC, G, lambda ap: ap[:, C:N][:, ::-1])):
                        nc.vector.scalar_tensor_tensor(AR[:, n0:n1, 0, :], tiled(rd(kkS[:])), -1.0,
                                                       tiled(rd(Pv[:, d, :])), MUL, MUL)
                    dve.wait_ge(bsum_done, 1)
                    dve.wait_ge(vs_ready, 1)
                    nc.vector.tensor_tensor(vT[:, p, C:N], bank(0), vT[:, p, C:N], MUL)

        with ExitStack() as st:
            att_, btt, ktt, vtt = (sb(st, n, [P, G, P]) for n in ("at_tok", "b_tok", "k_tok", "v_tok"))
            LT, X, XT, W1, MT = (sb(st, n, [P, 2 * G, Q]) for n in ("LT", "X", "XT", "W1", "MT"))
            RBT, RKT = (sb(st, n, [P, 4 * (GD - GC), Q]) for n in ("RBT", "RKT"))
            yS = sb(st, "yS", [P, T])
            Z = sb(st, "Z", [P, 2, ND + 1, Q])
            F, E, GP, U = LT, X, MT, W1
            S = sems(st, "t_done", "t_ready", "pk_done", "lt_done", "l_done", "rb_done", "pk_used", "lt_used",
                     "l_used", "rb_used", "x0_ready", "x0t_done", "xt0_ready", "x_ready", "xt_ready", "tr_done",
                     "w_done", "w_ready", "xx_done", "me_done", "me_ready", "fg_done", "fg_ready",
                     "u_done", "u_ready", "zp_done", "z_ready", "y_done", "dve_chain", "mprod_ready",
                     "mod_done")
            (t_done, t_ready, pk_done, lt_done, l_done, rb_done, pk_used, lt_used, l_used, rb_used, x0_ready, x0t_done,
             xt0_ready, x_ready, xt_ready, tr_done, w_done, w_ready,
             xx_done, me_done, me_ready, fg_done, fg_ready, u_done, u_ready, zp_done, z_ready, y_done, dve_chain,
             mprod_ready, mod_done) = S
            msum = [t[:].rearrange("p d n -> p (d n)") for t in (kt, vs)]
            NBT = 3

            def half(i):
                return slice(i * Q, (i + 1) * Q)

            def is_lat(g):
                return g % GD >= GC

            def lat(k):
                return k - 2 * GC * (1 + k // (2 * GD))

            def lat_blocks(b):
                ks = [2 * g + h for g in range(4 * b, 4 * b + 4) for h in range(2) if is_lat(g)]
                return ks[0], ks[-1] + 1

            def units(b):
                return [(g, h, c) for g in range(4 * b, 4 * b + 4) for h in range(2) for c in range(2)]

            def by_rows(b):
                return [(g, c, h) for g in range(4 * b, 4 * b + 4) for c in range(2) for h in range(2)]

            def cols(i, b):
                return bank(i).rearrange("p (k j) -> p k j", j=Q)

            def chunk_bank(b, c):
                return bank((2 * b + 1, 6 + b % 2)[c], 0, 4 * Q)

            def of_chunks(t, b):
                return t[:, 8 * b:8 * b + 8, :].rearrange("p (g c) j -> p g c j", c=2)

            def by_head(t, k0, k1):
                return t[:, k0:k1, :].rearrange("p (g h) j -> p h g j", h=2)

            with clear_then_block(S) as block:
                @block.sync
                def _(sp):
                    with sp.Fori(0, TURNS) as t:
                        for s in range(2):
                            n = S_MOD + s
                            sp.wait_ge(mod_used[n % 2], TURNS * p + t + nth(n))
                            sp_load(sp, n + 2, 2 * TURNS * p + 2 * t)

                @block.tensor
                def _(pe):
                    def transposes(src, b, out):
                        for g in range(4 * b, 4 * b + 4):
                            at = (g - 4 * b) * P
                            i = nc.tensor.transpose(out[:, at:at + P],
                                                    src[:, 2 * g:2 * g + 2, :].rearrange("p k j -> p (k j)"),
                                                    K("ident"))
                        return i

                    def first_transposes(b):
                        pe.wait_ge(x0_ready, b + 1)
                        if b:
                            pe.wait_ge(xt0_ready, b)
                        transposes(X, b, bank(5)).then_inc(x0t_done, 1)

                    for b in range(NBT):
                        for i in (1, 2, 3, 0):
                            if b and i == 2:
                                pe.wait_ge(rb_used, b)
                            if b and i == 0:
                                pe.wait_ge(l_used, b)
                            for g in range(4 * b, 4 * b + 4):
                                src = (AR[:, g, 0, :], bt[:, g // GD, (g % GD) * P:(g % GD + 1) * P],
                                       kt[:, g // GD, (g % GD) * P:(g % GD + 1) * P],
                                       vs[:, g // GD, (g % GD) * P:(g % GD + 1) * P])[i]
                                last = nc.tensor.transpose(bank(i, (g - 4 * b) * P, (g - 4 * b + 1) * P), src,
                                                           K("ident"))
                        last.then_inc(t_done, 1)
                        if b:
                            pe.wait_ge(pk_used, b)
                        for g, h, c in units(b):
                            at = 512 * h + (g - 4 * b) * P
                            w = 2 if is_lat(g) else 1
                            t0 = (g % GD) * P + c * Q
                            last = nc.tensor.matmul(psum[3][half(c), at:at + w * Q], kt[half(h), g // GD, t0:t0 + Q],
                                                    AR[half(h), g, 0:w, half(c)], start=True, stop=True)
                        last.then_inc(pk_done, 1)
                        if b:
                            pe.wait_ge(lt_used, b)
                        keep_warm(1, bank(4), WARM)
                        for g, c, h in by_rows(b):
                            t0, at = (g % GD) * P + c * Q, (2 * (g - 4 * b) + c) * Q
                            last = nc.tensor.matmul(bank(4, at, at + Q)[half(h)], bt[half(h), g // GD, t0:t0 + Q],
                                                    AR[half(h), g, 0, half(c)], start=True, stop=True)
                        last.then_inc(lt_done, 1)
                        pe.wait_ge(t_ready, b + 1)
                        keep_warm(1, bank(2), WARM)
                        for g, c, h in by_rows(b):
                            if is_lat(g):
                                t0, at = (g % GD) * P + c * Q, (g - 4 * b) * Q
                                last = nc.tensor.matmul(bank(2 + h, at, at + Q)[half(c)],
                                                        bt[half(h), g // GD, t0:t0 + Q], AR[half(h), g, 1, half(c)],
                                                        start=True, stop=True)
                        last.then_inc(rb_done, 1)
                        for g, c, h in by_rows(b):
                            t0, at = (g % GD) * P + c * Q, (2 * (g - 4 * b) + c) * Q
                            last = nc.tensor.matmul(bank(0, at, at + Q)[half(h)], AR[half(h), g, 0, half(c)],
                                                    bt[half(h), g // GD, t0:t0 + Q], start=True, stop=True)
                        last.then_inc(l_done, 1)
                        if b:
                            first_transposes(b - 1)
                        keep_warm(1, bank(1))
                    pe.wait_ge(pk_used, NBT)
                    keep_warm(5, bank(6))
                    first_transposes(NBT - 1)

                    def next_x(lv, b):
                        pe.wait_ge(xt_ready, NBT * lv + b + 1)
                        transposes(XT, b, bank(2 * b + 1)).then_inc(tr_done, 1)

                    for lv in range(LVL):
                        for b in range(NBT):
                            if lv:
                                pe.wait_ge(x_ready, NBT * (lv - 1) + b + 1)
                            else:
                                pe.wait_ge(*((l_used, NBT), (rb_used, NBT), (xt0_ready, NBT))[b])
                                if b:
                                    keep_warm(2, bank(2 * b))
                            for g, c, h in by_rows(b):
                                n, at = 2 * g + c, (g - 4 * b) * Q
                                last = nc.tensor.matmul(bank(2 * b + h, at, at + Q)[half(c)], LT[half(h), n, :],
                                                        X[half(h), n, :], start=True, stop=True)
                            last.then_inc(w_done, 1)
                            keep_warm(1, bank(6), WARM)
                        for b in range(NBT):
                            pe.wait_ge(w_ready, NBT * lv + b + 1)
                            for g, h, c in units(b):
                                k = 2 * g + h
                                last = nc.tensor.matmul(bank(2 * b, (k - 8 * b) * Q, (k - 8 * b + 1) * Q)[half(c)],
                                                        W1[half(c), k, :], XT[half(c), k, :], start=True, stop=True)
                            last.then_inc(xx_done, 1)
                            keep_warm(1, bank(6), WARM)
                            if b and lv < LVL - 1:
                                next_x(lv, b - 1)
                        if lv < LVL - 1:
                            next_x(lv, NBT - 1)
                    def by_chunk(n, b):
                        at = (n // 2 - 4 * b) * Q
                        return chunk_bank(b, n % 2)[:, at:at + Q]

                    for b in range(NBT):
                        pe.wait_ge(xt_ready, NBT * (LVL - 1) + b + 1)
                        if b == 2:
                            pe.wait_ge(me_ready, 1)
                        keep_warm(1, bank(2 * b), 256)
                        for g, h, c in units(b):
                            k = 2 * g + h
                            nc.tensor.matmul(bank(2 * b, (k - 8 * b) * Q, (k - 8 * b + 1) * Q)[half(c)],
                                             MT[half(c), k, :], vtt[half(c), g, h * Q:(h + 1) * Q], start=True,
                                             stop=True)
                        keep_warm(1, bank(2 * b + 1), WARM)
                        for g, h, c in units(b):
                            k, n = 2 * g + h, 2 * g + c
                            last = nc.tensor.matmul(by_chunk(n, b)[half(h)],
                                                    att_[half(c), g, h * Q:(h + 1) * Q], XT[half(c), k, :],
                                                    start=True, stop=True)
                        last.then_inc(me_done, 1)
                    for b in range(NBT):
                        pe.wait_ge(me_ready, b + 1)
                        keep_warm(1, bank(2 * b), 256)
                        for g, h, c in units(b):
                            k = 2 * g + h
                            nc.tensor.matmul(bank(2 * b, (k - 8 * b) * Q, (k - 8 * b + 1) * Q)[half(c)],
                                             XT[half(c), k, :], F[half(c), k, :], start=True, stop=True)
                        if b == 0:
                            pe.wait_ge(me_ready, NBT)
                        if b == 2:
                            pe.wait_ge(fg_ready, 1)
                        keep_warm(1, bank(2 * b + 1), WARM)
                        for g, h, c in units(b):
                            n = 2 * g + c
                            last = nc.tensor.matmul(by_chunk(n, b)[half(h)],
                                                    ktt[half(c), g, h * Q:(h + 1) * Q],
                                                    vtt[half(c), g, h * Q:(h + 1) * Q], start=True, stop=True)
                        last.then_inc(fg_done, 1)
                    pe.wait_ge(fg_ready, NBT - 1)
                    keep_warm(2, bank(2))
                    pe.wait_ge(fg_ready, NBT)

                    def state_out(s):
                        for d in range(2):
                            n, at = ND * d + s, (s - C // Q) * Q
                            for h in range(2):
                                nc.tensor.matmul(bank(2 + d, at, at + Q)[half(h)], Z[half(h), d, s, :],
                                                 AR[half(h), n // 2, 1, half(n % 2)], start=True, stop=True)

                    def own_out(s):
                        for d in range(2):
                            n = ND * d + s
                            g, c = n // 2, n % 2
                            at = (4 * d + (s - C // Q) // 2) * Q
                            for h in range(2):
                                o = bank(4 + c, at, at + Q)[half(h)]
                                nc.tensor.matmul(o, U[half(c), 2 * g + h, :], RBT[half(c), lat(2 * g + h), :],
                                                 start=True, stop=False)
                                last = nc.tensor.matmul(o, vtt[half(c), g, h * Q:(h + 1) * Q],
                                                        RKT[half(c), lat(2 * g + h), :], start=False, stop=True)
                        return last

                    for s in range(ND):
                        pe.wait_ge(z_ready, s + 1)
                        for d in range(2):
                            n = ND * d + s
                            for h in range(2):
                                at = (2 * (s % 2) + d) * Q
                                last = nc.tensor.matmul(bank(6 + h, at, at + Q)[half(n % 2)], E[half(h), n, :],
                                                        Z[half(h), d, s, :], start=True, stop=True)
                        last.then_inc(u_done, 1)
                        keep_warm(1, bank((s + 1) % 2), 256)
                        if s >= C // Q:
                            state_out(s)
                        pe.wait_ge(u_ready, s + 1)
                        for d in range(2):
                            n = ND * d + s
                            g, c = n // 2, n % 2
                            for h in range(2):
                                last = nc.tensor.matmul(bank(s % 2, d * Q, (d + 1) * Q)[half(h)],
                                                        btt[half(c), g, h * Q:(h + 1) * Q], U[half(c), 2 * g + h, :],
                                                        start=True, stop=True)
                        last.then_inc(zp_done, 1)
                        keep_warm(1, bank((s + 1) % 2), 256)
                        if s >= C // Q:
                            last = own_out(s)
                    last.then_inc(y_done, 1)
                    for s in range(2):
                        pe.wait_ge(mod_used[s], TURNS * p + (S_IN // 2 + TURNS))
                    pe.wait_ge(z_ready, ND + 1)
                    for t in range(TURNS):
                        for s in range(2):
                            for m in range(2):
                                at = 4 * t + 2 * s + m
                                last = nc.tensor.matmul(bank(0, at, at + 1),
                                                        msum[s][:, 256 * t + m * P:256 * t + (m + 1) * P],
                                                        K("ones", 0, 1), start=True, stop=True)
                    last.then_inc(mod_done, 1)
                    keep_warm(4, bank(1))

                @block.scalar
                def _(act):
                    def first_xt(b):
                        act.wait_ge(x0t_done, b + 1)
                        nc.scalar.activation(XT[:, 8 * b:8 * b + 8, :], cols(5, b), ACT.Copy).then_inc(xt0_ready, 1)

                    for b in range(NBT):
                        act.wait_ge(t_done, b + 1)
                        for i, dst in enumerate((att_, btt, ktt, vtt)):
                            j = nc.scalar.activation(dst[:, 4 * b:4 * b + 4, :],
                                                     bank(i).rearrange("p (g c) -> p g c", c=P), ACT.Copy)
                        j.then_inc(t_ready, 1)
                        if b:
                            first_xt(b - 1)
                    first_xt(NBT - 1)
                    for lv in range(LVL - 1):
                        for b in range(NBT):
                            act.wait_ge(tr_done, NBT * lv + b + 1)
                            nc.scalar.activation(X[:, 8 * b:8 * b + 8, :], cols(2 * b + 1, b), ACT.Copy)\
                                .then_inc(x_ready, 1)
                    for b in range(NBT):
                        act.wait_ge(me_done, b + 1)
                        nc.scalar.activation(F[:, 8 * b:8 * b + 8, :], cols(2 * b, b), ACT.Copy)
                        for c in range(2):
                            i = nc.scalar.activation(of_chunks(E, b)[:, :, c, :],
                                                     chunk_bank(b, c).rearrange("p (g j) -> p g j", j=Q), ACT.Copy)
                        i.then_inc(me_ready, 1)

                @block.gpsimd
                def _(pool):
                    pool.wait_ge(pk_done, NBT)
                    with pool.Fori(0, TURNS) as t:
                        for s in range(2):
                            n = S_MOD + s
                            r = raw[n % 2]
                            pool.wait_ge(raw_loaded[n % 2], 16 * TURNS * p + 16 * t + 16 * (n // 2 + 1))
                            nc.gpsimd.tensor_tensor(r[:], r[:], cs[:, :, 0].unsqueeze(2).to_broadcast([P, KT, 256]),
                                                    MUL).then_inc(mprod_ready, 1)
                            for i, w in enumerate((4, 2)):
                                pool.wait_ge(mprod_ready, 6 * t + (3 * s + i + 1))
                                nc.gpsimd.tensor_tensor(r[:, 0:w, :], r[:, 0:w, :], r[:, w:2 * w, :], ADD)\
                                    .then_inc(mprod_ready, 1)
                            pool.wait_ge(mprod_ready, 6 * t + (3 * s + 3))
                            nc.gpsimd.tensor_tensor(msum[s][:, bass.ds(256 * t, 256)], r[:, 0, :], r[:, 1, :], ADD)\
                                .then_inc(mod_used[n % 2], 1)

                @block.vector
                def _(dve):
                    link = Chain(dve, dve_chain)

                    def wide(name, n, lo=0, hi=None):
                        return K(name, lo, hi).unsqueeze(1).to_broadcast([P, n, Q])

                    def wide2(name, n):
                        return K(name).unsqueeze(1).unsqueeze(1).to_broadcast([P, 2, n, Q])

                    nc.vector.memset(Z[:, :, 0, :], 0.0)
                    for b in range(NBT):
                        k0, k1 = lat_blocks(b)
                        g0, g1 = k0 // 2 - 4 * b, k1 // 2 - 4 * b
                        k = slice(8 * b, 8 * b + 8)
                        pp = psum[3][:, :].rearrange("p (h g j) -> p h g j", h=2, j=P)
                        dve.wait_ge(pk_done, b + 1)
                        nc.vector.tensor_tensor(by_head(RKT, lat(k0), lat(k1 - 1) + 1), pp[:, :, g0:g1, Q:P],
                                                wide2("upper_eq", g1 - g0), MUL)
                        nc.vector.tensor_tensor(by_head(MT, 8 * b, 8 * b + 8), pp[:, :, :, 0:Q], wide2("upper", 4),
                                                MUL).then_inc(pk_used, 1)
                        dve.wait_ge(lt_done, b + 1)
                        nc.vector.tensor_tensor(LT[:, k, :], cols(4, b), wide("upper", 8), MUL).then_inc(lt_used, 1)
                        dve.wait_ge(rb_done, b + 1)
                        rb = psum[1][:, :].rearrange("p (h w) -> p h w", h=2)[:, :, g0 * Q:g1 * Q]\
                            .rearrange("p h (g j) -> p h g j", j=Q)
                        nc.vector.tensor_tensor(by_head(RBT, lat(k0), lat(k1 - 1) + 1), rb,
                                                wide2("upper_eq", g1 - g0), MUL).then_inc(rb_used, 1)
                        dve.wait_ge(l_done, b + 1)
                        link(nc.vector.tensor_tensor(X[:, k, :], cols(0, b), wide("lvl1", 8), MUL))
                        dve.sem_inc(l_used, 1)
                        nc.vector.tensor_tensor(X[:, k, :], X[:, k, :], wide("eye64", 8), ADD).then_inc(x0_ready, 1)
                    for lv in range(LVL):
                        for b in range(NBT):
                            dve.wait_ge(w_done, NBT * lv + b + 1)
                            ww = psum[b][:, :].rearrange("p (h w) -> p h w", h=2)[:, :, 0:4 * Q]\
                                .rearrange("p h (g j) -> p h g j", j=Q)
                            m = K("lvl", lv * Q, (lv + 1) * Q).unsqueeze(1).unsqueeze(1).to_broadcast([P, 2, 4, Q])
                            nc.vector.tensor_tensor(by_head(W1, 8 * b, 8 * b + 8), ww, m, MUL).then_inc(w_ready, 1)
                        for b in range(NBT):
                            k = slice(8 * b, 8 * b + 8)
                            if lv == 0:
                                dve.wait_ge(xt0_ready, b + 1)
                            dve.wait_ge(xx_done, NBT * lv + b + 1)
                            nc.vector.tensor_tensor(XT[:, k, :], XT[:, k, :], cols(2 * b, b), ADD)\
                                .then_inc(xt_ready, 1)
                    for b in range(NBT):
                        k = slice(8 * b, 8 * b + 8)
                        dve.wait_ge(fg_done, b + 1)
                        nc.vector.tensor_copy(F[:, k, :], cols(2 * b, b))
                        for c in range(2):
                            i = nc.vector.tensor_tensor(of_chunks(GP, b)[:, :, c, :],
                                                        chunk_bank(b, c).rearrange("p (g j) -> p g j", j=Q),
                                                        PC[:, k].rearrange("p (g c) -> p g c", c=2)[:, :, c]
                                                        .unsqueeze(2).to_broadcast([P, 4, Q]), MUL)
                        i.then_inc(fg_ready, 1)
                    dve.wait_ge(fg_ready, NBT)
                    dve.sem_inc(z_ready, 1)
                    for s in range(ND):
                        for d in range(2):
                            n = ND * d + s
                            i = nc.vector.scalar_tensor_tensor(Z[:, d, s + 1, :], Z[:, d, s, :], PC[:, n:n + 1],
                                                               GP[:, n, :], MUL, ADD)
                        link(i)
                        dve.wait_ge(u_done, s + 1)
                        c = s % 2
                        uf = [t[half(c), :, :].rearrange("p (d g h) v -> p d g h v", d=2, h=2)[:, :, s // 2, :, :]
                              for t in (U, F)]
                        up_ = psum[3][half(c), :].rearrange("p (h w) -> p h w", h=2)[:, :, 2 * Q * c:2 * Q * c + 2 * Q]
                        nc.vector.tensor_tensor(uf[0], up_.rearrange("p h (d v) -> p d h v", d=2), uf[1], ADD)\
                            .then_inc(u_ready, 1)
                        dve.wait_ge(zp_done, s + 1)
                        for d in range(2):
                            n = ND * d + s
                            i = nc.vector.scalar_tensor_tensor(Z[:, d, s + 1, :], bank(c, d * Q, (d + 1) * Q),
                                                               PC[:, n:n + 1], Z[:, d, s + 1, :], MUL, ADD)
                        i.then_inc(z_ready, 1)
                        dve.wait_ge(z_ready, s + 2)
                    dve.wait_ge(y_done, 1)
                    own_ = psum[2][:, :].rearrange("p (c d s j) -> p d s c j", c=2, d=2, j=Q)
                    for d in range(2):
                        y = yS[:] if d == 0 else yS[:][:, ::-1]
                        if d == 0:
                            link(nc.vector.tensor_copy(y, bank(2)))
                        else:
                            link(nc.vector.tensor_tensor(y, bank(3), y, ADD))
                        y4 = y.rearrange("p (s c j) -> p s c j", c=2, j=Q)
                        link(nc.vector.tensor_tensor(y4, own_[:, d], y4, ADD))
                    nc.vector.tensor_copy(rT[:, p, :], yS[:])
                    dve.wait_ge(mod_done, 1)
                    nc.vector.tensor_tensor(mod[:, bass.ds(4 * TURNS * p + 16, 4 * TURNS)], bank(0, 0, 4 * TURNS),
                                            prm[:, bass.ds(4 * TURNS * p + 16, 4 * TURNS)], ADD)
    drw.close()

    one = ((lambda s, m: 2 * s + m, (0, T)),)
    out_proj = ExitStack()
    W = [[sb(out_proj, f"wo{i}{s}", [P, KT, 256], F32R) for s in range(2)] for i in range(2)]
    h = [sb(out_proj, f"ho{i}", [P, KT, T], F32R) for i in range(2)]
    with ExitStack() as st:
        g2 = sb(st, "g2", [P, PAIRS * P])
        sq = [sb(st, f"gsq{i}", [P, T]) for i in range(2)]
        rg = [sb(st, f"grs{i}", [P, T]) for i in range(PAIRS)]
        S = sems(st, "g2_in", "mean_done", "yc_ready", "gsq_ready", "var_done", "root_ready", "yn_ready", "ys_ready",
                 "gate_done", "o_ready", "hi_made", "dve_chain", "lo_made")
        (g2_in, mean_done, yc_ready, gsq_ready, var_done, root_ready, yn_ready, ys_ready, gate_done, o_ready, hi_made,
         dve_chain, lo_made) = S
        with clear_then_block(S) as block:
            @block.sync
            def _(sp):
                sp.dma_start(g2[:], A["g2"]).then_inc(g2_in, 16)
                for j in range(2):
                    sp_next(sp, S_OUT + j)

            @block.tensor
            def _(pe):
                for i in range(PAIRS):
                    nc.tensor.matmul(bank(i), K("onesh"), rT[:, i, :], start=True, stop=True).then_inc(mean_done, 1)
                for i in range(PAIRS):
                    pe.wait_ge(gsq_ready, i + 1)
                    nc.tensor.matmul(bank(i), K("onesh"), sq[i % 2][:], start=True, stop=True).then_inc(var_done, 1)
                pe.wait_ge(g2_in, 16)
                for i in range(PAIRS):
                    nc.tensor.matmul(bank(4 + i), g2[:, i * P:(i + 1) * P], gT[:], start=True, stop=True)\
                        .then_inc(gate_done, 1)
                pe.wait_ge(root_ready, PAIRS)
                pe_block(pe, S_OUT, W, h, parts=one,
                         ready=lambda k: (lo_made, max(1, k - PAIRS + 2)))

            @block.scalar
            def _(act):
                for i in range(PAIRS):
                    act.wait_ge(yc_ready, i + 1)
                    if i >= 2:
                        act.wait_ge(var_done, i - 1)
                    nc.scalar.activation(sq[i % 2][:], rT[:, i, :], ACT.Square).then_inc(gsq_ready, 1)
                for i in range(PAIRS):
                    act.wait_ge(var_done, i + 1)
                    nc.scalar.activation(rg[i][:], bank(i), ACT.Sqrt, bias=small[:, 1:2], scale=1.0 / HD)\
                        .then_inc(root_ready, 1)
                act_hi(act, S_OUT, W)
                nc.scalar.activation(h[0][:, 0:PAIRS, :], attT, ACT.Copy).then_inc(hi_made, 1)
                act_hi(act, S_OUT + 1, W)
                for i in range(PAIRS):
                    act.wait_ge(yn_ready, i + 1)
                    nc.scalar.activation(rT[:, i, :], rT[:, i, :], ACT.Identity, scale=R("lnw", i, i + 1),
                                         bias=R("lnb", i, i + 1)).then_inc(ys_ready, 1)
                for i in range(PAIRS):
                    act.wait_ge(o_ready, i + 1)
                    nc.scalar.activation(h[0][:, PAIRS + i, :], rT[:, i, :], ACT.Copy).then_inc(hi_made, 1)

            @block.vector
            def _(dve):
                link = Chain(dve, dve_chain)
                for i in range(PAIRS):
                    dve.wait_ge(mean_done, i + 1)
                    nc.vector.scalar_tensor_tensor(rT[:, i, :], bank(i), -1.0 / HD, rT[:, i, :], MUL, ADD)\
                        .then_inc(yc_ready, 1)
                for i in range(PAIRS):
                    dve.wait_ge(root_ready, i + 1)
                    link(nc.vector.reciprocal(rg[i][:], rg[i][:]))
                    nc.vector.tensor_tensor(rT[:, i, :], rT[:, i, :], rg[i][:], MUL).then_inc(yn_ready, 1)
                for i in range(PAIRS):
                    dve.wait_ge(ys_ready, i + 1)
                    link(nc.vector.tensor_tensor(rT[:, i, :], rT[:, i, :], vT[:, i, C:N], ADD))
                    dve.wait_ge(gate_done, i + 1)
                    nc.vector.tensor_tensor(rT[:, i, :], bank(4 + i), rT[:, i, :], MUL).then_inc(o_ready, 1)

            @block.gpsimd
            def _(pool):
                pool_lo(pool, S_OUT, W)
                pool.wait_ge(hi_made, 1)
                nc.gpsimd.tensor_tensor(h[1][:, 0:PAIRS, :], attT, h[0][:, 0:PAIRS, :].bitcast(F32), SUB)\
                    .then_inc(lo_made, 1)
                pool_lo(pool, S_OUT + 1, W)
                for i in range(PAIRS):
                    pool.wait_ge(hi_made, i + 2)
                    nc.gpsimd.tensor_tensor(h[1][:, PAIRS + i, :], rT[:, i, :], h[0][:, PAIRS + i, :].bitcast(F32),
                                            SUB).then_inc(lo_made, 1)

    class SquareSum:

        def __init__(self, st):
            self.sq, self.acc = sb(st, "ysq", [P, T]), sb(st, "yacc", [P, T])
            self.ready, = sems(st, "ysum_ready")
            clear([self.ready])

        def add(self, dve, t):
            y = yb[:, t, :]
            nc.vector.tensor_tensor(self.acc[:] if t == 0 else self.sq[:], y, y, MUL).then_inc(self.ready, 1)
            dve.wait_ge(self.ready, max(1, 2 * t))
            if t:
                nc.vector.tensor_tensor(self.acc[:], self.acc[:], self.sq[:], ADD).then_inc(self.ready, 1)
                dve.wait_ge(self.ready, 2 * t + 1)

        def over_channels(self, pe):
            pe.wait_ge(self.ready, 2 * KT - 1)
            nc.tensor.matmul(bank(6), K("ones"), self.acc[:], start=True, stop=True)

    def dense(n0, nb, evac, W, h, squares=None, beside=None):
        with nc.Block() as block:
            if beside:
                @block.vector
                def _(dve):
                    beside(dve)

            if squares:
                @block.vector
                def _(dve):
                    for t in range(KT):
                        n = n0 + t // 2
                        dve.wait_ge(tile_free[n % 2][t % 2], nth(n))
                        squares.add(dve, t)

            @block.sync
            def _(sp):
                with sp.Fori(0, nb // 2 - 1) as turn:
                    up = 2 * turn
                    for j in range(2):
                        sp_next(sp, n0 + 2 + j, up)

            @block.gpsimd
            def _(pool):
                with pool.Fori(0, nb // 2 - 1) as turn:
                    up = 2 * turn
                    for j in range(2):
                        pool_lo(pool, n0 + 2 + j, W, up)

            @block.tensor
            def _(pe):
                pe_block(pe, n0 + 1, W, h, parts=one)
                with pe.Fori(0, nb // 2 - 1) as turn:
                    up = 2 * turn
                    for j in range(2):
                        pe_block(pe, n0 + 2 + j, W, h, up=up, parts=one)
                if squares:
                    squares.over_channels(pe)

            @block.scalar
            def _(act):
                for j in range(nb):
                    n = n0 + j
                    for m in range(2):
                        act.wait_ge(tile_done[n % 2][m], nth(n))
                        if m == 1 and j + 2 < nb:
                            act_hi(act, n + 2, W)
                        nc.scalar.activation(evac(2 * j + m), bank(2 * (n % 2) + m), ACT.Copy)\
                            .then_inc(tile_free[n % 2][m], 1)

    def norms(layer, g_post, gate_tile, g_pre=None, pre_layer=None, pre_tile=None, n0=None):
        with ExitStack() as st:
            sq = [sb(st, f"nsq{i}", [P, T]) for i in range(2)]
            rst = [sb(st, f"nrst{i}", [P, T]) for i in range(2)]
            hf = [sb(st, f"nhf{i}", [P, T]) for i in range(4)]
            S = sems(st, "sq_ready", "sq_used", "root_ready", "t_ready", "x_even", "x_odd", "hf_ready", "hs_ready",
                     "hhi_ready", "h_even", "h_odd", "dve_chain", "out_done")
            (sq_ready, sq_used, root_ready, t_ready, x_even, x_odd, hf_ready, hs_ready, hhi_ready, h_even, h_odd,
             dve_chain, out_done) = S
            x_ready, h_ready = (x_even, x_odd), (h_even, h_odd)
            rounds = 2 if g_pre else 1
            pre_at = 48 * pre_layer + pre_tile if g_pre else None

            def shift(k):
                return mod[:, pre_at + k:pre_at + k + 1]

            with clear_then_block(S) as block:
                if rounds == 2:
                    @block.sync
                    def _(sp):
                        for j in range(2):
                            sp_next(sp, n0 + j)

                @block.scalar
                def _(act):
                    for r in range(rounds):
                        if r:
                            for k in range(KT):
                                act.wait_ge(x_ready[k % 2], k // 2 + 1)
                                if k >= 2:
                                    act.wait_ge(sq_used, k - 1)
                                nc.scalar.activation(sq[k % 2][:], x[:, k, :], ACT.Square).then_inc(sq_ready, 1)
                            act.wait_ge(sq_used, KT)
                        nc.scalar.activation(rst[r][:], bank(6 + r), ACT.Sqrt, bias=small[:, 0:1], scale=1.0 / D)\
                            .then_inc(root_ready, 1)
                    if rounds == 1:
                        for k in range(KT):
                            act.wait_ge(x_ready[k % 2], k // 2 + 1)
                            act.dma_start(A["out"][:, k, :], x[:, k, :]).then_inc(out_done, 16)
                        act.wait_ge(out_done, 16 * KT)
                        return
                    for k in range(KT):
                        act.wait_ge(hf_ready, k + 1)
                        f = hf[k % 4][:]
                        if k % 2:
                            nc.scalar.activation(f, f, ACT.Identity, bias=shift(k), scale=1.0).then_inc(hs_ready, 1)
                            act.wait_ge(hs_ready, k // 2 + 1)
                            i = nc.scalar.activation(h[0][:, k], f, ACT.Copy)
                        else:
                            i = nc.scalar.activation(h[0][:, k], f, ACT.Identity, bias=shift(k), scale=1.0)
                        i.then_inc(hhi_ready, 1)

                if rounds == 2:
                    @block.tensor
                    def _(pe):
                        keep_warm(6, bank(5))
                        for k in range(KT):
                            pe.wait_ge(sq_ready, k + 1)
                            nc.tensor.matmul(bank(7), K("ones"), sq[k % 2][:], start=k == 0, stop=k == KT - 1)\
                                .then_inc(sq_used, 1)
                        keep_warm(5, bank(5))
                        pe_block(pe, n0, W, h, parts=one, ready=lambda k: (h_ready[k % 2], k // 2 + 1))

                @block.vector
                def _(dve):
                    link = Chain(dve, dve_chain)
                    if rounds == 2:
                        dve_hi(dve, n0, W)
                    link(nc.vector.tensor_tensor(nsc[:, 2, :], mod[:, 48 * layer + gate_tile:
                                                                   48 * layer + gate_tile + KT], R(g_post), MUL))
                    if g_pre:
                        link(nc.vector.scalar_tensor_tensor(nsc[:, 3, :], mod[:, pre_at + KT:pre_at + 2 * KT],
                                                            1.0, R(g_pre), ADD, MUL))
                    dve.wait_ge(root_ready, 1)
                    link(nc.vector.reciprocal(rst[0][:], rst[0][:]))
                    for k0 in range(0, KT, 2):
                        for k in (k0, k0 + 1):
                            nc.vector.scalar_tensor_tensor(yb[:, k, :], yb[:, k, :], nsc[:, 2, k:k + 1], rst[0][:],
                                                           MUL, MUL).then_inc(t_ready, 1)
                        dve.wait_ge(t_ready, k0 + 1)
                        nc.vector.tensor_tensor(x[:, k0, :], x[:, k0, :], yb[:, k0, :], ADD).then_inc(x_even, 1)
                    if rounds == 1:
                        return
                    dve_hi(dve, n0 + 1, W)
                    dve.wait_ge(root_ready, 2)
                    link(nc.vector.reciprocal(rst[1][:], rst[1][:]))
                    dve.wait_ge(x_even, KT // 2)
                    dve.wait_ge(x_odd, KT // 2)

                    def scaled(k):
                        if k >= 4:
                            dve.wait_ge(h_ready[k % 2], (k - 4) // 2 + 1)
                        nc.vector.scalar_tensor_tensor(hf[k % 4][:], x[:, k, :], nsc[:, 3, k:k + 1], rst[1][:], MUL,
                                                       MUL).then_inc(hf_ready, 1)

                    scaled(0)
                    for k in range(0, KT, 2):
                        for j in (k + 1, k + 2):
                            if j < KT:
                                scaled(j)
                        dve.wait_ge(hhi_ready, k + 1)
                        nc.vector.scalar_tensor_tensor(h[1][:, k], hf[k % 4][:], shift(k), h[0][:, k].bitcast(F32),
                                                       ADD, SUB).then_inc(h_even, 1)

                @block.gpsimd
                def _(pool):
                    if rounds == 2:
                        pool_lo(pool, n0, W)
                    for k in range(1, KT, 2):
                        pool.wait_ge(t_ready, k + 1)
                        nc.gpsimd.tensor_tensor(x[:, k, :], x[:, k, :], yb[:, k, :], ADD).then_inc(x_odd, 1)
                    if rounds == 2:
                        pool_lo(pool, n0 + 1, W)
                        for k in range(1, KT, 2):
                            pool.wait_ge(hhi_ready, k + 1)
                            nc.gpsimd.tensor_tensor(h[1][:, k], hf[k % 4][:], h[0][:, k].bitcast(F32), SUB)\
                                .then_inc(h_odd, 1)

    def mlp(n0, last_phase):
        with ExitStack() as st:
            hid = [sb(st, f"hid{i}", [P, KT, T], F32R) for i in range(2)]
            rl = [sb(st, f"rl{i}", [P, T]) for i in range(2)]
            sq = [sb(st, f"rs{i}", [P, T]) for i in range(2)]
            S = sems(st, "sq_ready", "hid_hi", "hid_ready")
            sq_ready, hid_hi, hid_ready = S
            NB = 32
            squares = SquareSum(st)
            with clear_then_block(S) as block:
                @block.sync
                def _(sp):
                    with sp.Fori(0, NB // 2 - 1 - last_phase) as turn:
                        up = 2 * turn
                        for j in range(2):
                            sp_next(sp, n0 + 2 + j, up)

                @block.gpsimd
                def _(pool):
                    with pool.Fori(0, NB // 2 - 1) as turn:
                        up = 2 * turn
                        for j in range(2):
                            pool_lo(pool, n0 + 2 + j, W, up)

                @block.tensor
                def _(pe):
                    def quarter(n, first, up, hidden):
                        for j in range(first, 8):
                            pe_block(pe, n + j, W, h if j < 4 else hid, up=up, parts=one,
                                     ready=(lambda k: (hid_ready, hidden + k + 1)) if j == 4 else None)

                    quarter(n0, 1, 0, 0)
                    with pe.Fori(0, NB // 8 - 1) as turn:
                        up = 8 * turn
                        quarter(n0 + 8, 0, up, up + 8)
                    squares.over_channels(pe)

                @block.scalar
                def _(act):
                    def quarter(up, ahead):
                        for j in range(8):
                            n = n0 + j
                            if j < 4:
                                for m in range(2):
                                    t = 2 * j + m
                                    act.wait_ge(tile_done[n % 2][m], nth(n) + up // 2)
                                    if m:
                                        act_hi(act, n + 2, W, up)
                                    nc.scalar.activation(rl[t % 2][:], bank(2 * (n % 2) + m), ACT.Relu)\
                                        .then_inc(tile_free[n % 2][m], 1)
                                    act.wait_ge(sq_ready, up + t + 1)
                                    nc.scalar.activation(hid[0][:, t], sq[t % 2][:], ACT.Copy).then_inc(hid_hi, 1)
                            elif j < 6 or ahead:
                                act_hi(act, n + 2, W, up)

                    with act.Fori(0, (NB - 8) // 8) as turn:
                        up = 8 * turn
                        quarter(up, True)
                    quarter(NB - 8, False)

                @block.vector
                def _(dve):
                    def quarter(up, first, last=False):
                        for j in range(8):
                            n = n0 + j
                            for m in range(2):
                                if j < 4:
                                    t = 2 * j + m
                                    dve.wait_ge(tile_free[n % 2][m], nth(n) + up // 2)
                                    nc.vector.tensor_tensor(sq[t % 2][:], rl[t % 2][:], rl[t % 2][:], MUL)\
                                        .then_inc(sq_ready, 1)
                                    dve.wait_ge(hid_hi, up + t + 1)
                                    nc.vector.tensor_tensor(hid[1][:, t], sq[t % 2][:], hid[0][:, t].bitcast(F32), SUB)\
                                        .then_inc(hid_ready, 1)
                                else:
                                    c = 2 * (j - 4) + m
                                    dve.wait_ge(tile_done[n % 2][m], nth(n) + up // 2)
                                    o = bank(2 * (n % 2) + m)
                                    if first:
                                        i = nc.vector.tensor_copy(yb[:, c, :], o)
                                    else:
                                        i = nc.vector.tensor_tensor(yb[:, c, :], o, yb[:, c, :], ADD)
                                    i.then_inc(tile_free[n % 2][m], 1)
                                    if last:
                                        dve.wait_ge(tile_free[n % 2][m], nth(n) + up // 2)
                                        squares.add(dve, c)

                    quarter(0, True)
                    with dve.Fori(0, NB // 8 - 2) as turn:
                        up = 8 * turn
                        quarter(up + 8, False)
                    quarter(NB - 8, False, True)

    with ExitStack() as st:
        dense(S_OUT, 4, lambda t: yb[:, t, :], W, h, SquareSum(st))
    out_proj.close()
    mix.close()
    tail = ExitStack()
    W = [[sb(tail, f"v{i}{s}", [P, KT, 256], F32R) for s in range(2)] for i in range(2)]
    h = [sb(tail, f"hm{i}", [P, KT, T], F32R) for i in range(2)]
    norms(0, "g01", 16, "g02", 0, 24, S_MLP0)
    mlp(S_MLP0, False)
    norms(0, "g03", 40, "g10", 1, 0, S_CIN)

    with ExitStack() as st:
        gates = sb(st, "gates", [P, 2 * KT, T])
        u = sb(st, "u", [P, KT, T + 2])
        S = sems(st, "chi_ready", "clo_ready", "conv_chain")
        chi_ready, clo_ready, conv_chain = S
        conv = gates[:, KT:2 * KT, :]

        def convolution(dve):
            link = Chain(dve, conv_chain)
            nc.vector.memset(u[:, :, 0], 0.0)
            link(nc.vector.memset(u[:, :, T + 1], 0.0))
            for k in range(KT):
                n = S_CIN + (2 * KT + k) // 2
                dve.wait_ge(tile_free[n % 2][k % 2], nth(n))
                c = conv[:, k, :]
                link(nc.vector.tensor_tensor(u[:, k, 1:T + 1], u[:, k, 1:T + 1], c, MUL))
                link(nc.vector.tensor_scalar(c, u[:, k, 1:T + 1], R("cw", KT + k, KT + k + 1), None, MUL))
                for tap in (0, 2):
                    link(nc.vector.scalar_tensor_tensor(c, u[:, k, tap:tap + T],
                                                        R("cw", tap * KT + k, tap * KT + k + 1), c, MUL, ADD))
                link(nc.vector.tensor_tensor(c, c, gates[:, k, :], MUL))

        clear(S)
        dense(S_CIN, 12, lambda t: gates[:, t, :] if t < 2 * KT else u[:, t - 2 * KT, 1:T + 1], W, h,
              beside=convolution)
        with nc.Block() as block:
            @block.sync
            def _(sp):
                for j in range(2):
                    sp_next(sp, S_COUT + j)

            @block.tensor
            def _(pe):
                keep_warm(5, bank(6))
                pe_block(pe, S_COUT, W, h, parts=one, ready=lambda k: (clo_ready, k + 1))

            @block.scalar
            def _(act):
                for k in range(KT):
                    nc.scalar.activation(h[0][:, k], conv[:, k, :], ACT.Copy).then_inc(chi_ready, 1)
                act_hi(act, S_COUT + 1, W)

            @block.vector
            def _(dve):
                dve_hi(dve, S_COUT, W)
                for k in range(KT):
                    dve.wait_ge(chi_ready, k + 1)
                    nc.vector.tensor_tensor(h[1][:, k], conv[:, k, :], h[0][:, k].bitcast(F32), SUB)\
                        .then_inc(clo_ready, 1)

            @block.gpsimd
            def _(pool):
                for j in range(2):
                    pool_lo(pool, S_COUT + j, W)
        dense(S_COUT, 4, lambda t: yb[:, t, :], W, h, SquareSum(st))
    norms(1, "g11", 16, "g12", 1, 24, S_MLP1)
    mlp(S_MLP1, True)
    norms(1, "g13", 40)
    tail.close()
    top.close()


def kernel(**inputs):
    import numpy as np
    import concourse.bacc as bacc
    from concourse import mybir
    from concourse.bass_utils import run_bass_kernel_spmd

    v = {k: np.asarray(a) for k, a in inputs.items()}
    T, C, D = v["x"].shape[1], v["ctx"].shape[1], v["x"].shape[2]
    KT = D // 128

    def columns(a):
        return np.ascontiguousarray(a.reshape(-1, 128).T)

    def blocks(w):
        k, m = w.shape
        if m % 256:
            w = np.concatenate([w, np.zeros((k, 256 - m % 256), w.dtype)], axis=1)
            m = w.shape[1]
        return w.reshape(k // 128, 128, m // 256, 256).transpose(2, 1, 0, 3).reshape(m // 256, 128, k * 2)

    def mlp(i):
        w1 = blocks(v["mlp_w1"][i])
        out = []
        for q in range(4):
            out += [w1[4 * q:4 * q + 4], blocks(v["mlp_w2"][i][q * D:(q + 1) * D])]
        return out

    stream = [blocks(v["mod_w"][0][:, :2 * D]), blocks(v["ab_w_in"][0]), blocks(v["mod_w"][0][:, 2 * D:]),
              blocks(v["mod_w"][1]), blocks(v["ab_w_out"][0])] + mlp(0) + \
             [blocks(v["conv_w_in"][0]), blocks(v["conv_w_out"][0])] + mlp(1)
    f = np.float32
    g = v["norm_g"]
    parts = dict(modb0=columns(v["mod_b"][0]), modb1=columns(v["mod_b"][1]), mu=columns(v["rwkv_mu"][0]),
                 w0=columns(v["rwkv_w0"][0]), a0=columns(v["rwkv_a0"][0]), kk=columns(v["rwkv_kk"][0]),
                 ka=columns(v["rwkv_ka"][0]), rk=columns(v["rwkv_rk"][0]), lnw=columns(v["rwkv_ln_w"][0]),
                 lnb=columns(v["rwkv_ln_b"][0]), cw=columns(v["conv_w"][0]),
                 sink=np.broadcast_to(v["att_sink"][0][None, :], (128, 8)),
                 c=np.stack([v["c"][0], v["c_ctx"]], -1).reshape(KT, 128, 2).transpose(1, 0, 2).reshape(128, 2 * KT))
    for i in range(2):
        for j in range(4):
            parts[f"g{i}{j}"] = columns(g[i, j])
    at, n = _columns(_PRM)
    prm = np.concatenate([parts[name].reshape(128, -1) for name, _ in _PRM], axis=1)
    assert prm.shape == (128, n)
    lw = np.stack([v["rwkv_w2"][0], v["rwkv_a2"][0]], 0).reshape(2, 128, 4, 128).transpose(2, 1, 0, 3)
    xT = v["x"][0].T.reshape(KT, 128, T).transpose(1, 0, 2)
    cT = v["ctx"][0].T.reshape(KT, 128, C).transpose(1, 0, 2)
    arrays = {"w": np.concatenate(stream), "prm": prm, "cst": _constants(np, T, C, _CST),
              "csa": _constants(np, T, C, _CSA),
              "x": xT, "ctx": cT,
              "lw": lw, "g2": v["rwkv_g2"][0]}
    arrays = {k: np.ascontiguousarray(a) for k, a in arrays.items()}
    nc = bacc.Bacc("TRN2", target_bir_lowering=False, num_devices=1)
    A = {k: nc.dram_tensor(k + "_in", a.shape, mybir.dt.from_np(a.dtype), kind="ExternalInput").ap()
         for k, a in arrays.items()}
    A["out"] = nc.dram_tensor("out_T", (128, KT, T), mybir.dt.float32, kind="ExternalOutput").ap()
    build(nc, A)
    r = run_bass_kernel_spmd(nc, [{k + "_in": a for k, a in arrays.items()}], core_ids=[0])
    o = r.results[0]["out_T"]
    return np.ascontiguousarray(o.transpose(1, 0, 2).reshape(D, T).T)[None]
```
